# Optimizing a Trainium2 kernel written in Bass

```python
import jax, jax.numpy as jnp
from jax import lax
import numpy as np

D_MODEL = 1024
BATCH = 1
SEQ = 1024
DEPTH = 2

N_MIXERS = 2
N_LAYERS_A = (DEPTH + N_MIXERS - 1) // N_MIXERS
N_LAYERS_B = DEPTH // N_MIXERS
CHUNK = 128
SGU_HEADS = 8
SGU_WIDTH = 2 * D_MODEL
SGU_HEAD_DIM = SGU_WIDTH // SGU_HEADS
POOL_WINDOWS = (2, 4, 8, 16)
POOL_GROUPS = len(POOL_WINDOWS)
POOL_WIDTH = D_MODEL
POOL_GROUP_DIM = POOL_WIDTH // POOL_GROUPS
N_EXPERT_GROUPS = 4
EXPERTS_PER_GROUP = 8
N_EXPERTS = N_EXPERT_GROUPS * EXPERTS_PER_GROUP
TOP_K = 2
D_EXPERT = D_MODEL // 2
EXPERT_BLOCK = 128
EPS = 1e-6

kernel_name = "hybrid_sgu_pool_hmoe_encoder"

def rmsnorm(x, g):
    xf = x.astype(jnp.float32)
    y = xf * lax.rsqrt(jnp.mean(xf * xf, axis=-1, keepdims=True) + EPS)
    return (y * g.astype(jnp.float32)).astype(x.dtype)

def sgu_mixer(h, w_in, b_in, g_v, w_s, b_s, w_out):
    bsz, seq, _ = h.shape
    z = jax.nn.gelu(h @ w_in + b_in, approximate=False)
    u, v = jnp.split(z, 2, axis=-1)
    v = rmsnorm(v, g_v)
    v = v.reshape(bsz, seq // CHUNK, CHUNK, SGU_HEADS, SGU_HEAD_DIM)
    sv = jnp.einsum('hts,bcshd->bcthd', w_s, v) + b_s.T[:, :, None]
    y = u * sv.reshape(bsz, seq, SGU_WIDTH)
    return y @ w_out

def pool_mixer(h, w_in, w_group, scale, w_out):
    bsz, seq, _ = h.shape
    v = h @ w_in
    csum = jnp.cumsum(jnp.pad(v.astype(jnp.float32), ((0, 0), (1, 0), (0, 0))), axis=1)
    pos = jnp.arange(seq)
    outs = []
    for g, w in enumerate(POOL_WINDOWS):
        sl = slice(g * POOL_GROUP_DIM, (g + 1) * POOL_GROUP_DIM)
        lo = jnp.clip(pos - w // 2, 0, seq)
        hi = jnp.clip(pos - w // 2 + w, 0, seq)
        cg = csum[:, :, sl]
        cnt = (hi - lo).astype(jnp.float32)[None, :, None]
        mean = (jnp.take(cg, hi, axis=1) - jnp.take(cg, lo, axis=1)) / cnt
        d = mean.astype(v.dtype) - v[..., sl]
        outs.append(d @ w_group[g])
    y = jnp.concatenate(outs, axis=-1) * scale
    return y @ w_out

def hierarchical_moe(h, rg_w, rg_b, re_w, re_b, w_gate, w_up, w_down):
    bsz, seq, d = h.shape
    n_tok = bsz * seq
    xt = h.reshape(n_tok, d)
    xf = xt.astype(jnp.float32)
    g_logits = xf @ rg_w.astype(jnp.float32) + rg_b.astype(jnp.float32)
    g_prob = jax.nn.softmax(g_logits, axis=-1)
    g_w, g_idx = lax.top_k(g_prob, 1)
    e_logits = (xf @ re_w.astype(jnp.float32) + re_b.astype(jnp.float32)).reshape(
        n_tok, N_EXPERT_GROUPS, EXPERTS_PER_GROUP)
    e_sel = jnp.take_along_axis(e_logits, g_idx[:, :, None], axis=1)[:, 0]
    e_prob = jax.nn.softmax(e_sel, axis=-1)
    e_w, e_idx = lax.top_k(e_prob, TOP_K)
    e_w = e_w / jnp.sum(e_w, axis=-1, keepdims=True)
    gate = g_w * e_w
    expert_id = g_idx * EXPERTS_PER_GROUP + e_idx

    n_assign = n_tok * TOP_K
    flat_e = expert_id.reshape(-1)
    order = jnp.argsort(flat_e)
    sorted_e = flat_e[order]
    tok = order // TOP_K
    counts = jnp.bincount(flat_e, length=N_EXPERTS)
    starts = jnp.cumsum(counts) - counts
    padded = ((counts + EXPERT_BLOCK - 1) // EXPERT_BLOCK) * EXPERT_BLOCK
    pend = jnp.cumsum(padded)
    pstart = pend - padded
    dest = pstart[sorted_e] + (jnp.arange(n_assign) - starts[sorted_e])
    n_blocks = -(-n_assign // EXPERT_BLOCK) + N_EXPERTS
    buf = jnp.zeros((n_blocks * EXPERT_BLOCK, d), xt.dtype).at[dest].set(xt[tok])
    block_expert = jnp.minimum(
        jnp.searchsorted(pend, jnp.arange(n_blocks) * EXPERT_BLOCK, side='right'), N_EXPERTS - 1)

    def expert_block(args):
        xb, e = args
        hid = jax.nn.silu(xb @ w_gate[e]) * (xb @ w_up[e])
        return hid @ w_down[e]

    yb = lax.map(expert_block, (buf.reshape(n_blocks, EXPERT_BLOCK, d), block_expert))
    y_sorted = yb.reshape(n_blocks * EXPERT_BLOCK, d)[dest]
    w_sorted = gate.reshape(-1)[order].astype(y_sorted.dtype)
    out = jax.ops.segment_sum(y_sorted * w_sorted[:, None], tok, num_segments=n_tok)
    return out.reshape(bsz, seq, d)

def setup_inputs(seed: int = 0) -> dict:
    key = jax.random.key(seed)
    ks = jax.random.split(key, 21)

    def nrm(k, shape, scale):
        return jax.random.normal(k, shape, jnp.float32) * scale

    D, F, E = D_MODEL, D_EXPERT, N_EXPERTS
    return {
        "x": nrm(ks[0], (BATCH, SEQ, D), 1.0),
        "norm_mix_g": 1.0 + nrm(ks[1], (DEPTH, D), 0.02),
        "norm_ffn_g": 1.0 + nrm(ks[2], (DEPTH, D), 0.02),
        "a_w_in": nrm(ks[3], (N_LAYERS_A, D, 2 * SGU_WIDTH), D ** -0.5),
        "a_b_in": nrm(ks[4], (N_LAYERS_A, 2 * SGU_WIDTH), 0.02),
        "a_norm_v": 1.0 + nrm(ks[5], (N_LAYERS_A, SGU_WIDTH), 0.02),
        "a_w_spatial": nrm(ks[6], (N_LAYERS_A, SGU_HEADS, CHUNK, CHUNK), CHUNK ** -0.5),
        "a_b_spatial": 1.0 + nrm(ks[7], (N_LAYERS_A, SGU_HEADS, CHUNK), 0.02),
        "a_w_out": nrm(ks[8], (N_LAYERS_A, SGU_WIDTH, D), SGU_WIDTH ** -0.5),
        "b_w_in": nrm(ks[9], (N_LAYERS_B, D, POOL_WIDTH), D ** -0.5),
        "b_w_group": nrm(ks[10], (N_LAYERS_B, POOL_GROUPS, POOL_GROUP_DIM, POOL_GROUP_DIM),
                         POOL_GROUP_DIM ** -0.5),
        "b_scale": 1.0 + nrm(ks[11], (N_LAYERS_B, POOL_WIDTH), 0.02),
        "b_w_out": nrm(ks[12], (N_LAYERS_B, POOL_WIDTH, D), POOL_WIDTH ** -0.5),
        "router_group_w": nrm(ks[13], (DEPTH, D, N_EXPERT_GROUPS), D ** -0.5),
        "router_group_b": nrm(ks[14], (DEPTH, N_EXPERT_GROUPS), 0.01),
        "router_expert_w": nrm(ks[15], (DEPTH, D, E), D ** -0.5),
        "router_expert_b": nrm(ks[16], (DEPTH, E), 0.01),
        "w_gate": nrm(ks[17], (DEPTH, E, D, F), D ** -0.5),
        "w_up": nrm(ks[18], (DEPTH, E, D, F), D ** -0.5),
        "w_down": nrm(ks[19], (DEPTH, E, F, D), F ** -0.5),
        "final_norm_g": 1.0 + nrm(ks[20], (D,), 0.02),
    }

def reference(x, norm_mix_g, norm_ffn_g, a_w_in, a_b_in, a_norm_v, a_w_spatial, a_b_spatial,
              a_w_out, b_w_in, b_w_group, b_scale, b_w_out, router_group_w, router_group_b,
              router_expert_w, router_expert_b, w_gate, w_up, w_down, final_norm_g):
    for i in range(DEPTH):
        h = rmsnorm(x, norm_mix_g[i])
        j = i // N_MIXERS
        if i % N_MIXERS == 0:
            x = x + sgu_mixer(h, a_w_in[j], a_b_in[j], a_norm_v[j], a_w_spatial[j],
                              a_b_spatial[j], a_w_out[j])
        else:
            x = x + pool_mixer(h, b_w_in[j], b_w_group[j], b_scale[j], b_w_out[j])
        h = rmsnorm(x, norm_ffn_g[i])
        x = x + hierarchical_moe(h, router_group_w[i], router_group_b[i], router_expert_w[i],
                                 router_expert_b[i], w_gate[i], w_up[i], w_down[i])
    return rmsnorm(x, final_norm_g)


_drawn_inputs = setup_inputs


def setup_inputs(seed=0):
    import zlib

    import numpy as np

    out = dict(_drawn_inputs(seed))
    spreads = {}
    factors = {'b_scale': 23.771,
     'router_group_b': 14.24,
     'router_expert_b': 12.479,
     'final_norm_g': 25.684,
     'a_norm_v': 8.815,
     'a_b_spatial': 9.816,
     'norm_ffn_g': 4.147}
    for name, (base, spread) in spreads.items():
        noise = np.random.default_rng([zlib.crc32(name.encode()), seed]).standard_normal(out[name].shape)
        drawn = base * np.exp(spread * noise) if base else spread * noise
        out[name] = __import__('jax').numpy.asarray(drawn.astype(out[name].dtype))
    for name, factor in factors.items():
        out[name] = (out[name] * factor).astype(out[name].dtype)
    return out
```

```python
from collections import namedtuple
from contextlib import ExitStack

import concourse.bass as bass
from concourse import mybir

F32, F32R, BF16, I32, U32 = (mybir.dt.float32, mybir.dt.float32r, mybir.dt.bfloat16,
                             mybir.dt.int32, mybir.dt.uint32)
ALU, ACT, AX = mybir.AluOpType, mybir.ActivationFunctionType, mybir.AxisListType

P = 128
D = 1024
SEQ = 1024
TT = SEQ // P
HALVES = 2
HT = TT // HALVES
HTOK = HT * P
KC = D // P
SGU = 2 * D
HEADS = 8
F = D // 2
E = 32
GROUPS = 4
EPG = E // GROUPS
LAYERS = 2
BANKS = 8
RING = 4
UNIT = 1024
GU, DN = 8, 4
ROUND = GU + DN
BLK = P
LISTED = SEQ
BPE = LISTED // BLK
EXTRA = 2 * SEQ // BLK
ITEMS_MAX = E + EXTRA - 1
TABLE = 64
EPS = 1e-6
WINDOWS = (2, 4, 8, 16)
PAD = WINDOWS[-1] // 2
BIG = 1e30

C_ID, C_TRI, C_E, C_GRP, C_BASE = 0, P, 2 * P, 2 * P + E, 2 * P + 2 * E
C_ASC = C_BASE + E
C_DESC, C_THR = C_ASC + 16, C_ASC + 32
C_J = C_THR + BPE - 1
C_E8 = C_J + 16
C_ALL = C_E8 + E


def encoder_trunk(nc, A, out):
    ctx = ExitStack()
    with ctx:
        def sb(name, shape, dt):
            return ctx.enter_context(nc.sbuf_tensor(name, shape, dt))

        def sems(phase, names, arrays):
            def one(n):
                return ctx.enter_context(nc.semaphore(f"{phase}_{n}"))
            made = {n: one(n) for n in names} | {n: [one(f"{n}{i}") for i in range(k)] for n, k in arrays.items()}
            return namedtuple("Sems", made)(**made)

        x_res = sb("x_res", [P, TT, D], F32)
        raw = sb("raw", [P, RING, UNIT], F32)
        w_hi = sb("w_hi", [P, RING, UNIT], F32R)
        w_lo = sb("w_lo", [P, RING, UNIT], F32R)
        a_hi = sb("a_hi", [P, KC, HTOK], F32R)
        a_lo = sb("a_lo", [P, KC, HTOK], F32R)
        y_hi = sb("y_hi", [P, 2, HTOK], F32R)
        y_lo = sb("y_lo", [P, 2, HTOK], F32R)
        bu = sb("bu", [P, 8 * 1024], F32)
        bv = sb("bv", [P, 8 * 1024], F32)
        gain = sb("gain", [P, D], F32)
        spatial = sb("spatial", [P, HEADS * P], F32)
        sbias = sb("sbias", [P, HEADS * P], F32)
        vbias = sb("vbias", [P, SGU], F32)
        cf = sb("cf", [P, C_ALL], F32)
        tri = sb("tri", [P, P], BF16)
        ones = sb("ones", [P, P], BF16)
        chosen = sb("chosen", [P, TT, E], BF16)
        payload = sb("payload", [P, TT, 2, 4], I32)
        place = sb("place", [P, TT, 2], I32)
        table = sb("table", [1, 2, TABLE], I32)
        metas = sb("metas", [P, 8], I32)
        cols = sb("cols", [P, 72], F32)
        bank = [ctx.enter_context(nc.psum_tensor(f"bank{b}", [P, 512], F32)) for b in range(BANKS)]

        def dram(name, shape, dt):
            return nc.dram_tensor(name, shape, dt, kind="Internal").ap()
        normed = [dram(f"normed{n}", (SEQ, D), F32) for n in range(LAYERS)]
        y_rows = [dram(f"y_rows{n}", (2 * SEQ, D), F32) for n in range(LAYERS)]
        lists = [dram(f"lists{n}", (E * LISTED, 4), I32) for n in range(LAYERS)]

        meta_g, meta_s = metas[:, 0:4], metas[:, 4:8]
        ss, var, std, rstd = [cols[:, 40 + 4 * n:44 + 4 * n] for n in range(4)]
        v_ss = cols[:, 56:72].rearrange("p (t c) -> p t c", c=4)
        ident = cf[:, C_ID:C_ID + P]
        hn = [bv[:, h * HT * D:(h + 1) * HT * D].rearrange("p (t d) -> p t d", d=D) for h in range(2)]
        u_all = bu[:, :].rearrange("p (c t) -> p c t", t=HTOK)
        v_all = bv[:, :].rearrange("p (t d) -> p t d", d=SGU)
        w_s = spatial[:, :].rearrange("p (h t) -> p h t", h=HEADS)
        b_s = sbias[:, :].rearrange("p (h t) -> p h t", h=HEADS)
        pooled = bu[:, :].rearrange("p (c t) -> p c t", t=SEQ)
        xg = bv[:, 4096:5120]
        y_sb = bv[:, 5120:6144].rearrange("p (n f) -> p n f", n=2)
        silu_g = bv[:, 6144:6144 + F]
        hid = bv[:, 6144 + F:6144 + 2 * F]
        comb = [bv[:, n * 2048:(n + 1) * 2048].rearrange("p (k d) -> p k d", k=2) for n in range(2)]
        x_hi = a_hi[:, 0:2, :].rearrange("p a (k t) -> p (a k) t", t=P)
        x_lo = a_lo[:, 0:2, :].rearrange("p a (k t) -> p (a k) t", t=P)
        h_hi = a_hi[:, 2, :].rearrange("p (k t) -> p k t", t=P)
        h_lo = a_lo[:, 2, :].rearrange("p (k t) -> p k t", t=P)
        moe_raw = [raw[:, n, :] for n in range(RING)] + \
                  [bu[:, n * UNIT:(n + 1) * UNIT] for n in range(ROUND - RING)]

        rw = spatial[:, 0:KC * 36].rearrange("p (k c) -> p k c", c=36)
        rb = spatial[:, 300:336].rearrange("p (o c) -> p o c", o=1)
        lg = spatial[:, 336:336 + TT * 36].rearrange("p (t c) -> p t c", c=36)
        rw_hi = y_hi[:, 0, 0:KC * 36].rearrange("p (k c) -> p k c", c=36)
        rw_lo = y_lo[:, 0, 0:KC * 36].rearrange("p (k c) -> p k c", c=36)

        def scratch(at, width, dt=F32):
            v = vbias[:, at:at + TT * width]
            return (v if dt is F32 else v.bitcast(dt)).rearrange("p (t c) -> p t c", c=width)
        r_gpad, r_gmax, r_gidx = scratch(0, 8), scratch(64, 8), scratch(128, 8, U32)
        r_gexp, r_gsum, r_gw, r_grp = scratch(192, GROUPS), scratch(224, 1), scratch(232, 1), scratch(240, 1)
        r_mask, r_el = scratch(256, E), scratch(512, E)
        r_emax, r_eidx, r_e = scratch(768, 8), scratch(832, 8, U32), scratch(896, 2)
        r_ediff, r_eexp, r_den, r_rden = scratch(912, 1), scratch(920, 1), scratch(928, 1), scratch(936, 1)
        r_w, r_place = scratch(944, 2), scratch(960, 2)
        r_oh, r_pos = [scratch(1024, E), scratch(1280, E)], scratch(1536, E)

        def const3(at, width, n):
            return cf[:, at:at + width].rearrange("p (o e) -> p o e", o=1).to_broadcast([P, n, width])
        padded = [bv[:, n * 1040:(n + 1) * 1040] for n in range(2)]
        sums = [bv[:, 2080:3120], vbias[:, 0:1040]]
        y_f32 = bv[:, 4096:8192].rearrange("p (c t) -> p c t", t=HTOK)

        def f32(ap):
            return ap.bitcast(F32)

        g = sems("g", ["consts", "cast", "init", "lists_ready", "gain_ready", "x_loaded", "small",
                       "sq", "var", "std", "rstd", "waited", "hn", "t_full", "t_hi", "t_lo", "out_stored"], {})
        RINGS = ["hi", "lo", "used"]
        s = sems("sgu", RINGS + ["full", "ev_act", "ev_dve", "v_sq", "v_gelu", "v_sum", "v_var", "v_std",
                                 "v_rstd", "v_scaled", "gated", "y_ready", "y_hi", "y_lo"],
                 {"raw": RING})
        q = sems("pool", RINGS + ["full", "ev_act", "ev_dve", "zeroed", "padded", "chain", "d_ready", "d_hi",
                                  "d_lo", "g_out", "y_hi", "y_lo"],
                 {"raw": RING})
        MOE = ["hi", "lo", "used", "rw_hi", "rw_lo", "logits", "logits_read", "chain",
               "exp_g", "exp_e", "g_shifted", "e_shifted", "chosen", "ranked", "placed", "listed", "table",
               "meta_g", "gathered", "x_full", "x_hi", "x_lo", "silu", "hid",
               "h_full", "h_hi", "h_lo", "y_out", "meta_s", "scattered",
               "added", "small", "summed"]
        m = [sems(f"moe{n}", MOE, {"raw": ROUND, "stored": HALVES, "comb": 2}) for n in range(LAYERS)]

        SU = 3 * 2 * KC
        PV, PG, PO = KC, 2, KC

        BF = BANKS - 1
        S_FULL = 2 * BF + 2 * BF + SGU // P + BF
        S_EVD = 2 * BANKS + SGU // P + BANKS
        S_EVA = 2 * BANKS

        block = ctx.enter_context(nc.Block())

        @block.sync
        def _(sp):
            sp.dma_start(cf[:, :], A["c_float"]).then_inc(g.consts, 16)
            xv = A["x"].rearrange("o (t p) d -> p (o t) d", p=P)
            for h in range(HALVES):
                sp.dma_start(x_res[:, h * HT:(h + 1) * HT, :], xv[:, h * HT:(h + 1) * HT, :]) \
                    .then_inc(g.x_loaded, 16)
                sp.wait_ge(g.x_loaded, 16 * (h + 1))
                if h == 0:
                    for kc in range(RING):
                        sp.dma_start(raw[:, kc, :], A["a_w_in"][0, kc * P:(kc + 1) * P, 0:UNIT]) \
                            .then_inc(s.raw[kc], 16)
            sp.sem_inc(s.lo, RING)

            def sgu_in(hf, c, first):
                for kc in range(first, KC):
                    sp.wait_ge(s.lo, hf * SU + c * KC + kc + 1)
                    sp.dma_start(raw[:, kc % RING, :],
                                 A["a_w_in"][0, kc * P:(kc + 1) * P, bass.ds(c * UNIT, UNIT)]) \
                        .then_inc(s.raw[kc % RING], 16)

            def sgu_half(hf, first):
                if first:
                    sgu_in(hf, 0, RING)
                    with sp.Fori(1, 4) as c:
                        sgu_in(hf, c, 0)
                else:
                    with sp.Fori(0, 4) as c:
                        sgu_in(hf, c, 0)
                with sp.Fori(0, 2) as o:
                    for kc in range(KC):
                        sp.wait_ge(s.lo, hf * SU + 4 * KC + o * KC + kc + 1)
                        sp.dma_start(raw[:, kc % RING, :], A["a_w_out"][0, bass.ds((o * KC + kc) * P, P), :]) \
                            .then_inc(s.raw[kc % RING], 16)
            sgu_half(0, True)
            sgu_half(1, False)

            def moe(L, before_lo, before_y):
                M = m[L]
                gate = A["w_gate"][L].rearrange("e (p k) f -> p e k f", k=KC)
                up = A["w_up"][L].rearrange("e (p k) f -> p e k f", k=KC)
                down = A["w_down"][L].rearrange("e (p k) d -> p e k d", k=DN)

                def load_gu(e, j):
                    w = gate if j < DN else up
                    k = 2 * (j % DN)
                    sp.dma_start(moe_raw[j].rearrange("p (e k f) -> p e k f", e=1, k=2),
                                 w[:, bass.ds(e, 1), k:k + 2, :]).then_inc(M.raw[j], 16)

                def load_dn(e, j):
                    sp.dma_start(moe_raw[GU + j].rearrange("p (e k d) -> p e k d", e=1, k=1),
                                 down[:, bass.ds(e, 1), j:j + 1, :]).then_inc(M.raw[GU + j], 16)

                before_lo(sp)
                for j in range(RING):
                    load_gu(0, j)
                before_y(sp)
                for j in range(RING, GU):
                    load_gu(0, j)
                for j in range(DN):
                    load_dn(0, j)
                for h in range(HALVES):
                    sp.wait_ge(g.hn, 4 * (4 * L + 2 + h + 1))
                    sp.dma_start(normed[L].rearrange("(t p) d -> p t d", p=P)[:, h * HT:(h + 1) * HT, :],
                                 hn[h]).then_inc(M.stored[h], 16)
                for j in range(GU):
                    sp.wait_ge(M.lo, j + 1)
                    load_gu(1, j)
                sp.wait_ge(M.table, 1)
                n = sp.value_load(table[0:1, 0, TABLE - 1:TABLE], min_val=E - 2, max_val=ITEMS_MAX - 2) + 2
                with sp.Fori(2, n) as i:
                    e_up = sp.value_load(table[0:1, 0, bass.ds(i, 1)], min_val=0, max_val=E - 1)
                    e_dn = sp.value_load(table[0:1, 0, bass.ds(i - 1, 1)], min_val=0, max_val=E - 1)
                    for j in range(GU):
                        sp.wait_ge(M.lo, ROUND * (i - 1) + j + 1)
                        load_gu(e_up, j)
                    for j in range(DN):
                        sp.wait_ge(M.lo, ROUND * (i - 1) + GU + j + 1)
                        load_dn(e_dn, j)
                e_dn = sp.value_load(table[0:1, 0, bass.ds(n - 1, 1)], min_val=0, max_val=E - 1)
                for j in range(DN):
                    sp.wait_ge(M.lo, ROUND * (n - 1) + GU + j + 1)
                    load_dn(e_dn, j)
                sp.wait_ge(M.scattered, 16 * n)
                yv = y_rows[L].rearrange("(t p k) d -> p t k d", p=P, k=2)
                for t in range(TT):
                    if t >= 2:
                        sp.wait_ge(M.added, t - 1)
                    sp.dma_start(comb[t % 2], yv[:, t, :, :]).then_inc(M.comb[t % 2], 16)
                return n

            moe(0, lambda e: e.wait_ge(s.lo, RING + 2 * SU), lambda e: e.wait_ge(s.y_lo, 2 * 2 * KC))

            sp.sem_inc(q.lo, RING)
            sp.wait_ge(m[0].added, TT)
            wg = A["b_w_group"][0].rearrange("g (k p) f -> p g k f", k=2)
            with sp.Fori(0, HALVES) as hf:
                for kc in range(KC):
                    sp.wait_ge(q.lo, hf * PV + kc + 1)
                    sp.dma_start(raw[:, kc % RING, :], A["b_w_in"][0, kc * P:(kc + 1) * P, :]) \
                        .then_inc(q.raw[kc % RING], 16)

            def pool_out(hf, base):
                for r in range(PG + PO):
                    sp.wait_ge(q.lo, base + r + 1)
                    slot = (base + r) % RING
                    if r < PG:
                        sp.dma_start(raw[:, slot, :].rearrange("p (g k f) -> p g k f", g=2, k=2),
                                     wg[:, 2 * r:2 * r + 2, :, :]).then_inc(q.raw[slot], 16)
                    else:
                        kc = r - PG
                        sp.dma_start(raw[:, slot, :], A["b_w_out"][0, kc * P:(kc + 1) * P, :]) \
                            .then_inc(q.raw[slot], 16)
            for hf in range(HALVES):
                pool_out(hf, HALVES * PV + hf * (PG + PO))
            total = HALVES * (PV + PG + PO)
            moe(1, lambda e: e.wait_ge(q.lo, RING + total), lambda e: e.wait_ge(q.y_lo, HALVES * KC))

            ov = out.rearrange("o (t p) d -> p (o t) d", p=P)
            for h in range(HALVES):
                for t in range(HT):
                    sp.wait_ge(g.hn, 4 * (8 + h) + t + 1)
                    sp.dma_start(ov[:, h * HT + t, :], hn[h][:, t, :]).then_inc(g.out_stored, 16)
            sp.wait_ge(g.out_stored, 16 * TT)

        @block.gpsimd
        def _(pool):
            def waited():
                pool.sem_inc(g.waited, 1)

            def load_gain(k, src):
                if k:
                    pool.wait_ge(g.hn, 8 * k)
                pool.dma_start(gain[:, :], src.partition_broadcast(P)).then_inc(g.gain_ready, 16)

            load_gain(0, A["norm_mix_g"][0])
            pool.dma_start(payload[:, :, :, :].rearrange("p t k w -> p (t k w)"), A["c_payload"]).then_inc(g.small, 16)
            pool.dma_start(table[:, :, :], A["c_table"]).then_inc(g.small, 16)
            pool.dma_start(cols[:, 0:16], A["u_bias"]).then_inc(g.small, 16)
            pool.dma_start(cols[:, 16:32], A["v_gain"]).then_inc(g.small, 16)
            pool.dma_start(cols[:, 32:40], A["pool_scale"]).then_inc(g.small, 16)
            pool.dma_start(spatial[:, :], A["w_s"]).then_inc(g.small, 16)
            pool.dma_start(sbias[:, :], A["a_b_spatial"][0].rearrange("h t -> (h t)").partition_broadcast(P)) \
                .then_inc(g.small, 16)
            pool.dma_start(vbias[:, :], A["a_b_in"][0, SGU:2 * SGU].partition_broadcast(P)).then_inc(g.small, 16)
            pool.memset(ones[:, :], 1.0).then_inc(g.init, 1)
            pool.memset(bu[:, 0:1024], 1.0).then_inc(g.init, 1)
            pool.wait_ge(g.init, 2)
            for L in range(LAYERS):
                pool.dma_start(lists[L].rearrange("(p r) w -> p (r w)", p=P), bu[:, 0:1024].bitcast(I32)) \
                    .then_inc(g.lists_ready, 16)
            load_gain(1, A["norm_ffn_g"][0])

            def moe(L):
                M = m[L]
                lst = lists[L].rearrange("(b p) w -> p b w", p=BLK)
                if L == 0:
                    pool.wait_ge(s.ev_dve, BANKS + HALVES * S_EVD)
                else:
                    pool.wait_ge(q.ev_dve, HALVES * BANKS)
                pool.dma_start(spatial[:, 0:KC * 36], A["router_w"][L]).then_inc(M.small, 16)
                pool.dma_start(spatial[:, 300:336], A["router_b"][L].partition_broadcast(P)).then_inc(M.small, 16)
                load_gain(2 * L + 2, A["norm_mix_g"][1] if L == 0 else A["final_norm_g"])
                pool.wait_ge(g.lists_ready, 16 * LAYERS)
                pool.wait_ge(M.placed, 1)
                for t in range(TT):
                    for k in range(2):
                        pool.indirect_dma_start(
                            out=lists[L][:, :],
                            out_offset=bass.IndirectOffsetOnAxis(ap=place[:, t, k:k + 1], axis=0),
                            in_=payload[:, t, k, :], in_offset=None).then_inc(M.listed, 16)
                pool.wait_ge(M.listed, 16 * 2 * TT)
                for h in range(HALVES):
                    pool.wait_ge(M.stored[h], 16)
                pool.wait_ge(M.table, 1)
                n = pool.value_load(table[0:1, 0, TABLE - 1:TABLE], min_val=E - 2, max_val=ITEMS_MAX - 2) + 2

                def block_of(i):
                    return pool.value_load(table[0:1, 1, bass.ds(i, 1)], min_val=0, max_val=E * BPE - 1)

                def gather(i):
                    b = block_of(i)
                    if not isinstance(i, int) or i > 0:
                        pool.wait_ge(M.x_full, i)
                        waited()
                    pool.dma_start(meta_g, lst[:, bass.ds(b, 1), :].rearrange("p b w -> p (b w)")).then_inc(M.meta_g, 16)
                    pool.wait_ge(M.meta_g, 16 * (i + 1))
                    waited()
                    pool.indirect_dma_start(
                        out=xg, out_offset=None, in_=normed[L][:, :],
                        in_offset=bass.IndirectOffsetOnAxis(ap=meta_g[:, 0:1], axis=0),
                        bounds_check=SEQ - 1, oob_is_err=False).then_inc(M.gathered, 16)

                def load_meta(i):
                    b = block_of(i)
                    pool.dma_start(meta_s, lst[:, bass.ds(b, 1), :].rearrange("p b w -> p (b w)")).then_inc(M.meta_s, 16)

                def scatter(i):
                    pool.wait_ge(M.y_out, 2 * (i + 1))
                    waited()
                    pool.indirect_dma_start(
                        out=y_rows[L][:, :],
                        out_offset=bass.IndirectOffsetOnAxis(ap=meta_s[:, 1:2], axis=0),
                        in_=y_sb.rearrange("p n f -> p (n f)"), in_offset=None,
                        bounds_check=2 * SEQ - 1, oob_is_err=False).then_inc(M.scattered, 16)
                    pool.wait_ge(M.scattered, 16 * (i + 1))
                    waited()

                gather(0)
                load_meta(0)
                gather(1)
                gather(2)
                with pool.Fori(2, n) as i:
                    gather(i + 1)
                    scatter(i - 2)
                    load_meta(i - 1)
                scatter(n - 2)
                load_meta(n - 1)
                scatter(n - 1)
                pool.wait_ge(M.gathered, 16 * (n + 1))
                waited()

            moe(0)
            load_gain(3, A["norm_ffn_g"][1])
            moe(1)

        @block.tensor
        def _(pe):
            def three(dst, left_hi, left_lo, right_hi, right_lo, first, last):
                pe.matmul(dst, left_hi, right_hi, start=first, stop=False)
                pe.matmul(dst, left_hi, right_lo, start=False, stop=False)
                return pe.matmul(dst, left_lo, right_hi, start=False, stop=last)

            def transposes(n, h):
                pe.wait_ge(g.hn, HT * (n + 1))
                for k in range(KC):
                    for t in range(HT):
                        last = pe.transpose(bank[k][:, t * P:(t + 1) * P], hn[h][:, t, k * P:(k + 1) * P], ident)
                    last.then_inc(g.t_full, 1)

            def channels_by_tokens(slot, kc, used, full, wait_bank):
                for c in range(BANKS):
                    if kc == 0:
                        wait_bank(c)
                    w = slice(c * P, (c + 1) * P)
                    last = three(bank[c][:, :], w_hi[:, slot, w], w_lo[:, slot, w],
                                 a_hi[:, kc, :], a_lo[:, kc, :], kc == 0, kc == KC - 1)
                    if kc == KC - 1 and c < BF:
                        last.then_inc(full, 1)
                last.then_inc(used, 1)

            def tokens_by_channels(slot, left_hi, left_lo, first, final, used, full, wait_bank):
                for t in range(HT):
                    for c in range(2):
                        if first:
                            wait_bank(2 * t + c)
                        col, row = slice(c * 512, (c + 1) * 512), slice(t * P, (t + 1) * P)
                        last = three(bank[2 * t + c][:, :], left_hi[:, row], left_lo[:, row],
                                     w_hi[:, slot, col], w_lo[:, slot, col], first, final)
                        if final and 2 * t + c < BF:
                            last.then_inc(full, 1)
                last.then_inc(used, 1)

            pe.wait_ge(g.consts, 16)

            pe.sem_inc(s.used, RING)
            with pe.Fori(0, HALVES) as hf:
                transposes(hf, 0)
                with pe.Fori(0, 2) as c4:
                    for kc in range(KC):
                        pe.wait_ge(s.lo, RING + hf * SU + c4 * KC + kc + 1)

                        def wait_bank(c):
                            pe.wait_ge(g.t_lo, hf * KC + c + 1)
                            pe.wait_ge(s.ev_act, hf * S_EVA + c4 * BANKS + c + 1)
                        channels_by_tokens(kc % RING, kc, s.used, s.full, wait_bank)
                with pe.Fori(0, 2) as c4:
                    for kc in range(KC):
                        pe.wait_ge(s.lo, RING + hf * SU + (2 + c4) * KC + kc + 1)

                        def wait_bank(b):
                            pe.wait_ge(s.ev_act, BANKS + hf * S_EVA + BANKS + b + 1)
                            pe.wait_ge(s.ev_dve, hf * S_EVD + c4 * BANKS + b + 1)
                        tokens_by_channels(kc % RING, a_hi[:, kc, :], a_lo[:, kc, :], kc == 0, kc == KC - 1,
                                           s.used, s.full, wait_bank)
                pe.wait_ge(s.v_scaled, HT * (hf + 1))
                for c in range(SGU // P):
                    pe.wait_ge(s.ev_dve, BANKS + hf * S_EVD + BANKS + c + 1)
                    for t in range(HT):
                        last = pe.matmul(bank[c % BANKS][:, t * P:(t + 1) * P], v_all[:, t, c * P:(c + 1) * P],
                                         w_s[:, c * P * HEADS // SGU, :], start=True, stop=True)
                    last.then_inc(s.full, 1)
                for kc in range(SGU // P):
                    pe.wait_ge(s.lo, RING + hf * SU + 4 * KC + kc + 1)
                    pe.wait_ge(s.y_lo, hf * (SGU // P) + kc + 1)

                    def wait_bank(b):
                        pe.wait_ge(s.ev_dve, BANKS + hf * S_EVD + BANKS + SGU // P + b + 1)
                    tokens_by_channels(kc % RING, y_hi[:, kc % 2, :], y_lo[:, kc % 2, :], kc == 0,
                                       kc == SGU // P - 1, s.used, s.full, wait_bank)

            def moe(L):
                M, n0 = m[L], 4 * L + 2
                for h in range(HALVES):
                    if h:
                        pe.wait_ge(M.logits_read, h)
                    transposes(n0 + h, h)
                    pe.wait_ge(M.rw_lo, 1)
                    pe.wait_ge(g.t_lo, KC * (n0 + h + 1))
                    for t in range(HT):
                        for k in range(KC):
                            row = slice(t * P, (t + 1) * P)
                            last = three(bank[0][:, t * 36:(t + 1) * 36], a_hi[:, k, row], a_lo[:, k, row],
                                         rw_hi[:, k, :], rw_lo[:, k, :], k == 0, k == KC - 1)
                    last.then_inc(M.logits, 1)
                pe.wait_ge(M.chosen, 1)
                pe.wait_ge(M.logits_read, 2)
                pe.wait_ge(g.cast, 1)
                pe.wait_ge(g.init, 1)
                for t in range(TT):
                    dst = bank[0][:, t * E:(t + 1) * E]
                    pe.matmul(dst, tri[:, :], chosen[:, t, :], start=True, stop=t == 0)
                    for b in range(t):
                        pe.matmul(dst, ones[:, :], chosen[:, b, :], start=False, stop=b == t - 1)
                for t in range(TT):
                    last = pe.matmul(bank[1][:, 0:E], ones[:, :], chosen[:, t, :], start=t == 0, stop=t == TT - 1)
                last.then_inc(M.ranked, 1)

                def x_transposes(i):
                    pe.wait_ge(M.gathered, 16 * (i + 1))
                    rows = xg.rearrange("t (p k) -> t k p", k=KC)
                    for k in range(KC):
                        last = pe.transpose(bank[4 + k // 4][:, k % 4 * P:(k % 4 + 1) * P], rows[:, k, :], ident)
                    last.then_inc(M.x_full, 1)

                def gate_up(i, lo_wait, gap):
                    pe.wait_ge(M.x_lo, 2 * (i + 1))
                    for j in range(GU):
                        lo_wait(j)
                        for k in range(2):
                            c = 2 * (j % DN) + k
                            col = slice(k * F, (k + 1) * F)
                            last = three(bank[j // DN][:, :], x_hi[:, c, :], x_lo[:, c, :],
                                         w_hi[:, j % RING, col], w_lo[:, j % RING, col], c == 0, c == KC - 1)
                        last.then_inc(M.used, 1 + (gap if j == GU - 1 else 0))

                def down(i, lo_wait):
                    pe.wait_ge(M.h_lo, i + 1)
                    for j in range(DN):
                        lo_wait(j)
                        for c in range(2):
                            col = slice(c * 512, (c + 1) * 512)
                            last = three(bank[2 + c][:, :], h_hi[:, j, :], h_lo[:, j, :],
                                         w_hi[:, j, col], w_lo[:, j, col], j == 0, j == DN - 1)
                        last.then_inc(M.used, 1)

                def h_transposes(i):
                    pe.wait_ge(M.hid, i + 1)
                    cols_of = hid.rearrange("t (p k) -> t k p", k=DN)
                    for k in range(DN):
                        last = pe.transpose(bank[6][:, k * P:(k + 1) * P], cols_of[:, k, :], ident)
                    last.then_inc(M.h_full, 1)

                def round_(i, before_down):
                    pe.wait_ge(M.hid, i)
                    gate_up(i, lambda j: pe.wait_ge(M.lo, ROUND * i + j + 1), 0)
                    x_transposes(i + 1)
                    before_down(i)
                    down(i - 1, lambda j: pe.wait_ge(M.lo, ROUND * i + GU + j + 1))
                    h_transposes(i)

                x_transposes(0)
                pe.wait_ge(M.table, 1)
                n = pe.value_load(table[0:1, 0, TABLE - 1:TABLE], min_val=E - 2, max_val=ITEMS_MAX - 2) + 2
                gate_up(0, lambda j: pe.wait_ge(M.lo, j + 1), DN)
                x_transposes(1)
                h_transposes(0)
                round_(1, lambda i: None)
                with pe.Fori(2, n) as i:
                    round_(i, lambda i: pe.wait_ge(M.y_out, 2 * (i - 1)))
                pe.wait_ge(M.y_out, 2 * (n - 1))
                down(n - 1, lambda j: pe.wait_ge(M.lo, ROUND * n + j + 1))

            moe(0)

            pe.sem_inc(q.used, RING)
            with pe.Fori(0, HALVES) as hf:
                pe.wait_ge(q.ev_act, BANKS + hf * BANKS)
                transposes(4 + hf, 0)
                for kc in range(KC):
                    pe.wait_ge(q.lo, RING + hf * PV + kc + 1)
                    channels_by_tokens(kc % RING, kc, q.used, q.full,
                                       lambda c: pe.wait_ge(g.t_lo, (4 + hf) * KC + c + 1))
            for hf in range(HALVES):
                base = HALVES * PV + hf * (PG + PO)
                for r in range(PG):
                    pe.wait_ge(q.lo, RING + base + r + 1)
                    for c in range(4):
                        b, grp, o = 4 * r + c, c // 2, c % 2
                        pe.wait_ge(q.d_lo, hf * KC + 4 * r + 2 * grp + 2)
                        if hf == 0:
                            pe.wait_ge(q.ev_act, BANKS + HALVES * BANKS)
                        else:
                            pe.wait_ge(q.ev_dve, (hf - 1) * BANKS + b + 1)
                        for k in range(2):
                            w = slice((2 * grp + k) * 256 + o * P, (2 * grp + k) * 256 + (o + 1) * P)
                            a = 4 * r + 2 * grp + k
                            last = three(bank[b][:, :], w_hi[:, (base + r) % RING, w], w_lo[:, (base + r) % RING, w],
                                         a_hi[:, a, :], a_lo[:, a, :], k == 0, k == 1)
                        if c < 3:
                            last.then_inc(q.full, 1)
                    last.then_inc(q.used, 1)
                for kc in range(KC):
                    u = base + PG + kc
                    pe.wait_ge(q.lo, RING + u + 1)
                    pe.wait_ge(q.y_lo, hf * KC + kc + 1)
                    tokens_by_channels(u % RING, y_hi[:, kc % 2, :], y_lo[:, kc % 2, :], kc == 0, kc == KC - 1,
                                       q.used, q.full, lambda b: pe.wait_ge(q.g_out, hf * BANKS + b + 1))
            moe(1)

        Q_V = HALVES * BF
        Q_HALF = 6 + BF

        @block.scalar
        def _(act):
            def copy(dst, src):
                return nc.scalar.activation(dst, src, ACT.Copy)

            def split(M, slot_raw, slot, src, loads, used):
                act.wait_ge(M.raw[slot_raw], 16 * loads)
                act.wait_ge(M.used, used)
                copy(w_hi[:, slot, :], src).then_inc(M.hi, 1)

            def norm(n, h, base):
                for t in range(HT):
                    nc.scalar.activation(hn[h][:, t, :], x_res[:, bass.ds(base + t, 1), :].rearrange("p o d -> p (o d)"),
                                         ACT.Square, accum_out=ss[:, t:t + 1]).then_inc(g.sq, 1)
                act.wait_ge(g.var, n + 1)
                nc.scalar.activation(std, var, ACT.Sqrt).then_inc(g.std, 1)

            def transposed(n):
                for k in range(KC):
                    act.wait_ge(g.t_full, n * KC + k + 1)
                    copy(a_hi[:, k, :], bank[k][:, :]).then_inc(g.t_hi, 1)

            act.sem_inc(s.ev_act, BANKS)
            act.wait_ge(g.small, 16 * 8)
            act.wait_ge(g.lists_ready, 16 * LAYERS)
            with act.Fori(0, HALVES) as hf:
                act.wait_ge(g.x_loaded, 16 * (hf + 1))
                norm(hf, 0, hf * HT)
                transposed(hf)

                def unit(u):
                    split(s, u % RING, u % RING, raw[:, u % RING, :],
                          hf * (SU // RING) + u // RING + 1, hf * SU + u + 1)

                def wait_full(first_full, b, last_unit):
                    if b < BF:
                        act.wait_ge(s.full, hf * S_FULL + first_full + b + 1)
                    else:
                        act.wait_ge(s.used, RING + hf * SU + last_unit)

                def v_tiles(c4):
                    for b in range(BANKS):
                        act.wait_ge(s.ev_dve, BANKS + hf * S_EVD + c4 * BANKS + b + 1)
                        col = slice(c4 * 1024 + b % 2 * 512, c4 * 1024 + b % 2 * 512 + 512)
                        nc.scalar.activation(v_all[:, b // 2, col], v_all[:, b // 2, col], ACT.Gelu).then_inc(s.v_gelu, 1)
                        act.wait_ge(s.v_gelu, hf * 2 * BANKS + c4 * BANKS + b + 1)
                        nc.scalar.activation(y_hi[:, 0, :], v_all[:, b // 2, col], ACT.Square,
                                             accum_out=v_ss[:, b // 2, 2 * c4 + b % 2:2 * c4 + b % 2 + 1]) \
                            .then_inc(s.v_sq, 1)
                for c4 in range(4):
                    for kc in range(3):
                        unit(c4 * KC + kc)
                    if c4 in (1, 2):
                        for b in range(BANKS):
                            wait_full((c4 - 1) * BF, b, c4 * KC)
                            c = (c4 - 1) * BANKS + b
                            nc.scalar.activation(u_all[:, c, :], bank[b][:, :], ACT.Gelu,
                                                 bias=cols[:, c:c + 1]).then_inc(s.ev_act, 1)
                    if c4 == 3:
                        v_tiles(0)
                    for kc in range(3, KC):
                        unit(c4 * KC + kc)
                for kc in range(3):
                    unit(4 * KC + kc)
                v_tiles(1)
                act.wait_ge(s.v_var, hf + 1)
                nc.scalar.activation(std, var, ACT.Sqrt).then_inc(s.v_std, 1)
                for kc in range(SGU // P):
                    act.wait_ge(s.y_ready, hf * (SGU // P) + kc + 1)
                    if kc >= 2:
                        act.wait_ge(s.used, RING + hf * SU + 4 * KC + kc - 1)
                    copy(y_hi[:, kc % 2, :], u_all[:, kc, :]).then_inc(s.y_hi, 1)
                    if kc + 3 < SGU // P:
                        unit(4 * KC + kc + 3)

            def moe(L, wait_x):
                M, n0 = m[L], 4 * L + 2
                wait_x()
                act.wait_ge(M.small, 32)
                copy(rw_hi, rw).then_inc(M.rw_hi, 1)
                for h in range(HALVES):
                    norm(n0 + h, h, h * HT)
                    transposed(n0 + h)
                act.wait_ge(M.g_shifted, 1)
                nc.scalar.activation(r_gexp, r_gexp, ACT.Exp).then_inc(M.exp_g, 1)
                act.wait_ge(M.e_shifted, 1)
                nc.scalar.activation(r_eexp, r_ediff, ACT.Exp).then_inc(M.exp_e, 1)

                def unit(c, loads, used, gap=0):
                    act.wait_ge(M.raw[c], 16 * loads)
                    if used is not None:
                        act.wait_ge(M.used, used)
                    copy(w_hi[:, c % RING, :], moe_raw[c]).then_inc(M.hi, 1 + gap)

                def x_split(i):
                    act.wait_ge(M.x_full, i + 1)
                    for b in range(2):
                        copy(x_hi[:, 4 * b:4 * b + 4, :].rearrange("p k t -> p (k t)"), bank[4 + b][:, :]) \
                            .then_inc(M.x_hi, 1)

                def silu(i):
                    act.wait_ge(M.used, ROUND * i + DN)
                    nc.scalar.activation(silu_g, bank[0][:, :], ACT.Silu).then_inc(M.silu, 1)

                def h_split(i):
                    act.wait_ge(M.h_full, i + 1)
                    copy(h_hi.rearrange("p k t -> p (k t)"), bank[6][:, :]).then_inc(M.h_hi, 1)

                def y_out(i, used):
                    act.wait_ge(M.used, used)
                    act.wait_ge(M.meta_s, 16 * (i + 1))
                    for c in range(2):
                        nc.scalar.activation(y_sb[:, c, :], bank[2 + c][:, :], ACT.Copy,
                                             scale=meta_s[:, 2:3].bitcast(F32)).then_inc(M.y_out, 1)

                def round_(i, with_y):
                    for c in range(4):
                        unit(c, i + 1, ROUND * i + c - 3)
                    if with_y:
                        y_out(i - 2, ROUND * i)
                    h_split(i - 1)
                    for c in range(4, GU):
                        unit(c, i + 1, ROUND * i + c - 3)
                    silu(i)
                    for c in range(GU, ROUND):
                        unit(c, i, ROUND * i + c - 3)
                    x_split(i + 1)

                x_split(0)
                for c in range(GU):
                    unit(c, 1, c - 3 if c >= RING else None, DN if c == GU - 1 else 0)
                silu(0)
                x_split(1)
                act.wait_ge(M.table, 1)
                n = act.value_load(table[0:1, 0, TABLE - 1:TABLE], min_val=E - 2, max_val=ITEMS_MAX - 2) + 2
                round_(1, False)
                with act.Fori(2, n) as i:
                    round_(i, True)
                for c in range(DN):
                    unit(GU + c, n, ROUND * (n - 1) + GU + c + 1)
                y_out(n - 2, ROUND * n)
                h_split(n - 1)
                y_out(n - 1, ROUND * n + DN)

            moe(0, lambda: act.wait_ge(s.ev_dve, BANKS + HALVES * S_EVD))

            act.sem_inc(q.ev_act, BANKS)
            act.wait_ge(m[0].added, TT)
            with act.Fori(0, HALVES) as hf:
                norm(4 + hf, 0, hf * HT)
                transposed(4 + hf)
                for u in range(PV):
                    split(q, u % RING, u % RING, raw[:, u % RING, :], hf * (PV // RING) + u // RING + 1, hf * PV + u + 1)
                for c in range(BANKS):
                    if c < BF:
                        act.wait_ge(q.full, hf * BF + c + 1)
                    else:
                        act.wait_ge(q.used, RING + hf * PV + PV)
                    copy(pooled[:, c, bass.ds(hf * HTOK, HTOK)], bank[c][:, :]).then_inc(q.ev_act, 1)

            def d_split(hf, c):
                act.wait_ge(q.d_ready, c + 1)
                copy(a_hi[:, c, :], pooled[:, c, hf * HTOK:(hf + 1) * HTOK]).then_inc(q.d_hi, 1)

            act.wait_ge(q.zeroed, 4)
            act.wait_ge(q.ev_act, BANKS + HALVES * BANKS)
            for c in range(KC):
                if c >= 2:
                    act.wait_ge(q.d_ready, c - 1)
                copy(padded[c % 2][:, PAD:PAD + SEQ], pooled[:, c, :]).then_inc(q.padded, 1)
                if c:
                    d_split(0, c - 1)
            d_split(0, KC - 1)
            for hf in range(HALVES):
                base = HALVES * PV + hf * (PG + PO)

                def unit(u):
                    split(q, u % RING, u % RING, raw[:, u % RING, :], u // RING + 1, u + 1)
                for r in range(3):
                    unit(base + r)
                for b in range(BANKS):
                    if b % 4 < 3:
                        act.wait_ge(q.full, Q_V + hf * Q_HALF + b // 4 * 3 + b % 4 + 1)
                    else:
                        act.wait_ge(q.used, RING + base + b // 4 + 1)
                    if hf:
                        act.wait_ge(q.y_lo, hf * KC)
                    nc.scalar.activation(y_f32[:, b, :], bank[b][:, :], ACT.Copy, scale=cols[:, 32 + b:33 + b]) \
                        .then_inc(q.g_out, 1)
                for kc in range(KC):
                    act.wait_ge(q.g_out, hf * BANKS + kc + 1)
                    if kc >= 2:
                        act.wait_ge(q.used, RING + base + PG + kc - 1)
                    elif hf:
                        act.wait_ge(q.used, RING + base)
                    copy(y_hi[:, kc % 2, :], y_f32[:, kc, :]).then_inc(q.y_hi, 1)
                    if kc + 3 < PG + PO:
                        if PG + kc + 1 < PG + PO:
                            unit(base + PG + kc + 1)
                    if hf == 0:
                        act.wait_ge(q.used, RING + base + PG)
                        d_split(1, kc)

            moe(1, lambda: act.wait_ge(q.ev_dve, HALVES * BANKS))

            act.wait_ge(m[1].added, TT)
            for h in range(HALVES):
                norm(8 + h, h, h * HT)

        @block.vector
        def _(dve):
            def lo_of(dst, src, hi):
                return nc.vector.tensor_tensor(dst, src, f32(hi), ALU.subtract)

            def norm(n, h, base):
                dve.wait_ge(g.sq, HT * (n + 1))
                nc.vector.tensor_scalar(var, ss, 1.0 / D, EPS, ALU.mult, ALU.add).then_inc(g.var, 1)
                dve.wait_ge(g.std, n + 1)
                nc.vector.reciprocal(rstd, std).then_inc(g.rstd, 1)
                dve.wait_ge(g.rstd, n + 1)
                for t in range(HT):
                    nc.vector.scalar_tensor_tensor(hn[h][:, t, :], x_res[:, bass.ds(base + t, 1), :].rearrange("p o d -> p (o d)"),
                                                   rstd[:, t:t + 1], gain[:, :], ALU.mult, ALU.mult).then_inc(g.hn, 1)

            def transposed(n):
                for k in range(KC):
                    dve.wait_ge(g.t_hi, n * KC + k + 1)
                    lo_of(a_lo[:, k, :], bank[k][:, :], a_hi[:, k, :]).then_inc(g.t_lo, 1)

            dve.wait_ge(g.consts, 16)
            nc.vector.tensor_copy(tri[:, :], cf[:, C_TRI:C_TRI + P]).then_inc(g.cast, 1)
            dve.sem_inc(s.ev_dve, BANKS)
            dve.wait_ge(g.small, 16 * 8)
            with dve.Fori(0, HALVES) as hf:
                dve.wait_ge(g.x_loaded, 16 * (hf + 1))
                dve.wait_ge(g.gain_ready, 16)
                norm(hf, 0, hf * HT)
                transposed(hf)

                def unit(u):
                    dve.wait_ge(s.hi, hf * SU + u + 1)
                    lo_of(w_lo[:, u % RING, :], raw[:, u % RING, :], w_hi[:, u % RING, :]).then_inc(s.lo, 1)

                def wait_full(first_full, b, last_unit):
                    if b < BF:
                        dve.wait_ge(s.full, hf * S_FULL + first_full + b + 1)
                    else:
                        dve.wait_ge(s.used, RING + hf * SU + last_unit)

                def v_banks(c4):
                    for b in range(BANKS):
                        wait_full((2 + c4) * BF, b, (3 + c4) * KC)
                        col = slice(c4 * 1024 + b % 2 * 512, c4 * 1024 + b % 2 * 512 + 512)
                        nc.vector.tensor_tensor(v_all[:, b // 2, col], bank[b][:, :], vbias[:, col], ALU.add) \
                            .then_inc(s.ev_dve, 1)
                for c4 in range(4):
                    for kc in range(3):
                        unit(c4 * KC + kc)
                    if c4 == 3:
                        v_banks(0)
                    for kc in range(3, KC):
                        unit(c4 * KC + kc)
                for kc in range(3):
                    unit(4 * KC + kc)
                v_banks(1)
                dve.wait_ge(s.v_sq, (hf + 1) * 2 * BANKS)
                nc.vector.tensor_reduce(ss, v_ss, AX.X, ALU.add).then_inc(s.v_sum, 1)
                dve.wait_ge(s.v_sum, hf + 1)
                nc.vector.tensor_scalar(var, ss, 1.0 / SGU, EPS, ALU.mult, ALU.add).then_inc(s.v_var, 1)
                dve.wait_ge(s.v_std, hf + 1)
                nc.vector.reciprocal(rstd, std).then_inc(s.v_rstd, 1)
                dve.wait_ge(s.v_rstd, hf + 1)
                for t in range(HT):
                    nc.vector.tensor_scalar(v_all[:, t, :], v_all[:, t, :], rstd[:, t:t + 1], None, ALU.mult) \
                        .then_inc(s.v_scaled, 1)
                for c in range(SGU // P):
                    dve.wait_ge(s.full, hf * S_FULL + 4 * BF + c + 1)
                    sv = bank[c % BANKS][:, :].rearrange("p (t s) -> p t s", s=P)
                    head = c * P * HEADS // SGU
                    nc.vector.scalar_tensor_tensor(sv, sv, cols[:, 16 + c:17 + c],
                                                   b_s[:, head:head + 1, :].to_broadcast([P, HT, P]),
                                                   ALU.mult, ALU.add).then_inc(s.gated, 1)
                    dve.wait_ge(s.gated, hf * (SGU // P) + c + 1)
                    if c:
                        dve.wait_ge(s.y_ready, hf * (SGU // P) + c)
                    nc.vector.tensor_tensor(u_all[:, c, :], bank[c % BANKS][:, :], u_all[:, c, :], ALU.mult) \
                        .then_inc(s.ev_dve, 1)
                    dve.wait_ge(s.ev_dve, BANKS + hf * S_EVD + 2 * BANKS + c + 1)
                    dve.sem_inc(s.y_ready, 1)
                for kc in range(SGU // P):
                    dve.wait_ge(s.y_hi, hf * (SGU // P) + kc + 1)
                    lo_of(y_lo[:, kc % 2, :], u_all[:, kc, :], y_hi[:, kc % 2, :]).then_inc(s.y_lo, 1)
                    if kc + 3 < SGU // P:
                        unit(4 * KC + kc + 3)
                for b in range(BANKS):
                    wait_full(4 * BF + SGU // P, b, SU)
                    x = x_res[:, bass.ds(hf * HT + b // 2, 1), b % 2 * 512:b % 2 * 512 + 512].rearrange("p o d -> p (o d)")
                    nc.vector.tensor_tensor(x, bank[b][:, :], x, ALU.add).then_inc(s.ev_dve, 1)
                dve.wait_ge(s.ev_dve, BANKS + (hf + 1) * S_EVD)

            def moe(L):
                M, n0 = m[L], 4 * L + 2
                dve.wait_ge(M.small, 32)
                dve.wait_ge(M.rw_hi, 1)
                lo_of(rw_lo, rw, rw_hi).then_inc(M.rw_lo, 1)
                for h in range(HALVES):
                    dve.wait_ge(g.gain_ready, 16 * (2 * L + 2))
                    norm(n0 + h, h, h * HT)
                    transposed(n0 + h)
                    dve.wait_ge(M.logits, h + 1)
                    nc.vector.tensor_tensor(lg[:, h * HT:(h + 1) * HT, :],
                                            bank[0][:, 0:HT * 36].rearrange("p (t c) -> p t c", c=36),
                                            rb.to_broadcast([P, HT, 36]), ALU.add).then_inc(M.logits_read, 1)
                dve.wait_ge(M.logits_read, HALVES)

                steps = [0]

                def step(ins):
                    steps[0] += 1
                    ins.then_inc(M.chain, 1)
                    dve.wait_ge(M.chain, steps[0])

                def tt(dst, a, b, op):
                    return nc.vector.tensor_tensor(dst, a, b, op)

                step(nc.vector.memset(r_gpad, -BIG))
                step(nc.vector.tensor_copy(r_gpad[:, :, 0:GROUPS], lg[:, :, 0:GROUPS]))
                for t in range(TT):
                    last = nc.vector.max(r_gmax[:, t, :], r_gpad[:, t, :])
                step(last)
                tt(r_gexp, lg[:, :, 0:GROUPS], r_gmax[:, :, 0:1].to_broadcast([P, TT, GROUPS]), ALU.subtract) \
                    .then_inc(M.g_shifted, 1)
                for t in range(TT):
                    last = nc.vector.max_index(r_gidx[:, t, :], r_gmax[:, t, :], r_gpad[:, t, :])
                step(last)
                step(nc.vector.tensor_copy(r_grp, r_gidx[:, :, 0:1]))
                step(tt(r_mask, const3(C_GRP, E, TT), r_grp.to_broadcast([P, TT, E]), ALU.is_equal))
                step(tt(r_el, r_mask, lg[:, :, GROUPS:36], ALU.mult))
                step(nc.vector.tensor_scalar(r_mask, r_mask, BIG, -BIG, ALU.mult, ALU.add))
                step(tt(r_el, r_el, r_mask, ALU.add))
                for t in range(TT):
                    last = nc.vector.max(r_emax[:, t, :], r_el[:, t, :])
                step(last)
                tt(r_ediff, r_emax[:, :, 1:2], r_emax[:, :, 0:1], ALU.subtract).then_inc(M.e_shifted, 1)
                for t in range(TT):
                    last = nc.vector.max_index(r_eidx[:, t, :], r_emax[:, t, :], r_el[:, t, :])
                step(last)
                step(nc.vector.tensor_copy(r_e, r_eidx[:, :, 0:2]))
                step(tt(r_oh[0], const3(C_E, E, TT), r_e[:, :, 0:1].to_broadcast([P, TT, E]), ALU.is_equal))
                step(tt(r_oh[1], const3(C_E, E, TT), r_e[:, :, 1:2].to_broadcast([P, TT, E]), ALU.is_equal))
                tt(chosen[:, :, :], r_oh[0], r_oh[1], ALU.add).then_inc(M.chosen, 1)
                dve.wait_ge(M.exp_g, 1)
                step(nc.vector.tensor_reduce(r_gsum, r_gexp, AX.X, ALU.add))
                step(nc.vector.reciprocal(r_gw, r_gsum))
                dve.wait_ge(M.exp_e, 1)
                step(nc.vector.tensor_scalar(r_den, r_eexp, 1.0, None, ALU.add))
                step(nc.vector.reciprocal(r_rden, r_den))
                step(tt(r_w[:, :, 0:1], r_gw, r_rden, ALU.mult))
                step(tt(r_w[:, :, 1:2], r_w[:, :, 0:1], r_eexp, ALU.mult))
                step(nc.vector.tensor_copy(payload[:, :, :, 2:3].bitcast(F32).rearrange("p t k w -> p t (k w)"), r_w))
                dve.wait_ge(M.ranked, 1)
                step(tt(r_pos, bank[0][:, 0:TT * E].rearrange("p (t e) -> p t e", e=E), const3(C_BASE, E, TT), ALU.add))
                for k in range(2):
                    step(tt(r_oh[k], r_oh[k], r_pos, ALU.mult))
                    step(nc.vector.tensor_reduce(r_place[:, :, k:k + 1], r_oh[k], AX.X, ALU.add))
                nc.vector.tensor_copy(place[:, :, :], r_place).then_inc(M.placed, 1)

                step(nc.vector.memset(sbias[0:1, 0:12 * E], 0.0))
                over = [sbias[0:1, 2 * E * k:2 * E * (k + 1)] for k in range(6)]
                cmp = sbias[0:1, 512:512 + E * (BPE - 1)].rearrange("p (e b) -> p e b", b=BPE - 1)
                thr = cf[0:1, C_THR:C_THR + BPE - 1].rearrange("p (o b) -> p o b", o=1)
                step(tt(cmp, bank[1][0:1, 0:E].rearrange("p (e o) -> p e o", o=1).to_broadcast([1, E, BPE - 1]),
                        thr.to_broadcast([1, E, BPE - 1]), ALU.is_gt))
                step(nc.vector.tensor_reduce(over[0][:, E:2 * E], cmp, AX.X, ALU.add))
                for k in range(5):
                    step(tt(over[k + 1][:, E:2 * E], over[k][:, E:2 * E], over[k][:, E - 2 ** k:2 * E - 2 ** k], ALU.add))
                incl, excl, row = over[5][:, E:2 * E], sbias[0:1, 768:768 + E], sbias[0:1, 800:800 + E]
                step(tt(excl, incl, over[0][:, E:2 * E], ALU.subtract))
                step(tt(row, cf[0:1, C_E8:C_E8 + E], excl, ALU.subtract))
                ind, tmp = [vbias[0:1, 512 * k:512 * (k + 1)].rearrange("p (j e) -> p j e", e=E) for k in (0, 1)]

                def by_e(ap):
                    return ap.rearrange("p (o e) -> p o e", o=1).to_broadcast([1, EXTRA, E])
                by_j = cf[0:1, C_J:C_J + EXTRA].rearrange("p (j o) -> p j o", o=1).to_broadcast([1, EXTRA, E])
                step(tt(ind, by_e(excl), by_j, ALU.is_le))
                step(tt(tmp, by_e(incl), by_j, ALU.is_gt))
                step(tt(ind, ind, tmp, ALU.mult))
                step(tt(tmp, ind, by_e(cf[0:1, C_E:C_E + E]), ALU.mult))
                step(nc.vector.tensor_reduce(sbias[0:1, 832:832 + EXTRA], tmp, AX.X, ALU.add))
                step(tt(tmp, by_e(row), by_j, ALU.add))
                step(tt(tmp, tmp, ind, ALU.mult))
                step(nc.vector.tensor_reduce(sbias[0:1, 848:848 + EXTRA], tmp, AX.X, ALU.add))
                step(nc.vector.tensor_copy(table[0:1, 0, E:E + EXTRA], sbias[0:1, 832:832 + EXTRA]))
                step(nc.vector.tensor_copy(table[0:1, 1, E:E + EXTRA], sbias[0:1, 848:848 + EXTRA]))
                nc.vector.tensor_scalar(table[0:1, 0, TABLE - 1:TABLE], incl[:, E - 1:E], float(E - 2), None, ALU.add) \
                    .then_inc(M.table, 1)

                def unit(c, hi):
                    dve.wait_ge(M.hi, hi)
                    return lo_of(w_lo[:, c % RING, :], moe_raw[c], w_hi[:, c % RING, :])

                def x_split(i):
                    for b in range(2):
                        dve.wait_ge(M.x_hi, 2 * i + b + 1)
                        lo_of(x_lo[:, 4 * b:4 * b + 4, :].rearrange("p k t -> p (k t)"), bank[4 + b][:, :],
                              x_hi[:, 4 * b:4 * b + 4, :].rearrange("p k t -> p (k t)")).then_inc(M.x_lo, 1)

                def hidden(i):
                    dve.wait_ge(M.silu, i + 1)
                    dve.wait_ge(M.used, ROUND * i + GU)
                    if not isinstance(i, int) or i:
                        dve.wait_ge(M.h_full, i)
                    nc.vector.tensor_tensor(hid, bank[1][:, :], silu_g, ALU.mult).then_inc(M.hid, 1)

                def h_split(i):
                    dve.wait_ge(M.h_hi, i + 1)
                    lo_of(h_lo.rearrange("p k t -> p (k t)"), bank[6][:, :],
                          h_hi.rearrange("p k t -> p (k t)")).then_inc(M.h_lo, 1)

                def round_(i):
                    for c in range(4):
                        unit(c, ROUND * i + c + 1).then_inc(M.lo, 1)
                    h_split(i - 1)
                    for c in range(4, ROUND):
                        unit(c, ROUND * i + c + 1).then_inc(M.lo, 1)
                    hidden(i)
                    x_split(i + 1)

                x_split(0)
                for c in range(GU):
                    unit(c, c + 1).then_inc(M.lo, 1 + (DN if c == GU - 1 else 0))
                hidden(0)
                x_split(1)
                dve.wait_ge(M.table, 1)
                n = dve.value_load(table[0:1, 0, TABLE - 1:TABLE], min_val=E - 2, max_val=ITEMS_MAX - 2) + 2
                round_(1)
                with dve.Fori(2, n) as i:
                    round_(i)
                for c in range(DN):
                    unit(GU + c, ROUND * n + c + 1).then_inc(M.lo, 1)
                h_split(n - 1)
                for t in range(TT):
                    dve.wait_ge(M.comb[t % 2], 16 * (t // 2 + 1))
                    nc.vector.tensor_tensor(x_res[:, t, :], x_res[:, t, :], comb[t % 2][:, 0, :], ALU.add) \
                        .then_inc(M.summed, 1)
                    dve.wait_ge(M.summed, t + 1)
                    nc.vector.tensor_tensor(x_res[:, t, :], x_res[:, t, :], comb[t % 2][:, 1, :], ALU.add) \
                        .then_inc(M.added, 1)
                dve.wait_ge(M.added, TT)

            moe(0)

            dve.wait_ge(g.gain_ready, 16 * 3)
            with dve.Fori(0, HALVES) as hf:
                norm(4 + hf, 0, hf * HT)
                transposed(4 + hf)
                for u in range(PV):
                    dve.wait_ge(q.hi, hf * PV + u + 1)
                    lo_of(w_lo[:, u % RING, :], raw[:, u % RING, :], w_hi[:, u % RING, :]).then_inc(q.lo, 1)
            dve.wait_ge(g.t_full, 6 * KC)
            for n in range(2):
                nc.vector.memset(padded[n][:, 0:PAD], 0.0).then_inc(q.zeroed, 1)
                nc.vector.memset(padded[n][:, PAD + SEQ:], 0.0).then_inc(q.zeroed, 1)
            steps = [0]

            def step(ins):
                steps[0] += 1
                ins.then_inc(q.chain, 1)
                dve.wait_ge(q.chain, steps[0])

            def d_split(hf, c):
                dve.wait_ge(q.d_hi, hf * KC + c + 1)
                lo_of(a_lo[:, c, :], pooled[:, c, hf * HTOK:(hf + 1) * HTOK], a_hi[:, c, :]).then_inc(q.d_lo, 1)

            for c in range(KC):
                w = WINDOWS[c * P * len(WINDOWS) // D]
                dve.wait_ge(q.padded, c + 1)
                v = padded[c % 2]
                cur, lo, hi, width, other = v, 0, SEQ + 2 * PAD, 1, 0
                while width < w:
                    back, ahead = (1, 0) if width == 1 else (width // 2, width // 2)
                    nxt = sums[other]
                    step(nc.vector.tensor_tensor(nxt[:, lo + back:hi - ahead], cur[:, lo:hi - ahead - back],
                                                 cur[:, lo + ahead + back:hi], ALU.add))
                    cur, lo, hi, width, other = nxt, lo + back, hi - ahead, 2 * width, 1 - other
                h = w // 2
                edges = [(0, h, C_ASC + h)] + ([(SEQ - h + 1, h - 1, C_DESC + 16 - (w - 1))] if h > 1 else [])
                scaled = sums[other][:, 0:2 * PAD]
                for n, (at, size, cc) in enumerate(edges):
                    step(nc.vector.tensor_tensor(scaled[:, n * PAD:n * PAD + size], cur[:, PAD + at:PAD + at + size],
                                                 cf[:, cc:cc + size], ALU.mult))
                step(nc.vector.scalar_tensor_tensor(pooled[:, c, :], cur[:, PAD:PAD + SEQ], 1.0 / w, v[:, PAD:PAD + SEQ],
                                                    ALU.mult, ALU.subtract))
                for n, (at, size, cc) in enumerate(edges):
                    step(nc.vector.tensor_tensor(pooled[:, c, at:at + size], scaled[:, n * PAD:n * PAD + size],
                                                 v[:, PAD + at:PAD + at + size], ALU.subtract))
                dve.sem_inc(q.d_ready, 1)
                if c:
                    d_split(0, c - 1)
            d_split(0, KC - 1)
            for hf in range(HALVES):
                base = HALVES * PV + hf * (PG + PO)

                def unit(u):
                    dve.wait_ge(q.hi, u + 1)
                    lo_of(w_lo[:, u % RING, :], raw[:, u % RING, :], w_hi[:, u % RING, :]).then_inc(q.lo, 1)
                for r in range(3):
                    unit(base + r)
                for kc in range(KC):
                    dve.wait_ge(q.y_hi, hf * KC + kc + 1)
                    lo_of(y_lo[:, kc % 2, :], y_f32[:, kc, :], y_hi[:, kc % 2, :]).then_inc(q.y_lo, 1)
                    if PG + kc + 1 < PG + PO:
                        unit(base + PG + kc + 1)
                    if hf == 0:
                        d_split(1, kc)
                for b in range(BANKS):
                    if b < BF:
                        dve.wait_ge(q.full, Q_V + hf * Q_HALF + 6 + b + 1)
                    else:
                        dve.wait_ge(q.used, RING + base + PG + PO)
                    x = x_res[:, hf * HT + b // 2, b % 2 * 512:b % 2 * 512 + 512]
                    nc.vector.tensor_tensor(x, bank[b][:, :], x, ALU.add).then_inc(q.ev_dve, 1)
            dve.wait_ge(q.ev_dve, HALVES * BANKS)

            moe(1)

            dve.wait_ge(g.gain_ready, 16 * 5)
            for h in range(HALVES):
                norm(8 + h, h, h * HT)


_SHAPES = ((1, SEQ, D), "float32")


def kernel(**inputs):
    import numpy as np
    import concourse.bacc as bacc
    from concourse.bass_utils import run_bass_kernel_spmd as run

    def by_partition(a, width):
        return np.ascontiguousarray(a.reshape(width, P).T)

    a = {k: np.ascontiguousarray(inputs[k]) for k in (
        "x", "norm_mix_g", "norm_ffn_g", "final_norm_g", "a_w_in", "a_b_in", "a_w_out", "a_b_spatial",
        "b_w_in", "b_w_group", "b_w_out", "w_gate", "w_up", "w_down")}
    a["w_s"] = np.ascontiguousarray(np.asarray(inputs["a_w_spatial"])[0].transpose(2, 0, 1).reshape(P, HEADS * P))
    a["u_bias"] = by_partition(np.asarray(inputs["a_b_in"])[0, :SGU], SGU // P)
    a["v_gain"] = by_partition(np.asarray(inputs["a_norm_v"])[0], SGU // P)
    a["pool_scale"] = by_partition(np.asarray(inputs["b_scale"])[0], KC)
    rw = np.concatenate([np.asarray(inputs["router_group_w"]), np.asarray(inputs["router_expert_w"])], axis=2)
    a["router_w"] = np.ascontiguousarray(rw.reshape(LAYERS, KC, P, 36).transpose(0, 2, 1, 3).reshape(LAYERS, P, KC * 36))
    a["router_b"] = np.concatenate([np.asarray(inputs["router_group_b"]), np.asarray(inputs["router_expert_b"])], axis=1)

    c = np.zeros((P, C_ALL), np.float32)
    c[:, C_ID:C_ID + P] = np.eye(P)
    c[:, C_TRI:C_TRI + P] = np.triu(np.ones((P, P)), 1)
    c[:, C_E:C_E + E] = np.arange(E)
    c[:, C_GRP:C_GRP + E] = np.arange(E) // EPG
    c[:, C_BASE:C_BASE + E] = np.arange(E) * LISTED
    c[:, C_ASC + 1:C_ASC + 16] = 1.0 / np.arange(1, 16)
    c[:, C_DESC:C_DESC + 16] = 1.0 / (16 - np.arange(16))
    c[:, C_THR:C_THR + BPE - 1] = BLK * np.arange(1, BPE)
    c[:, C_J:C_J + EXTRA] = np.arange(EXTRA)
    c[:, C_E8:C_E8 + E] = BPE * np.arange(E) + 1
    a["c_float"] = c
    tok = np.arange(TT)[None, :] * P + np.arange(P)[:, None]
    pay = np.zeros((P, TT, 2, 4), np.int32)
    pay[..., 0] = tok[..., None]
    pay[..., 1] = 2 * tok[..., None] + np.arange(2)
    a["c_payload"] = pay.reshape(P, TT * 8)
    tab = np.zeros((1, 2, TABLE), np.int32)
    tab[0, 0, :E] = np.arange(E)
    tab[0, 1, :E] = np.arange(E) * BPE
    a["c_table"] = tab

    nc = bacc.Bacc("TRN2", target_bir_lowering=False, num_devices=1)
    arrays, aps = {}, {}
    for name, v in a.items():
        arrays[f"in_{name}"] = v
        aps[name] = nc.dram_tensor(f"in_{name}", v.shape, mybir.dt.from_np(v.dtype), kind="ExternalInput").ap()
    out = nc.dram_tensor("out_0", _SHAPES[0], F32, kind="ExternalOutput").ap()
    encoder_trunk(nc, aps, out)
    r = run(nc, [arrays], core_ids=[0])
    return r.results[0]["out_0"]
```

```python
from collections import namedtuple
from contextlib import ExitStack

import concourse.bass as bass
from concourse import mybir

F32, F32R, BF16, I32, U32 = (mybir.dt.float32, mybir.dt.float32r, mybir.dt.bfloat16,
                             mybir.dt.int32, mybir.dt.uint32)
ALU, ACT, AX = mybir.AluOpType, mybir.ActivationFunctionType, mybir.AxisListType

P = 128
D = 1024
SEQ = 1024
TT = SEQ // P
HALVES = 2
HT = TT // HALVES
HTOK = HT * P
KC = D // P
SGU = 2 * D
HEADS = 8
F = D // 2
E = 32
GROUPS = 4
EPG = E // GROUPS
LAYERS = 2
BANKS = 8
RING = 4
UNIT = 1024
GU, DN = 8, 4
ROUND = GU + DN
COMBS = 4
BLK = P
LISTED = SEQ
BPE = LISTED // BLK
EXTRA = 2 * SEQ // BLK
ITEMS_MAX = E + EXTRA - 1
TABLE = 64
EPS = 1e-6
WINDOWS = (2, 4, 8, 16)
PAD = WINDOWS[-1] // 2
BIG = 1e30

C_ID, C_TRI, C_E, C_GRP, C_BASE = 0, P, 2 * P, 2 * P + E, 2 * P + 2 * E
C_ASC = C_BASE + E
C_DESC, C_THR = C_ASC + 16, C_ASC + 32
C_J = C_THR + BPE - 1
C_E8 = C_J + 16
C_ALL = C_E8 + E


def encoder_trunk(nc, A, out):
    ctx = ExitStack()
    with ctx:
        def sb(name, shape, dt):
            return ctx.enter_context(nc.sbuf_tensor(name, shape, dt))

        def sems(phase, names, arrays):
            def one(n):
                return ctx.enter_context(nc.semaphore(f"{phase}_{n}"))
            made = {n: one(n) for n in names} | {n: [one(f"{n}{i}") for i in range(k)] for n, k in arrays.items()}
            return namedtuple("Sems", made)(**made)

        x_res = sb("x_res", [P, TT, D], F32)
        raw = sb("raw", [P, RING, UNIT], F32)
        w_hi = sb("w_hi", [P, RING, UNIT], F32R)
        w_lo = sb("w_lo", [P, RING, UNIT], F32R)
        a_hi = sb("a_hi", [P, KC, HTOK], F32R)
        a_lo = sb("a_lo", [P, KC, HTOK], F32R)
        y_hi = sb("y_hi", [P, 2, HTOK], F32R)
        y_lo = sb("y_lo", [P, 2, HTOK], F32R)
        bu = sb("bu", [P, 8 * 1024], F32)
        bv = sb("bv", [P, 8 * 1024], F32)
        gain = sb("gain", [P, D], F32)
        spatial = sb("spatial", [P, HEADS * P], F32)
        sbias = sb("sbias", [P, HEADS * P], F32)
        vbias = sb("vbias", [P, SGU], F32)
        cf = sb("cf", [P, C_ALL], F32)
        tri = sb("tri", [P, P], BF16)
        ones = sb("ones", [P, P], BF16)
        chosen = sb("chosen", [P, TT, E], BF16)
        payload = sb("payload", [P, TT, 2, 4], I32)
        place = sb("place", [P, TT, 2], I32)
        table = sb("table", [1, 2, TABLE], I32)
        metas = sb("metas", [P, 8], I32)
        cols = sb("cols", [P, 72], F32)
        bank = [ctx.enter_context(nc.psum_tensor(f"bank{b}", [P, 512], F32)) for b in range(BANKS)]

        def dram(name, shape, dt):
            return nc.dram_tensor(name, shape, dt, kind="Internal").ap()
        normed = [dram(f"normed{n}", (SEQ, D), F32) for n in range(LAYERS)]
        y_rows = [dram(f"y_rows{n}", (2 * SEQ, D), F32) for n in range(LAYERS)]
        lists = [dram(f"lists{n}", (E * LISTED, 4), I32) for n in range(LAYERS)]

        meta_g, meta_s = metas[:, 0:4], metas[:, 4:8]
        ss, var, std, rstd = [cols[:, 40 + 4 * n:44 + 4 * n] for n in range(4)]
        rb = cols[:, 0:1]
        v_ss = cols[:, 56:72].rearrange("p (t c) -> p t c", c=4)
        ident = cf[:, C_ID:C_ID + P]
        hn = [bv[:, h * HT * D:(h + 1) * HT * D].rearrange("p (t d) -> p t d", d=D) for h in range(2)]
        u_all = bu[:, :].rearrange("p (c t) -> p c t", t=HTOK)
        v_all = bv[:, :].rearrange("p (t d) -> p t d", d=SGU)
        w_s = spatial[:, :].rearrange("p (h t) -> p h t", h=HEADS)
        b_s = sbias[:, :].rearrange("p (h t) -> p h t", h=HEADS)
        pooled = bu[:, :].rearrange("p (c t) -> p c t", t=SEQ)
        xg = bv[:, 4096:5120]
        y_sb = bv[:, 5120:6144].rearrange("p (n f) -> p n f", n=2)
        silu_g = bv[:, 6144:6144 + F]
        hid = bv[:, 6144 + F:6144 + 2 * F]
        comb = [bu[:, n * 2048:(n + 1) * 2048].rearrange("p (k d) -> p k d", k=2) for n in range(COMBS)]
        x_hi = a_hi[:, 0:2, :].rearrange("p a (k t) -> p (a k) t", t=P)
        x_lo = a_lo[:, 0:2, :].rearrange("p a (k t) -> p (a k) t", t=P)
        h_hi = a_hi[:, 2, :].rearrange("p (k t) -> p k t", t=P)
        h_lo = a_lo[:, 2, :].rearrange("p (k t) -> p k t", t=P)
        moe_raw = [raw[:, n, :] for n in range(RING)] + \
                  [bu[:, n * UNIT:(n + 1) * UNIT] for n in range(ROUND - RING)]

        rw_hi = y_hi[:, :, :].rearrange("p a (k c) -> p (a k) c", c=P)
        rw_lo = y_lo[:, :, :].rearrange("p a (k c) -> p (a k) c", c=P)
        lt = sbias[:, 0:HTOK]
        lg = sbias[:, HTOK:HTOK + TT * 36].rearrange("p (t c) -> p t c", c=36)

        def scratch(at, width, dt=F32):
            v = vbias[:, at:at + TT * width]
            return (v if dt is F32 else v.bitcast(dt)).rearrange("p (t c) -> p t c", c=width)
        r_gpad, r_gmax, r_gidx = scratch(0, 8), scratch(64, 8), scratch(128, 8, U32)
        r_gexp, r_gsum, r_gw, r_grp = scratch(192, GROUPS), scratch(224, 1), scratch(232, 1), scratch(240, 1)
        r_mask, r_el = scratch(256, E), scratch(512, E)
        r_emax, r_eidx, r_e = scratch(768, 8), scratch(832, 8, U32), scratch(896, 2)
        r_ediff, r_eexp, r_den, r_rden = scratch(912, 1), scratch(920, 1), scratch(928, 1), scratch(936, 1)
        r_w, r_place = scratch(944, 2), scratch(960, 2)
        r_oh, r_pos = [scratch(1024, E), scratch(1280, E)], scratch(1536, E)

        def const3(at, width, n):
            return cf[:, at:at + width].rearrange("p (o e) -> p o e", o=1).to_broadcast([P, n, width])
        padded = [bv[:, n * 1040:(n + 1) * 1040] for n in range(2)]
        sums = [bv[:, 2080:3120], vbias[:, 0:1040]]
        y_f32 = bv[:, 4096:8192].rearrange("p (c t) -> p c t", t=HTOK)

        def f32(ap):
            return ap.bitcast(F32)

        g = sems("g", ["consts", "cast", "init", "lists_ready", "gain_ready", "small",
                       "sq", "var", "std", "rstd", "waited", "hn", "t_full", "t_hi", "t_lo", "out_stored"], 
                 {"x_loaded": HT, "comb": COMBS})
        RINGS = ["hi", "lo", "used"]
        s = sems("sgu", RINGS + ["full", "ev_act", "ev_dve", "v_sq", "v_gelu", "v_chain", "v_var", "v_std",
                                 "v_scaled", "gated", "y_hi", "y_lo"],
                 {"raw": RING})
        q = sems("pool", RINGS + ["full", "ev_act", "ev_dve", "zeroed", "padded", "chain", "d_ready", "d_hi",
                                  "d_lo", "g_out", "y_hi", "y_lo"],
                 {"raw": RING})
        MOE = ["hi", "lo", "used", "rw_hi", "rw_lo", "logits", "biased", "logits_read", "chain",
               "exps", "g_shifted", "e_shifted", "chosen", "ranked", "placed", "listed", "table",
               "meta_g", "gathered", "x_full", "x_hi", "x_lo", "silu", "hid",
               "h_full", "h_hi", "h_lo", "y_out", "meta_s", "scattered",
               "added", "small", "summed"]
        m = [sems(f"moe{n}", MOE, {"raw": ROUND, "stored": HALVES}) for n in range(LAYERS)]

        SU = 3 * 2 * KC
        PV, PG, PO = KC, 2, KC

        BF = BANKS - 1
        S_FULL = 2 * BF + 2 * BF + SGU // P + BF
        S_EVD = 2 * BANKS + SGU // P + BANKS
        S_EVA = 2 * BANKS

        block = ctx.enter_context(nc.Block())

        @block.sync
        def _(sp):
            sp.dma_start(cf[:, :], A["c_float"]).then_inc(g.consts, 16)
            xv = A["x"].rearrange("o (t p) d -> p (o t) d", p=P)
            for h in range(HALVES):
                for t in range(HT):
                    if h:
                        sp.wait_ge(g.x_loaded[t], 16)
                    sp.dma_start(x_res[:, h * HT + t, :], xv[:, h * HT + t, :]).then_inc(g.x_loaded[t], 16)
                if h == 0:
                    for kc in range(RING):
                        sp.dma_start(raw[:, kc, :], A["a_w_in"][0, kc * P:(kc + 1) * P, SGU:SGU + UNIT]) \
                            .then_inc(s.raw[kc], 16)
            sp.sem_inc(s.lo, RING)

            def sgu_in(hf, c, col, first):
                for kc in range(first, KC):
                    sp.wait_ge(s.lo, hf * SU + c * KC + kc + 1)
                    sp.dma_start(raw[:, kc % RING, :], A["a_w_in"][0, kc * P:(kc + 1) * P, bass.ds(col, UNIT)]) \
                        .then_inc(s.raw[kc % RING], 16)

            def sgu_half(hf, first):
                sgu_in(hf, 0, SGU, RING if first else 0)
                sgu_in(hf, 1, SGU + UNIT, 0)
                with sp.Fori(0, 2) as c:
                    sgu_in(hf, c + 2, c * UNIT, 0)
                with sp.Fori(0, 2) as o:
                    for kc in range(KC):
                        sp.wait_ge(s.lo, hf * SU + 4 * KC + o * KC + kc + 1)
                        sp.dma_start(raw[:, kc % RING, :], A["a_w_out"][0, bass.ds((o * KC + kc) * P, P), :]) \
                            .then_inc(s.raw[kc % RING], 16)
            sgu_half(0, True)
            sgu_half(1, False)

            def moe(L, before_lo, before_y):
                M = m[L]
                gate = A["w_gate"][L].rearrange("e (p k) f -> p e k f", k=KC)
                up = A["w_up"][L].rearrange("e (p k) f -> p e k f", k=KC)
                down = A["w_down"][L].rearrange("e (p k) d -> p e k d", k=DN)

                def load_gu(e, j):
                    w = gate if j < DN else up
                    k = 2 * (j % DN)
                    sp.dma_start(moe_raw[j].rearrange("p (e k f) -> p e k f", e=1, k=2),
                                 w[:, bass.ds(e, 1), k:k + 2, :]).then_inc(M.raw[j], 16)

                def load_dn(e, j):
                    sp.dma_start(moe_raw[GU + j].rearrange("p (e k d) -> p e k d", e=1, k=1),
                                 down[:, bass.ds(e, 1), j:j + 1, :]).then_inc(M.raw[GU + j], 16)

                before_lo(sp)
                for j in range(RING):
                    load_gu(0, j)
                before_y(sp)
                for j in range(RING, GU):
                    load_gu(0, j)
                for j in range(DN):
                    load_dn(0, j)
                for h in range(HALVES):
                    sp.wait_ge(g.hn, HT * (4 * L + 2 + h + 1))
                    sp.dma_start(normed[L].rearrange("(t p) d -> p t d", p=P)[:, h * HT:(h + 1) * HT, :],
                                 hn[h]).then_inc(M.stored[h], 16)
                for j in range(GU):
                    sp.wait_ge(M.lo, j + 1)
                    load_gu(1, j)
                sp.wait_ge(M.table, 1)
                n = sp.value_load(table[0:1, 0, TABLE - 1:TABLE], min_val=E - 2, max_val=ITEMS_MAX - 2) + 2
                with sp.Fori(2, n) as i:
                    e_up = sp.value_load(table[0:1, 0, bass.ds(i, 1)], min_val=0, max_val=E - 1)
                    e_dn = sp.value_load(table[0:1, 0, bass.ds(i - 1, 1)], min_val=0, max_val=E - 1)
                    for j in range(GU):
                        sp.wait_ge(M.lo, ROUND * (i - 1) + j + 1)
                        load_gu(e_up, j)
                    for j in range(DN):
                        sp.wait_ge(M.lo, ROUND * (i - 1) + GU + j + 1)
                        load_dn(e_dn, j)
                e_dn = sp.value_load(table[0:1, 0, bass.ds(n - 1, 1)], min_val=0, max_val=E - 1)
                for j in range(DN):
                    sp.wait_ge(M.lo, ROUND * (n - 1) + GU + j + 1)
                    load_dn(e_dn, j)
                sp.wait_ge(M.scattered, 16 * n)
                yv = y_rows[L].rearrange("(t p k) d -> p t k d", p=P, k=2)
                for t in range(TT):
                    if t >= COMBS:
                        sp.wait_ge(M.added, t - COMBS + 1)
                    sp.dma_start(comb[t % COMBS], yv[:, t, :, :]).then_inc(g.comb[t % COMBS], 16)
                return n

            moe(0, lambda e: e.wait_ge(s.lo, RING + 2 * SU), lambda e: e.wait_ge(s.y_lo, 2 * 2 * KC))

            sp.sem_inc(q.lo, RING)
            wg = A["b_w_group"][0].rearrange("g (k p) f -> p g k f", k=2)
            with sp.Fori(0, HALVES) as hf:
                for kc in range(KC):
                    sp.wait_ge(q.lo, hf * PV + kc + 1)
                    sp.dma_start(raw[:, kc % RING, :], A["b_w_in"][0, kc * P:(kc + 1) * P, :]) \
                        .then_inc(q.raw[kc % RING], 16)

            def pool_out(hf, base):
                for r in range(PG + PO):
                    sp.wait_ge(q.lo, base + r + 1)
                    slot = (base + r) % RING
                    if r < PG:
                        sp.dma_start(raw[:, slot, :].rearrange("p (g k f) -> p g k f", g=2, k=2),
                                     wg[:, 2 * r:2 * r + 2, :, :]).then_inc(q.raw[slot], 16)
                    else:
                        kc = r - PG
                        sp.dma_start(raw[:, slot, :], A["b_w_out"][0, kc * P:(kc + 1) * P, :]) \
                            .then_inc(q.raw[slot], 16)
            for hf in range(HALVES):
                pool_out(hf, HALVES * PV + hf * (PG + PO))
            total = HALVES * (PV + PG + PO)
            moe(1, lambda e: e.wait_ge(q.lo, RING + total), lambda e: e.wait_ge(q.y_lo, HALVES * KC))

            ov = out.rearrange("o (t p) d -> p (o t) d", p=P)
            for h in range(HALVES):
                for t in range(HT):
                    sp.wait_ge(g.hn, 4 * (8 + h) + t + 1)
                    sp.dma_start(ov[:, h * HT + t, :], hn[h][:, t, :]).then_inc(g.out_stored, 16)
            sp.wait_ge(g.out_stored, 16 * TT)

        @block.gpsimd
        def _(pool):
            def waited():
                pool.sem_inc(g.waited, 1)

            def load_gain(k, src):
                if k:
                    pool.wait_ge(g.hn, 8 * k)
                pool.dma_start(gain[:, :], src.partition_broadcast(P)).then_inc(g.gain_ready, 16)

            load_gain(0, A["norm_mix_g"][0])
            pool.dma_start(payload[:, :, :, :].rearrange("p t k w -> p (t k w)"), A["c_payload"]).then_inc(g.small, 16)
            pool.dma_start(table[:, :, :], A["c_table"]).then_inc(g.small, 16)
            pool.dma_start(cols[:, 0:16], A["u_bias"]).then_inc(g.small, 16)
            pool.dma_start(cols[:, 16:32], A["v_gain"]).then_inc(g.small, 16)
            pool.dma_start(cols[:, 32:40], A["pool_scale"]).then_inc(g.small, 16)
            pool.dma_start(spatial[:, :], A["w_s"]).then_inc(g.small, 16)
            pool.dma_start(sbias[:, :], A["a_b_spatial"][0].rearrange("h t -> (h t)").partition_broadcast(P)) \
                .then_inc(g.small, 16)
            pool.dma_start(vbias[:, :], A["a_b_in"][0, SGU:2 * SGU].partition_broadcast(P)).then_inc(g.small, 16)
            pool.memset(ones[:, :], 1.0).then_inc(g.init, 1)
            pool.memset(bu[:, 0:1024], 1.0).then_inc(g.init, 1)
            pool.wait_ge(g.init, 2)
            for L in range(LAYERS):
                pool.dma_start(lists[L].rearrange("(p r) w -> p (r w)", p=P), bu[:, 0:1024].bitcast(I32)) \
                    .then_inc(g.lists_ready, 16)
            load_gain(1, A["norm_ffn_g"][0])

            def moe(L):
                M = m[L]
                lst = lists[L].rearrange("(b p) w -> p b w", p=BLK)
                if L == 0:
                    pool.wait_ge(s.ev_dve, BANKS + HALVES * S_EVD)
                else:
                    pool.wait_ge(q.ev_dve, HALVES * BANKS)
                pool.dma_start(spatial[:, :], A["router_w"][L]).then_inc(M.small, 16)
                pool.dma_start(rb, A["router_b"][L]).then_inc(M.small, 16)
                load_gain(2 * L + 2, A["norm_mix_g"][1] if L == 0 else A["final_norm_g"])
                pool.wait_ge(g.lists_ready, 16 * LAYERS)
                for t in range(TT):
                    if t % HT == 0:
                        pool.wait_ge(M.placed, t // HT + 1)
                    for k in range(2):
                        pool.indirect_dma_start(
                            out=lists[L][:, :],
                            out_offset=bass.IndirectOffsetOnAxis(ap=place[:, t, k:k + 1], axis=0),
                            in_=payload[:, t, k, :], in_offset=None).then_inc(M.listed, 16)
                pool.wait_ge(M.listed, 16 * 2 * TT)
                for h in range(HALVES):
                    pool.wait_ge(M.stored[h], 16)
                def block_of(i):
                    if isinstance(i, int):
                        return i * BPE
                    return pool.value_load(table[0:1, 1, bass.ds(i, 1)], min_val=0, max_val=E * BPE - 1)

                def gather(i):
                    b = block_of(i)
                    if not isinstance(i, int) or i > 0:
                        pool.wait_ge(M.x_full, i)
                        waited()
                    pool.dma_start(meta_g, lst[:, bass.ds(b, 1), :].rearrange("p b w -> p (b w)")).then_inc(M.meta_g, 16)
                    pool.wait_ge(M.meta_g, 16 * (i + 1))
                    waited()
                    pool.indirect_dma_start(
                        out=xg, out_offset=None, in_=normed[L][:, :],
                        in_offset=bass.IndirectOffsetOnAxis(ap=meta_g[:, 0:1], axis=0),
                        bounds_check=SEQ - 1, oob_is_err=False).then_inc(M.gathered, 16)

                def load_meta(i):
                    b = block_of(i)
                    pool.dma_start(meta_s, lst[:, bass.ds(b, 1), :].rearrange("p b w -> p (b w)")).then_inc(M.meta_s, 16)

                def scatter(i):
                    pool.wait_ge(M.y_out, 2 * (i + 1))
                    waited()
                    pool.indirect_dma_start(
                        out=y_rows[L][:, :],
                        out_offset=bass.IndirectOffsetOnAxis(ap=meta_s[:, 1:2], axis=0),
                        in_=y_sb.rearrange("p n f -> p (n f)"), in_offset=None,
                        bounds_check=2 * SEQ - 1, oob_is_err=False).then_inc(M.scattered, 16)
                    pool.wait_ge(M.scattered, 16 * (i + 1))
                    waited()

                gather(0)
                load_meta(0)
                gather(1)
                gather(2)
                pool.wait_ge(M.table, 1)
                n = pool.value_load(table[0:1, 0, TABLE - 1:TABLE], min_val=E - 2, max_val=ITEMS_MAX - 2) + 2
                with pool.Fori(2, n) as i:
                    gather(i + 1)
                    scatter(i - 2)
                    load_meta(i - 1)
                scatter(n - 2)
                load_meta(n - 1)
                scatter(n - 1)
                pool.wait_ge(M.gathered, 16 * (n + 1))
                waited()

            moe(0)
            load_gain(3, A["norm_ffn_g"][1])
            moe(1)

        @block.tensor
        def _(pe):
            def three(dst, left_hi, left_lo, right_hi, right_lo, first, last):
                pe.matmul(dst, left_hi, right_hi, start=first, stop=False)
                pe.matmul(dst, left_hi, right_lo, start=False, stop=False)
                return pe.matmul(dst, left_lo, right_hi, start=False, stop=last)

            def transposes(n, h, wait_bank):
                for t in range(HT):
                    pe.wait_ge(g.hn, HT * n + t + 1)
                    for k in range(KC):
                        if t == 0:
                            wait_bank(k)
                        last = pe.transpose(bank[k][:, t * P:(t + 1) * P], hn[h][:, t, k * P:(k + 1) * P], ident)
                        if t == HT - 1:
                            last.then_inc(g.t_full, 1)

            def channels_by_tokens(slot, kc, used, full, wait_bank):
                for c in range(BANKS):
                    if kc == 0:
                        wait_bank(c)
                    w = slice(c * P, (c + 1) * P)
                    last = three(bank[c][:, :], w_hi[:, slot, w], w_lo[:, slot, w],
                                 a_hi[:, kc, :], a_lo[:, kc, :], kc == 0, kc == KC - 1)
                    if kc == KC - 1 and c < BF:
                        last.then_inc(full, 1)
                last.then_inc(used, 1)

            def tokens_by_channels(slot, left_hi, left_lo, first, final, used, full, wait_bank):
                for t in range(HT):
                    for c in range(2):
                        if first:
                            wait_bank(2 * t + c)
                        col, row = slice(c * 512, (c + 1) * 512), slice(t * P, (t + 1) * P)
                        last = three(bank[2 * t + c][:, :], left_hi[:, row], left_lo[:, row],
                                     w_hi[:, slot, col], w_lo[:, slot, col], first, final)
                        if final and 2 * t + c < BF:
                            last.then_inc(full, 1)
                last.then_inc(used, 1)

            pe.wait_ge(g.consts, 16)

            pe.sem_inc(s.used, RING)
            with pe.Fori(0, HALVES) as hf:
                transposes(hf, 0, lambda k: pe.wait_ge(s.ev_dve, hf * S_EVD + k + 1))
                with pe.Fori(0, 2) as c4:
                    for kc in range(KC):
                        pe.wait_ge(s.lo, RING + hf * SU + c4 * KC + kc + 1)

                        def wait_bank(b):
                            pe.wait_ge(g.t_lo, hf * KC + KC)
                            pe.wait_ge(s.ev_dve, hf * S_EVD + c4 * BANKS + b + 1)
                        tokens_by_channels(kc % RING, a_hi[:, kc, :], a_lo[:, kc, :], kc == 0, kc == KC - 1,
                                           s.used, s.full, wait_bank)
                with pe.Fori(0, 2) as c4:
                    for kc in range(KC):
                        pe.wait_ge(s.lo, RING + hf * SU + (2 + c4) * KC + kc + 1)

                        def wait_bank(c):
                            pe.wait_ge(s.ev_dve, BANKS + hf * S_EVD + BANKS + c + 1)
                            pe.wait_ge(s.ev_act, hf * S_EVA + c4 * BANKS + c + 1)
                        channels_by_tokens(kc % RING, kc, s.used, s.full, wait_bank)
                pe.wait_ge(g.small, 16 * 8)
                pe.wait_ge(s.v_scaled, HT * (hf + 1))
                for c in range(SGU // P):
                    if c < BANKS:
                        pe.wait_ge(s.ev_act, BANKS + hf * S_EVA + BANKS + c + 1)
                    else:
                        pe.wait_ge(s.ev_dve, BANKS + hf * S_EVD + 2 * BANKS + c - BANKS + 1)
                    for t in range(HT):
                        last = pe.matmul(bank[c % BANKS][:, t * P:(t + 1) * P], v_all[:, t, c * P:(c + 1) * P],
                                         w_s[:, c * P * HEADS // SGU, :], start=True, stop=True)
                    last.then_inc(s.full, 1)
                for kc in range(SGU // P):
                    pe.wait_ge(s.lo, RING + hf * SU + 4 * KC + kc + 1)
                    pe.wait_ge(s.y_lo, hf * (SGU // P) + kc + 1)

                    def wait_bank(b):
                        pe.wait_ge(s.ev_dve, BANKS + hf * S_EVD + BANKS + SGU // P + b + 1)
                    tokens_by_channels(kc % RING, y_hi[:, kc % 2, :], y_lo[:, kc % 2, :], kc == 0,
                                       kc == SGU // P - 1, s.used, s.full, wait_bank)

            def moe(L, wait_mixer):
                M, n0 = m[L], 4 * L + 2
                for h in range(HALVES):
                    if h:
                        transposes(n0 + h, h, lambda k: pe.wait_ge(M.logits_read, 1) if k == 1 else None)
                    else:
                        transposes(n0, 0, wait_mixer)
                    pe.wait_ge(M.rw_lo, 1)
                    pe.wait_ge(g.t_lo, KC * (n0 + h + 1))
                    for k in range(KC):
                        last = three(bank[0][:, :], rw_hi[:, k, :], rw_lo[:, k, :], a_hi[:, k, :], a_lo[:, k, :],
                                     k == 0, k == KC - 1)
                    last.then_inc(M.logits, 1)
                    pe.wait_ge(M.biased, h + 1)
                    for t in range(HT):
                        last = pe.transpose(bank[1][:, t * P:(t + 1) * P], lt[:, t * P:(t + 1) * P], ident)
                    last.then_inc(M.logits, 1)
                pe.wait_ge(g.cast, 1)
                pe.wait_ge(g.init, 1)
                for h in range(HALVES):
                    pe.wait_ge(M.chosen, h + 1)
                    for t in range(h * HT, (h + 1) * HT):
                        dst = bank[2 + h][:, t % HT * E:(t % HT + 1) * E]
                        last = pe.matmul(dst, tri[:, :], chosen[:, t, :], start=True, stop=t == 0)
                        for b in range(t):
                            last = pe.matmul(dst, ones[:, :], chosen[:, b, :], start=False, stop=b == t - 1)
                    last.then_inc(M.ranked, 1)
                for t in range(TT):
                    last = pe.matmul(bank[7][:, 0:E], ones[:, :], chosen[:, t, :], start=t == 0, stop=t == TT - 1)
                last.then_inc(M.ranked, 1)

                def x_transposes(i):
                    pe.wait_ge(M.gathered, 16 * (i + 1))
                    rows = xg.rearrange("t (p k) -> t k p", k=KC)
                    for k in range(KC):
                        last = pe.transpose(bank[4 + k // 4][:, k % 4 * P:(k % 4 + 1) * P], rows[:, k, :], ident)
                    last.then_inc(M.x_full, 1)

                def gate_up(i, lo_wait, gap):
                    pe.wait_ge(M.x_lo, 2 * (i + 1))
                    for j in range(GU):
                        lo_wait(j)
                        for k in range(2):
                            c = 2 * (j % DN) + k
                            col = slice(k * F, (k + 1) * F)
                            last = three(bank[j // DN][:, :], x_hi[:, c, :], x_lo[:, c, :],
                                         w_hi[:, j % RING, col], w_lo[:, j % RING, col], c == 0, c == KC - 1)
                        last.then_inc(M.used, 1 + (gap if j == GU - 1 else 0))

                def down(i, lo_wait):
                    pe.wait_ge(M.h_lo, i + 1)
                    for j in range(DN):
                        lo_wait(j)
                        for c in range(2):
                            col = slice(c * 512, (c + 1) * 512)
                            last = three(bank[2 + c][:, :], h_hi[:, j, :], h_lo[:, j, :],
                                         w_hi[:, j, col], w_lo[:, j, col], j == 0, j == DN - 1)
                        last.then_inc(M.used, 1)

                def h_transposes(i):
                    pe.wait_ge(M.hid, i + 1)
                    cols_of = hid.rearrange("t (p k) -> t k p", k=DN)
                    for k in range(DN):
                        last = pe.transpose(bank[6][:, k * P:(k + 1) * P], cols_of[:, k, :], ident)
                    last.then_inc(M.h_full, 1)

                def round_(i, before_down):
                    pe.wait_ge(M.hid, i)
                    gate_up(i, lambda j: pe.wait_ge(M.lo, ROUND * i + j + 1), 0)
                    x_transposes(i + 1)
                    before_down(i)
                    down(i - 1, lambda j: pe.wait_ge(M.lo, ROUND * i + GU + j + 1))
                    h_transposes(i)

                x_transposes(0)
                pe.wait_ge(M.table, 1)
                n = pe.value_load(table[0:1, 0, TABLE - 1:TABLE], min_val=E - 2, max_val=ITEMS_MAX - 2) + 2
                gate_up(0, lambda j: pe.wait_ge(M.lo, j + 1), DN)
                x_transposes(1)
                h_transposes(0)
                round_(1, lambda i: None)
                with pe.Fori(2, n) as i:
                    round_(i, lambda i: pe.wait_ge(M.y_out, 2 * (i - 1)))
                pe.wait_ge(M.y_out, 2 * (n - 1))
                down(n - 1, lambda j: pe.wait_ge(M.lo, ROUND * n + j + 1))

            moe(0, lambda k: pe.wait_ge(s.ev_dve, HALVES * S_EVD + k + 1))

            pe.sem_inc(q.used, RING)
            with pe.Fori(0, HALVES) as hf:
                pe.wait_ge(q.ev_act, BANKS + hf * BANKS)
                transposes(4 + hf, 0, lambda k: None)
                for kc in range(KC):
                    pe.wait_ge(q.lo, RING + hf * PV + kc + 1)
                    channels_by_tokens(kc % RING, kc, q.used, q.full,
                                       lambda c: pe.wait_ge(g.t_lo, (4 + hf) * KC + c + 1))
            for hf in range(HALVES):
                base = HALVES * PV + hf * (PG + PO)
                for r in range(PG):
                    pe.wait_ge(q.lo, RING + base + r + 1)
                    for c in range(4):
                        b, grp, o = 4 * r + c, c // 2, c % 2
                        pe.wait_ge(q.d_lo, hf * KC + 4 * r + 2 * grp + 2)
                        if hf == 0:
                            pe.wait_ge(q.ev_act, BANKS + HALVES * BANKS)
                        else:
                            pe.wait_ge(q.ev_dve, (hf - 1) * BANKS + b + 1)
                        for k in range(2):
                            w = slice((2 * grp + k) * 256 + o * P, (2 * grp + k) * 256 + (o + 1) * P)
                            a = 4 * r + 2 * grp + k
                            last = three(bank[b][:, :], w_hi[:, (base + r) % RING, w], w_lo[:, (base + r) % RING, w],
                                         a_hi[:, a, :], a_lo[:, a, :], k == 0, k == 1)
                        if c < 3:
                            last.then_inc(q.full, 1)
                    last.then_inc(q.used, 1)
                for kc in range(KC):
                    u = base + PG + kc
                    pe.wait_ge(q.lo, RING + u + 1)
                    pe.wait_ge(q.y_lo, hf * KC + kc + 1)
                    tokens_by_channels(u % RING, y_hi[:, kc % 2, :], y_lo[:, kc % 2, :], kc == 0, kc == KC - 1,
                                       q.used, q.full, lambda b: pe.wait_ge(q.g_out, hf * BANKS + b + 1))
            moe(1, lambda k: pe.wait_ge(q.ev_dve, BANKS + k + 1))

        Q_V = HALVES * BF
        Q_HALF = 6 + BF

        @block.scalar
        def _(act):
            def copy(dst, src):
                return nc.scalar.activation(dst, src, ACT.Copy)

            def split(M, slot_raw, slot, src, loads, used):
                act.wait_ge(M.raw[slot_raw], 16 * loads)
                act.wait_ge(M.used, used)
                copy(w_hi[:, slot, :], src).then_inc(M.hi, 1)

            def norm(n, h, base, wait_x):
                for t in range(HT + 1):
                    if t < HT:
                        wait_x(t)
                        nc.scalar.activation(hn[h][:, t, :], x_res[:, bass.ds(base + t, 1), :].rearrange("p o d -> p (o d)"),
                                             ACT.Square, accum_out=ss[:, t:t + 1]).then_inc(g.sq, 1)
                    if t:
                        act.wait_ge(g.var, n * HT + t)
                        nc.scalar.activation(std[:, t - 1:t], var[:, t - 1:t], ACT.Sqrt).then_inc(g.std, 1)

            def transposed(n):
                for k in range(KC):
                    act.wait_ge(g.t_full, n * KC + k + 1)
                    copy(a_hi[:, k, :], bank[k][:, :]).then_inc(g.t_hi, 1)

            act.sem_inc(s.ev_act, BANKS)
            norm(0, 0, 0, lambda t: act.wait_ge(g.x_loaded[t], 16))
            with act.Fori(0, HALVES) as hf:
                transposed(hf)

                def unit(u):
                    split(s, u % RING, u % RING, raw[:, u % RING, :],
                          hf * (SU // RING) + u // RING + 1, hf * SU + u + 1)

                def wait_full(first_full, b, last_unit):
                    if b < BF:
                        act.wait_ge(s.full, hf * S_FULL + first_full + b + 1)
                    else:
                        act.wait_ge(s.used, RING + hf * SU + last_unit)

                def v_tiles(c4):
                    for b in range(BANKS):
                        act.wait_ge(s.ev_dve, BANKS + hf * S_EVD + c4 * BANKS + b + 1)
                        col = slice(c4 * 1024 + b % 2 * 512, c4 * 1024 + b % 2 * 512 + 512)
                        nc.scalar.activation(v_all[:, b // 2, col], v_all[:, b // 2, col], ACT.Gelu).then_inc(s.v_gelu, 1)
                        act.wait_ge(s.v_gelu, hf * 2 * BANKS + c4 * BANKS + b + 1)
                        nc.scalar.activation(y_hi[:, 0, :], v_all[:, b // 2, col], ACT.Square,
                                             accum_out=v_ss[:, b // 2, 2 * c4 + b % 2:2 * c4 + b % 2 + 1]) \
                            .then_inc(s.v_sq, 1)
                def u_banks(c4):
                    for b in range(BANKS):
                        wait_full((2 + c4) * BF, b, (3 + c4) * KC)
                        c = c4 * BANKS + b
                        nc.scalar.activation(u_all[:, c, :], bank[b][:, :], ACT.Gelu,
                                             bias=cols[:, c:c + 1]).then_inc(s.ev_act, 1)
                for c4 in range(5):
                    for kc in range(3):
                        unit(c4 * KC + kc)
                    if c4 in (1, 2):
                        v_tiles(c4 - 1)
                    if c4 in (3, 4):
                        act.wait_ge(g.small, 16 * 8)
                        act.wait_ge(g.lists_ready, 16 * LAYERS)
                        u_banks(c4 - 3)
                    if c4 < 4:
                        for kc in range(3, KC):
                            unit(c4 * KC + kc)
                    if c4 == 2:
                        act.wait_ge(s.v_var, hf + 1)
                        nc.scalar.activation(std, var, ACT.Sqrt).then_inc(s.v_std, 1)
                for kc in range(SGU // P):
                    act.wait_ge(s.ev_dve, BANKS + hf * S_EVD + 2 * BANKS + kc + 1)
                    if kc >= 2:
                        act.wait_ge(s.used, RING + hf * SU + 4 * KC + kc - 1)
                    copy(y_hi[:, kc % 2, :], u_all[:, kc, :]).then_inc(s.y_hi, 1)
                    if kc + 3 < SGU // P:
                        unit(4 * KC + kc + 3)
                act.wait_ge(s.ev_dve, BANKS + hf * S_EVD)
                norm(hf + 1, 0, HT - hf * HT, lambda t: act.wait_ge(g.x_loaded[t], 32))

            def moe(L, wait_x):
                M, n0 = m[L], 4 * L + 2
                wait_x()
                act.wait_ge(M.small, 32)
                copy(y_hi[:, :, :].rearrange("p a c -> p (a c)"), spatial[:, :]).then_inc(M.rw_hi, 1)
                for h in range(HALVES):
                    transposed(n0 + h)
                    if h == 0:
                        norm(n0 + 1, 1, HT, lambda t: None)
                    act.wait_ge(M.logits, 2 * h + 1)
                    nc.scalar.activation(lt, bank[0][:, :], ACT.Identity, bias=rb).then_inc(M.biased, 1)
                for h in range(HALVES):
                    half = slice(h * HT, (h + 1) * HT)
                    act.wait_ge(M.g_shifted, h + 1)
                    nc.scalar.activation(r_gexp[:, half, :], r_gexp[:, half, :], ACT.Exp).then_inc(M.exps, 1)
                    act.wait_ge(M.e_shifted, h + 1)
                    nc.scalar.activation(r_eexp[:, half, :], r_ediff[:, half, :], ACT.Exp).then_inc(M.exps, 1)

                def unit(c, loads, used, gap=0):
                    act.wait_ge(M.raw[c], 16 * loads)
                    if used is not None:
                        act.wait_ge(M.used, used)
                    copy(w_hi[:, c % RING, :], moe_raw[c]).then_inc(M.hi, 1 + gap)

                def x_split(i):
                    act.wait_ge(M.x_full, i + 1)
                    for b in range(2):
                        copy(x_hi[:, 4 * b:4 * b + 4, :].rearrange("p k t -> p (k t)"), bank[4 + b][:, :]) \
                            .then_inc(M.x_hi, 1)

                def silu(i):
                    act.wait_ge(M.used, ROUND * i + DN)
                    nc.scalar.activation(silu_g, bank[0][:, :], ACT.Silu).then_inc(M.silu, 1)

                def h_split(i):
                    act.wait_ge(M.h_full, i + 1)
                    copy(h_hi.rearrange("p k t -> p (k t)"), bank[6][:, :]).then_inc(M.h_hi, 1)

                def y_out(i, used):
                    act.wait_ge(M.used, used)
                    act.wait_ge(M.meta_s, 16 * (i + 1))
                    for c in range(2):
                        nc.scalar.activation(y_sb[:, c, :], bank[2 + c][:, :], ACT.Copy,
                                             scale=meta_s[:, 2:3].bitcast(F32)).then_inc(M.y_out, 1)

                def round_(i, with_y):
                    for c in range(4):
                        unit(c, i + 1, ROUND * i + c - 3)
                    if with_y:
                        y_out(i - 2, ROUND * i)
                    h_split(i - 1)
                    for c in range(4, GU):
                        unit(c, i + 1, ROUND * i + c - 3)
                    silu(i)
                    for c in range(GU, ROUND):
                        unit(c, i, ROUND * i + c - 3)
                    x_split(i + 1)

                for c in range(GU):
                    if c == RING:
                        x_split(0)
                    unit(c, 1, c - 3 if c >= RING else None, DN if c == GU - 1 else 0)
                silu(0)
                x_split(1)
                act.wait_ge(M.table, 1)
                n = act.value_load(table[0:1, 0, TABLE - 1:TABLE], min_val=E - 2, max_val=ITEMS_MAX - 2) + 2
                round_(1, False)
                with act.Fori(2, n) as i:
                    round_(i, True)
                for c in range(DN):
                    unit(GU + c, n, ROUND * (n - 1) + GU + c + 1)
                y_out(n - 2, ROUND * n)
                h_split(n - 1)
                y_out(n - 1, ROUND * n + DN)

            moe(0, lambda: act.wait_ge(s.ev_dve, BANKS + HALVES * S_EVD))

            act.sem_inc(q.ev_act, BANKS)
            norm(4, 0, 0, lambda t: act.wait_ge(m[0].added, t + 1))
            for hf in range(HALVES):
                transposed(4 + hf)
                for u in range(hf * PV, (hf + 1) * PV):
                    split(q, u % RING, u % RING, raw[:, u % RING, :], u // RING + 1, u + 1)
                if hf == 0:
                    norm(5, 0, HT, lambda t: act.wait_ge(m[0].added, HT + t + 1))
                for c in range(BANKS):
                    if c < BF:
                        act.wait_ge(q.full, hf * BF + c + 1)
                    else:
                        act.wait_ge(q.used, RING + hf * PV + PV)
                    copy(pooled[:, c, hf * HTOK:(hf + 1) * HTOK], bank[c][:, :]).then_inc(q.ev_act, 1)

            def d_split(hf, c):
                act.wait_ge(q.d_ready, c + 1)
                copy(a_hi[:, c, :], pooled[:, c, hf * HTOK:(hf + 1) * HTOK]).then_inc(q.d_hi, 1)

            act.wait_ge(q.zeroed, 4)
            act.wait_ge(q.ev_act, BANKS + HALVES * BANKS)
            for c in range(KC):
                if c >= 2:
                    act.wait_ge(q.d_ready, c - 1)
                copy(padded[c % 2][:, PAD:PAD + SEQ], pooled[:, c, :]).then_inc(q.padded, 1)
                if c:
                    d_split(0, c - 1)
            d_split(0, KC - 1)
            for hf in range(HALVES):
                base = HALVES * PV + hf * (PG + PO)

                def unit(u):
                    split(q, u % RING, u % RING, raw[:, u % RING, :], u // RING + 1, u + 1)
                for r in range(3):
                    unit(base + r)
                for b in range(BANKS):
                    if b % 4 < 3:
                        act.wait_ge(q.full, Q_V + hf * Q_HALF + b // 4 * 3 + b % 4 + 1)
                    else:
                        act.wait_ge(q.used, RING + base + b // 4 + 1)
                    if hf:
                        act.wait_ge(q.y_lo, hf * KC)
                    nc.scalar.activation(y_f32[:, b, :], bank[b][:, :], ACT.Copy, scale=cols[:, 32 + b:33 + b]) \
                        .then_inc(q.g_out, 1)
                for kc in range(KC):
                    act.wait_ge(q.g_out, hf * BANKS + kc + 1)
                    if kc >= 2:
                        act.wait_ge(q.used, RING + base + PG + kc - 1)
                    elif hf:
                        act.wait_ge(q.used, RING + base)
                    copy(y_hi[:, kc % 2, :], y_f32[:, kc, :]).then_inc(q.y_hi, 1)
                    if kc + 3 < PG + PO:
                        if PG + kc + 1 < PG + PO:
                            unit(base + PG + kc + 1)
                    if hf == 0:
                        act.wait_ge(q.used, RING + base + PG)
                        d_split(1, kc)
            act.wait_ge(q.ev_dve, BANKS)
            norm(6, 0, 0, lambda t: None)

            moe(1, lambda: act.wait_ge(q.ev_dve, HALVES * BANKS))

            for h in range(HALVES):
                norm(8 + h, h, h * HT, lambda t: act.wait_ge(m[1].added, h * HT + t + 1))

        @block.vector
        def _(dve):
            def lo_of(dst, src, hi):
                return nc.vector.tensor_tensor(dst, src, f32(hi), ALU.subtract)

            def norm(n, h, base, add):
                def mean_square(t):
                    dve.wait_ge(g.sq, HT * n + t + 1)
                    nc.vector.tensor_scalar(var[:, t:t + 1], ss[:, t:t + 1], 1.0 / D, EPS, ALU.mult, ALU.add) \
                        .then_inc(g.var, 1)
                add(0)
                add(1)
                mean_square(0)
                for t in range(HT):
                    if t + 1 < HT:
                        mean_square(t + 1)
                    x = x_res[:, bass.ds(base + t, 1), :].rearrange("p o d -> p (o d)")
                    dve.wait_ge(g.std, HT * n + t + 1)
                    nc.vector.reciprocal(rstd[:, t:t + 1], std[:, t:t + 1]).then_inc(g.rstd, 1)
                    dve.wait_ge(g.rstd, HT * n + t + 1)
                    nc.vector.scalar_tensor_tensor(hn[h][:, t, :], x, rstd[:, t:t + 1], gain[:, :], ALU.mult, ALU.mult) \
                        .then_inc(g.hn, 1)
                    if t + 2 < HT:
                        add(t + 2)

            def nothing(t):
                pass

            def transposed(n):
                for k in range(KC):
                    dve.wait_ge(g.t_hi, n * KC + k + 1)
                    lo_of(a_lo[:, k, :], bank[k][:, :], a_hi[:, k, :]).then_inc(g.t_lo, 1)

            dve.wait_ge(g.consts, 16)
            nc.vector.tensor_copy(tri[:, :], cf[:, C_TRI:C_TRI + P]).then_inc(g.cast, 1)
            dve.sem_inc(s.ev_dve, BANKS)
            dve.wait_ge(g.gain_ready, 16)
            norm(0, 0, 0, nothing)
            dve.wait_ge(g.small, 16 * 8)
            with dve.Fori(0, HALVES) as hf:
                transposed(hf)

                def unit(u):
                    dve.wait_ge(s.hi, hf * SU + u + 1)
                    lo_of(w_lo[:, u % RING, :], raw[:, u % RING, :], w_hi[:, u % RING, :]).then_inc(s.lo, 1)

                def wait_full(first_full, b, last_unit):
                    if b < BF:
                        dve.wait_ge(s.full, hf * S_FULL + first_full + b + 1)
                    else:
                        dve.wait_ge(s.used, RING + hf * SU + last_unit)

                def v_banks(c4):
                    for b in range(BANKS):
                        wait_full(c4 * BF, b, (1 + c4) * KC)
                        col = slice(c4 * 1024 + b % 2 * 512, c4 * 1024 + b % 2 * 512 + 512)
                        nc.vector.tensor_tensor(v_all[:, b // 2, col], bank[b][:, :], vbias[:, col], ALU.add) \
                            .then_inc(s.ev_dve, 1)

                for c4 in range(5):
                    for kc in range(3):
                        unit(c4 * KC + kc)
                    if c4 in (1, 2):
                        v_banks(c4 - 1)
                    if c4 < 4:
                        for kc in range(3, KC):
                            unit(c4 * KC + kc)
                    if c4 == 2:
                        dve.wait_ge(s.v_sq, (hf + 1) * 2 * BANKS)
                        nc.vector.tensor_reduce(ss, v_ss, AX.X, ALU.add).then_inc(s.v_chain, 1)
                        dve.wait_ge(s.v_chain, 2 * hf + 1)
                        nc.vector.tensor_scalar(var, ss, 1.0 / SGU, EPS, ALU.mult, ALU.add).then_inc(s.v_var, 1)
                        dve.wait_ge(s.v_std, hf + 1)
                        nc.vector.reciprocal(rstd, std).then_inc(s.v_chain, 1)
                        dve.wait_ge(s.v_chain, 2 * hf + 2)
                        for t in range(HT):
                            nc.vector.tensor_scalar(v_all[:, t, :], v_all[:, t, :], rstd[:, t:t + 1], None, ALU.mult) \
                                .then_inc(s.v_scaled, 1)

                def y_split(kc):
                    dve.wait_ge(s.y_hi, hf * (SGU // P) + kc + 1)
                    lo_of(y_lo[:, kc % 2, :], u_all[:, kc, :], y_hi[:, kc % 2, :]).then_inc(s.y_lo, 1)

                for c in range(SGU // P):
                    dve.wait_ge(s.full, hf * S_FULL + 4 * BF + c + 1)
                    sv = bank[c % BANKS][:, :].rearrange("p (t s) -> p t s", s=P)
                    head = c * P * HEADS // SGU
                    nc.vector.scalar_tensor_tensor(sv, sv, cols[:, 16 + c:17 + c],
                                                   b_s[:, head:head + 1, :].to_broadcast([P, HT, P]),
                                                   ALU.mult, ALU.add).then_inc(s.gated, 1)
                    dve.wait_ge(s.gated, hf * (SGU // P) + c + 1)
                    nc.vector.tensor_tensor(u_all[:, c, :], bank[c % BANKS][:, :], u_all[:, c, :], ALU.mult) \
                        .then_inc(s.ev_dve, 1)
                    if c == BANKS:
                        y_split(0)
                        unit(4 * KC + 3)
                    if c == BANKS + 2:
                        y_split(1)
                unit(4 * KC + 4)
                for kc in range(2, SGU // P):
                    y_split(kc)
                    if kc + 3 < SGU // P:
                        unit(4 * KC + kc + 3)
                dve.wait_ge(g.gain_ready, 16 * (hf + 1))
                norm(hf + 1, 0, HT - hf * HT, nothing)
                for b in range(BANKS):
                    wait_full(4 * BF + SGU // P, b, SU)
                    x = x_res[:, bass.ds(hf * HT + b // 2, 1), b % 2 * 512:b % 2 * 512 + 512].rearrange("p o d -> p (o d)")
                    nc.vector.tensor_tensor(x, bank[b][:, :], x, ALU.add).then_inc(s.ev_dve, 1)
                dve.wait_ge(s.ev_dve, BANKS + (hf + 1) * S_EVD)

            def moe(L):
                M, n0 = m[L], 4 * L + 2
                dve.wait_ge(M.rw_hi, 1)
                lo_of(y_lo[:, :, :].rearrange("p a c -> p (a c)"), spatial[:, :],
                      y_hi[:, :, :].rearrange("p a c -> p (a c)")).then_inc(M.rw_lo, 1)

                steps = [0]

                def step(ins):
                    steps[0] += 1
                    ins.then_inc(M.chain, 1)
                    dve.wait_ge(M.chain, steps[0])

                def tt(dst, a, b, op):
                    return nc.vector.tensor_tensor(dst, a, b, op)

                def logits(h):
                    dve.wait_ge(M.logits, 2 * h + 2)
                    nc.vector.tensor_copy(lg[:, h * HT:(h + 1) * HT, :],
                                          bank[1][:, :].rearrange("p (t c) -> p t c", c=P)[:, :, 0:36]) \
                        .then_inc(M.logits_read, 1)

                def choose(h):
                    ts, c3 = slice(h * HT, (h + 1) * HT), [P, HT, E]
                    tiles = range(h * HT, (h + 1) * HT)
                    dve.wait_ge(M.logits_read, h + 1)
                    step(nc.vector.tensor_copy(r_gpad[:, ts, 0:GROUPS], lg[:, ts, 0:GROUPS]))
                    for t in tiles:
                        last = nc.vector.max(r_gmax[:, t, :], r_gpad[:, t, :])
                    step(last)
                    tt(r_gexp[:, ts, :], lg[:, ts, 0:GROUPS], r_gmax[:, ts, 0:1].to_broadcast([P, HT, GROUPS]), ALU.subtract) \
                        .then_inc(M.g_shifted, 1)
                    for t in tiles:
                        last = nc.vector.max_index(r_gidx[:, t, :], r_gmax[:, t, :], r_gpad[:, t, :])
                    step(last)
                    step(nc.vector.tensor_copy(r_grp[:, ts, :], r_gidx[:, ts, 0:1]))
                    step(tt(r_mask[:, ts, :], const3(C_GRP, E, HT), r_grp[:, ts, :].to_broadcast(c3), ALU.is_equal))
                    tt(r_el[:, ts, :], r_mask[:, ts, :], lg[:, ts, GROUPS:36], ALU.mult)
                    step(nc.vector.tensor_scalar(r_mask[:, ts, :], r_mask[:, ts, :], BIG, -BIG, ALU.mult, ALU.add))
                    step(tt(r_el[:, ts, :], r_el[:, ts, :], r_mask[:, ts, :], ALU.add))
                    for t in tiles:
                        last = nc.vector.max(r_emax[:, t, :], r_el[:, t, :])
                    step(last)
                    tt(r_ediff[:, ts, :], r_emax[:, ts, 1:2], r_emax[:, ts, 0:1], ALU.subtract).then_inc(M.e_shifted, 1)
                    for t in tiles:
                        last = nc.vector.max_index(r_eidx[:, t, :], r_emax[:, t, :], r_el[:, t, :])
                    step(last)
                    step(nc.vector.tensor_copy(r_e[:, ts, :], r_eidx[:, ts, 0:2]))
                    for k in range(2):
                        last = tt(r_oh[k][:, ts, :], const3(C_E, E, HT), r_e[:, ts, k:k + 1].to_broadcast(c3), ALU.is_equal)
                    step(last)
                    tt(chosen[:, ts, :], r_oh[0][:, ts, :], r_oh[1][:, ts, :], ALU.add).then_inc(M.chosen, 1)
                    dve.wait_ge(M.exps, 2 * h + 1)
                    nc.vector.tensor_reduce(r_gsum[:, ts, :], r_gexp[:, ts, :], AX.X, ALU.add)
                    dve.wait_ge(M.exps, 2 * h + 2)
                    step(nc.vector.tensor_scalar(r_den[:, ts, :], r_eexp[:, ts, :], 1.0, None, ALU.add))
                    nc.vector.reciprocal(r_gw[:, ts, :], r_gsum[:, ts, :])
                    step(nc.vector.reciprocal(r_rden[:, ts, :], r_den[:, ts, :]))
                    step(tt(r_w[:, ts, 0:1], r_gw[:, ts, :], r_rden[:, ts, :], ALU.mult))
                    step(tt(r_w[:, ts, 1:2], r_w[:, ts, 0:1], r_eexp[:, ts, :], ALU.mult))
                    step(nc.vector.tensor_copy(payload[:, ts, :, 2:3].bitcast(F32).rearrange("p t k w -> p t (k w)"),
                                               r_w[:, ts, :]))

                def places(h):
                    ts = slice(h * HT, (h + 1) * HT)
                    dve.wait_ge(M.ranked, h + 1)
                    step(tt(r_pos[:, ts, :], bank[2 + h][:, 0:HT * E].rearrange("p (t e) -> p t e", e=E),
                            const3(C_BASE, E, HT), ALU.add))
                    for k in range(2):
                        last = tt(r_oh[k][:, ts, :], r_oh[k][:, ts, :], r_pos[:, ts, :], ALU.mult)
                    step(last)
                    for k in range(2):
                        last = nc.vector.tensor_reduce(r_place[:, ts, k:k + 1], r_oh[k][:, ts, :], AX.X, ALU.add)
                    step(last)
                    nc.vector.tensor_copy(place[:, ts, :], r_place[:, ts, :]).then_inc(M.placed, 1)

                transposed(n0)
                step(nc.vector.memset(r_gpad, -BIG))
                norm(n0 + 1, 1, HT, nothing)
                logits(0)
                transposed(n0 + 1)
                choose(0)
                logits(1)
                places(0)
                choose(1)
                places(1)
                dve.wait_ge(M.ranked, 3)

                step(nc.vector.memset(sbias[0:1, 0:12 * E], 0.0))
                over = [sbias[0:1, 2 * E * k:2 * E * (k + 1)] for k in range(6)]
                cmp = sbias[0:1, 512:512 + E * (BPE - 1)].rearrange("p (e b) -> p e b", b=BPE - 1)
                thr = cf[0:1, C_THR:C_THR + BPE - 1].rearrange("p (o b) -> p o b", o=1)
                step(tt(cmp, bank[7][0:1, 0:E].rearrange("p (e o) -> p e o", o=1).to_broadcast([1, E, BPE - 1]),
                        thr.to_broadcast([1, E, BPE - 1]), ALU.is_gt))
                step(nc.vector.tensor_reduce(over[0][:, E:2 * E], cmp, AX.X, ALU.add))
                for k in range(5):
                    step(tt(over[k + 1][:, E:2 * E], over[k][:, E:2 * E], over[k][:, E - 2 ** k:2 * E - 2 ** k], ALU.add))
                incl, excl, row = over[5][:, E:2 * E], sbias[0:1, 768:768 + E], sbias[0:1, 800:800 + E]
                step(tt(excl, incl, over[0][:, E:2 * E], ALU.subtract))
                step(tt(row, cf[0:1, C_E8:C_E8 + E], excl, ALU.subtract))
                ind, tmp = [vbias[0:1, 512 * k:512 * (k + 1)].rearrange("p (j e) -> p j e", e=E) for k in (0, 1)]

                def by_e(ap):
                    return ap.rearrange("p (o e) -> p o e", o=1).to_broadcast([1, EXTRA, E])
                by_j = cf[0:1, C_J:C_J + EXTRA].rearrange("p (j o) -> p j o", o=1).to_broadcast([1, EXTRA, E])
                step(tt(ind, by_e(excl), by_j, ALU.is_le))
                step(tt(tmp, by_e(incl), by_j, ALU.is_gt))
                step(tt(ind, ind, tmp, ALU.mult))
                step(tt(tmp, ind, by_e(cf[0:1, C_E:C_E + E]), ALU.mult))
                step(nc.vector.tensor_reduce(sbias[0:1, 832:832 + EXTRA], tmp, AX.X, ALU.add))
                step(tt(tmp, by_e(row), by_j, ALU.add))
                step(tt(tmp, tmp, ind, ALU.mult))
                step(nc.vector.tensor_reduce(sbias[0:1, 848:848 + EXTRA], tmp, AX.X, ALU.add))
                step(nc.vector.tensor_copy(table[0:1, 0, E:E + EXTRA], sbias[0:1, 832:832 + EXTRA]))
                step(nc.vector.tensor_copy(table[0:1, 1, E:E + EXTRA], sbias[0:1, 848:848 + EXTRA]))
                nc.vector.tensor_scalar(table[0:1, 0, TABLE - 1:TABLE], incl[:, E - 1:E], float(E - 2), None, ALU.add) \
                    .then_inc(M.table, 1)

                def unit(c, hi):
                    dve.wait_ge(M.hi, hi)
                    return lo_of(w_lo[:, c % RING, :], moe_raw[c], w_hi[:, c % RING, :])

                def x_split(i):
                    for b in range(2):
                        dve.wait_ge(M.x_hi, 2 * i + b + 1)
                        lo_of(x_lo[:, 4 * b:4 * b + 4, :].rearrange("p k t -> p (k t)"), bank[4 + b][:, :],
                              x_hi[:, 4 * b:4 * b + 4, :].rearrange("p k t -> p (k t)")).then_inc(M.x_lo, 1)

                def hidden(i):
                    dve.wait_ge(M.silu, i + 1)
                    dve.wait_ge(M.used, ROUND * i + GU)
                    if not isinstance(i, int) or i:
                        dve.wait_ge(M.h_full, i)
                    nc.vector.tensor_tensor(hid, bank[1][:, :], silu_g, ALU.mult).then_inc(M.hid, 1)

                def h_split(i):
                    dve.wait_ge(M.h_hi, i + 1)
                    lo_of(h_lo.rearrange("p k t -> p (k t)"), bank[6][:, :],
                          h_hi.rearrange("p k t -> p (k t)")).then_inc(M.h_lo, 1)

                def round_(i):
                    for c in range(4):
                        unit(c, ROUND * i + c + 1).then_inc(M.lo, 1)
                    h_split(i - 1)
                    for c in range(4, ROUND):
                        unit(c, ROUND * i + c + 1).then_inc(M.lo, 1)
                    hidden(i)
                    x_split(i + 1)

                for c in range(GU):
                    if c == RING:
                        x_split(0)
                    unit(c, c + 1).then_inc(M.lo, 1 + (DN if c == GU - 1 else 0))
                hidden(0)
                x_split(1)
                dve.wait_ge(M.table, 1)
                n = dve.value_load(table[0:1, 0, TABLE - 1:TABLE], min_val=E - 2, max_val=ITEMS_MAX - 2) + 2
                round_(1)
                with dve.Fori(2, n) as i:
                    round_(i)
                for c in range(DN):
                    unit(GU + c, ROUND * n + c + 1).then_inc(M.lo, 1)
                h_split(n - 1)

            def add(L, t):
                M = m[L]
                dve.wait_ge(g.comb[t % COMBS], 16 * ((L * TT + t) // COMBS + 1))
                nc.vector.tensor_tensor(x_res[:, t, :], x_res[:, t, :], comb[t % COMBS][:, 0, :], ALU.add).then_inc(M.summed, 1)
                dve.wait_ge(M.summed, t + 1)
                nc.vector.tensor_tensor(x_res[:, t, :], x_res[:, t, :], comb[t % COMBS][:, 1, :], ALU.add).then_inc(M.added, 1)

            moe(0)

            dve.wait_ge(g.gain_ready, 16 * 3)
            norm(4, 0, 0, lambda t: add(0, t))
            for hf in range(HALVES):
                transposed(4 + hf)
                for u in range(hf * PV, (hf + 1) * PV):
                    dve.wait_ge(q.hi, u + 1)
                    lo_of(w_lo[:, u % RING, :], raw[:, u % RING, :], w_hi[:, u % RING, :]).then_inc(q.lo, 1)
                if hf == 0:
                    norm(5, 0, HT, lambda t: add(0, HT + t))
            dve.wait_ge(g.t_full, 6 * KC)
            for n in range(2):
                nc.vector.memset(padded[n][:, 0:PAD], 0.0).then_inc(q.zeroed, 1)
                nc.vector.memset(padded[n][:, PAD + SEQ:], 0.0).then_inc(q.zeroed, 1)
            steps = [0]

            def step(ins):
                steps[0] += 1
                ins.then_inc(q.chain, 1)
                dve.wait_ge(q.chain, steps[0])

            def d_split(hf, c):
                dve.wait_ge(q.d_hi, hf * KC + c + 1)
                lo_of(a_lo[:, c, :], pooled[:, c, hf * HTOK:(hf + 1) * HTOK], a_hi[:, c, :]).then_inc(q.d_lo, 1)

            for c in range(KC):
                w = WINDOWS[c * P * len(WINDOWS) // D]
                dve.wait_ge(q.padded, c + 1)
                v = padded[c % 2]
                cur, lo, hi, width, other = v, 0, SEQ + 2 * PAD, 1, 0
                while width < w:
                    back, ahead = (1, 0) if width == 1 else (width // 2, width // 2)
                    nxt = sums[other]
                    step(nc.vector.tensor_tensor(nxt[:, lo + back:hi - ahead], cur[:, lo:hi - ahead - back],
                                                 cur[:, lo + ahead + back:hi], ALU.add))
                    cur, lo, hi, width, other = nxt, lo + back, hi - ahead, 2 * width, 1 - other
                h = w // 2
                edges = [(0, h, C_ASC + h)] + ([(SEQ - h + 1, h - 1, C_DESC + 16 - (w - 1))] if h > 1 else [])
                scaled = sums[other][:, 0:2 * PAD]
                for n, (at, size, cc) in enumerate(edges):
                    step(nc.vector.tensor_tensor(scaled[:, n * PAD:n * PAD + size], cur[:, PAD + at:PAD + at + size],
                                                 cf[:, cc:cc + size], ALU.mult))
                step(nc.vector.scalar_tensor_tensor(pooled[:, c, :], cur[:, PAD:PAD + SEQ], 1.0 / w, v[:, PAD:PAD + SEQ],
                                                    ALU.mult, ALU.subtract))
                for n, (at, size, cc) in enumerate(edges):
                    step(nc.vector.tensor_tensor(pooled[:, c, at:at + size], scaled[:, n * PAD:n * PAD + size],
                                                 v[:, PAD + at:PAD + at + size], ALU.subtract))
                dve.sem_inc(q.d_ready, 1)
                if c:
                    d_split(0, c - 1)
            d_split(0, KC - 1)
            for hf in range(HALVES):
                base = HALVES * PV + hf * (PG + PO)

                def unit(u):
                    dve.wait_ge(q.hi, u + 1)
                    lo_of(w_lo[:, u % RING, :], raw[:, u % RING, :], w_hi[:, u % RING, :]).then_inc(q.lo, 1)
                for r in range(3):
                    unit(base + r)
                for kc in range(KC):
                    dve.wait_ge(q.y_hi, hf * KC + kc + 1)
                    lo_of(y_lo[:, kc % 2, :], y_f32[:, kc, :], y_hi[:, kc % 2, :]).then_inc(q.y_lo, 1)
                    if PG + kc + 1 < PG + PO:
                        unit(base + PG + kc + 1)
                    if hf == 0:
                        d_split(1, kc)
                if hf:
                    dve.wait_ge(g.gain_ready, 16 * 4)
                    norm(6, 0, 0, nothing)
                for b in range(BANKS):
                    if b < BF:
                        dve.wait_ge(q.full, Q_V + hf * Q_HALF + 6 + b + 1)
                    else:
                        dve.wait_ge(q.used, RING + base + PG + PO)
                    x = x_res[:, hf * HT + b // 2, b % 2 * 512:b % 2 * 512 + 512]
                    nc.vector.tensor_tensor(x, bank[b][:, :], x, ALU.add).then_inc(q.ev_dve, 1)
            dve.wait_ge(q.ev_dve, HALVES * BANKS)

            moe(1)

            dve.wait_ge(g.gain_ready, 16 * 5)
            for h in range(HALVES):
                norm(8 + h, h, h * HT, lambda t: add(1, h * HT + t))


_SHAPES = ((1, SEQ, D), "float32")


def kernel(**inputs):
    import numpy as np
    import concourse.bacc as bacc
    from concourse.bass_utils import run_bass_kernel_spmd as run

    def by_partition(a, width):
        return np.ascontiguousarray(a.reshape(width, P).T)

    a = {k: np.ascontiguousarray(inputs[k]) for k in (
        "x", "norm_mix_g", "norm_ffn_g", "final_norm_g", "a_w_in", "a_b_in", "a_w_out", "a_b_spatial",
        "b_w_in", "b_w_group", "b_w_out", "w_gate", "w_up", "w_down")}
    a["w_s"] = np.ascontiguousarray(np.asarray(inputs["a_w_spatial"])[0].transpose(2, 0, 1).reshape(P, HEADS * P))
    a["u_bias"] = by_partition(np.asarray(inputs["a_b_in"])[0, :SGU], SGU // P)
    a["v_gain"] = by_partition(np.asarray(inputs["a_norm_v"])[0], SGU // P)
    a["pool_scale"] = by_partition(np.asarray(inputs["b_scale"])[0], KC)
    rw = np.concatenate([np.asarray(inputs["router_group_w"]), np.asarray(inputs["router_expert_w"])], axis=2)
    rw = np.pad(rw, ((0, 0), (0, 0), (0, P - rw.shape[2])))
    a["router_w"] = np.ascontiguousarray(rw.reshape(LAYERS, KC, P, P).transpose(0, 2, 1, 3).reshape(LAYERS, P, KC * P))
    rb = np.concatenate([np.asarray(inputs["router_group_b"]), np.asarray(inputs["router_expert_b"])], axis=1)
    a["router_b"] = np.ascontiguousarray(np.pad(rb, ((0, 0), (0, P - rb.shape[1])))[:, :, None])

    c = np.zeros((P, C_ALL), np.float32)
    c[:, C_ID:C_ID + P] = np.eye(P)
    c[:, C_TRI:C_TRI + P] = np.triu(np.ones((P, P)), 1)
    c[:, C_E:C_E + E] = np.arange(E)
    c[:, C_GRP:C_GRP + E] = np.arange(E) // EPG
    c[:, C_BASE:C_BASE + E] = np.arange(E) * LISTED
    c[:, C_ASC + 1:C_ASC + 16] = 1.0 / np.arange(1, 16)
    c[:, C_DESC:C_DESC + 16] = 1.0 / (16 - np.arange(16))
    c[:, C_THR:C_THR + BPE - 1] = BLK * np.arange(1, BPE)
    c[:, C_J:C_J + EXTRA] = np.arange(EXTRA)
    c[:, C_E8:C_E8 + E] = BPE * np.arange(E) + 1
    a["c_float"] = c
    tok = np.arange(TT)[None, :] * P + np.arange(P)[:, None]
    pay = np.zeros((P, TT, 2, 4), np.int32)
    pay[..., 0] = tok[..., None]
    pay[..., 1] = 2 * tok[..., None] + np.arange(2)
    a["c_payload"] = pay.reshape(P, TT * 8)
    tab = np.zeros((1, 2, TABLE), np.int32)
    tab[0, 0, :E] = np.arange(E)
    tab[0, 1, :E] = np.arange(E) * BPE
    a["c_table"] = tab

    nc = bacc.Bacc("TRN2", target_bir_lowering=False, num_devices=1)
    arrays, aps = {}, {}
    for name, v in a.items():
        arrays[f"in_{name}"] = v
        aps[name] = nc.dram_tensor(f"in_{name}", v.shape, mybir.dt.from_np(v.dtype), kind="ExternalInput").ap()
    out = nc.dram_tensor("out_0", _SHAPES[0], F32, kind="ExternalOutput").ap()
    encoder_trunk(nc, aps, out)
    r = run(nc, [arrays], core_ids=[0])
    return r.results[0]["out_0"]
```

```python
from collections import namedtuple
from contextlib import ExitStack

import concourse.bass as bass
from concourse import mybir

F32, F32R, BF16, I32, U32 = (mybir.dt.float32, mybir.dt.float32r, mybir.dt.bfloat16,
                             mybir.dt.int32, mybir.dt.uint32)
ALU, ACT, AX = mybir.AluOpType, mybir.ActivationFunctionType, mybir.AxisListType

P = 128
D = 1024
SEQ = 1024
TT = SEQ // P
HALVES = 2
HT = TT // HALVES
HTOK = HT * P
KC = D // P
SGU = 2 * D
HEADS = 8
F = D // 2
E = 32
GROUPS = 4
EPG = E // GROUPS
LAYERS = 2
BANKS = 8
RING = 4
UNIT = 1024
GU, DN = 8, 4
ROUND = GU + DN
COMBS = 4
BLK = P
LISTED = SEQ
BPE = LISTED // BLK
EXTRA = 2 * SEQ // BLK
ITEMS_MAX = E + EXTRA - 1
TABLE = 64
EPS = 1e-6
WINDOWS = (2, 4, 8, 16)
PAD = WINDOWS[-1] // 2
BIG = 1e30

C_ID, C_TRI, C_E, C_GRP, C_BASE = 0, P, 2 * P, 2 * P + E, 2 * P + 2 * E
C_ASC = C_BASE + E
C_DESC, C_THR = C_ASC + 16, C_ASC + 32
C_J = C_THR + BPE - 1
C_E8 = C_J + 16
C_ALL = C_E8 + E


def encoder_trunk(nc, A, out):
    ctx = ExitStack()
    with ctx:
        def sb(name, shape, dt):
            return ctx.enter_context(nc.sbuf_tensor(name, shape, dt))

        def sems(phase, names, arrays):
            def one(n):
                return ctx.enter_context(nc.semaphore(f"{phase}_{n}"))
            made = {n: one(n) for n in names} | {n: [one(f"{n}{i}") for i in range(k)] for n, k in arrays.items()}
            return namedtuple("Sems", made)(**made)

        x_res = sb("x_res", [P, TT, D], F32)
        raw = sb("raw", [P, RING, UNIT], F32)
        w_hi = sb("w_hi", [P, RING, UNIT], F32R)
        w_lo = sb("w_lo", [P, RING, UNIT], F32R)
        a_hi = sb("a_hi", [P, KC, HTOK], F32R)
        a_lo = sb("a_lo", [P, KC, HTOK], F32R)
        y_hi = sb("y_hi", [P, 2, HTOK], F32R)
        y_lo = sb("y_lo", [P, 2, HTOK], F32R)
        big = sb("big", [P, 16 * 1024], F32)
        bu = big[:, 0:8 * 1024]
        bv = big[:, 8 * 1024:]
        gain = sb("gain", [P, D], F32)
        spatial = sb("spatial", [P, HEADS * P], F32)
        sbias = sb("sbias", [P, HEADS * P], F32)
        vbias = sb("vbias", [P, SGU], F32)
        cf = sb("cf", [P, C_ALL], F32)
        tri = sb("tri", [P, P], BF16)
        ones = sb("ones", [P, P], BF16)
        chosen = sb("chosen", [P, TT, E], BF16)
        payload = sb("payload", [P, TT, 2, 4], I32)
        place = sb("place", [P, TT, 2], I32)
        table = sb("table", [1, 2, TABLE], I32)
        metas = sb("metas", [P, 8], I32)
        cols = sb("cols", [P, 72], F32)
        bank = [ctx.enter_context(nc.psum_tensor(f"bank{b}", [P, 512], F32)) for b in range(BANKS)]

        def dram(name, shape, dt):
            return nc.dram_tensor(name, shape, dt, kind="Internal").ap()
        normed = [dram(f"normed{n}", (SEQ, D), F32) for n in range(LAYERS)]
        y_rows = [dram(f"y_rows{n}", (2 * SEQ, D), F32) for n in range(LAYERS)]
        lists = [dram(f"lists{n}", (E * LISTED, 4), I32) for n in range(LAYERS)]

        meta_g, meta_s = metas[:, 0:4], metas[:, 4:8]
        ss, var, std, rstd = [cols[:, 40 + 4 * n:44 + 4 * n] for n in range(4)]
        rb = cols[:, 0:1]
        v_ss = cols[:, 56:72].rearrange("p (t c) -> p t c", c=4)
        ident = cf[:, C_ID:C_ID + P]
        hn = [bv[:, h * HT * D:(h + 1) * HT * D].rearrange("p (t d) -> p t d", d=D) for h in range(2)]
        u_all = bu[:, :].rearrange("p (c t) -> p c t", t=HTOK)
        v_all = bv[:, :].rearrange("p (t d) -> p t d", d=SGU)
        w_s = spatial[:, :].rearrange("p (h t) -> p h t", h=HEADS)
        b_s = sbias[:, :].rearrange("p (h t) -> p h t", h=HEADS)
        xg = bv[:, 4096:5120]
        y_sb = bv[:, 5120:6144].rearrange("p (n f) -> p n f", n=2)
        silu_g = bv[:, 6144:6144 + F]
        hid = bv[:, 6144 + F:6144 + 2 * F]
        comb = [bu[:, n * 2048:(n + 1) * 2048].rearrange("p (k d) -> p k d", k=2) for n in range(COMBS)]
        x_hi = a_hi[:, 0:2, :].rearrange("p a (k t) -> p (a k) t", t=P)
        x_lo = a_lo[:, 0:2, :].rearrange("p a (k t) -> p (a k) t", t=P)
        h_hi = a_hi[:, 2, :].rearrange("p (k t) -> p k t", t=P)
        h_lo = a_lo[:, 2, :].rearrange("p (k t) -> p k t", t=P)
        moe_raw = [raw[:, n, :] for n in range(RING)] + \
                  [bu[:, n * UNIT:(n + 1) * UNIT] for n in range(ROUND - RING)]

        early_raw = [bv[:, n * UNIT:(n + 1) * UNIT] for n in (0, 1, 2, 3, 7)] + \
                    [spatial[:, :], vbias[:, 0:UNIT], vbias[:, UNIT:2 * UNIT]]
        early_down = [None] * GU + early_raw[0:DN]

        rw_hi = y_hi[:, :, :].rearrange("p a (k c) -> p (a k) c", c=P)
        rw_lo = y_lo[:, :, :].rearrange("p a (k c) -> p (a k) c", c=P)
        lt = sbias[:, 0:HTOK]
        lg = sbias[:, HTOK:HTOK + TT * 36].rearrange("p (t c) -> p t c", c=36)

        def scratch(at, width, dt=F32):
            v = vbias[:, at:at + TT * width]
            return (v if dt is F32 else v.bitcast(dt)).rearrange("p (t c) -> p t c", c=width)
        r_gpad, r_gmax, r_gidx = scratch(0, 8), scratch(64, 8), scratch(128, 8, U32)
        r_gexp, r_gsum, r_gw, r_grp = scratch(192, GROUPS), scratch(224, 1), scratch(232, 1), scratch(240, 1)
        r_mask, r_el = scratch(256, E), scratch(512, E)
        r_emax, r_eidx, r_e = scratch(768, 8), scratch(832, 8, U32), scratch(896, 2)
        r_ediff, r_eexp, r_den, r_rden = scratch(912, 1), scratch(920, 1), scratch(928, 1), scratch(936, 1)
        r_w, r_place = scratch(944, 2), scratch(960, 2)
        r_oh, r_pos = [scratch(1024, E), scratch(1280, E)], scratch(1536, E)

        def const3(at, width, n):
            return cf[:, at:at + width].rearrange("p (o e) -> p o e", o=1).to_broadcast([P, n, width])
        padded = big[:, 0:KC * (SEQ + 2 * PAD)].rearrange("p (c t) -> p c t", t=SEQ + 2 * PAD)
        SUMS = HTOK + 2 * PAD
        sums = [bv[:, 1024 + n * 2 * SUMS:1024 + (n + 1) * 2 * SUMS].rearrange("p (c t) -> p c t", c=2) for n in range(2)]
        edge = bv[:, 512:512 + 2 * PAD].rearrange("p (c t) -> p c t", c=2)
        y_f32 = bv[:, 4096:8192].rearrange("p (c t) -> p c t", t=HTOK)
        d_first = y_f32
        d_of = [d_first, padded[:, :, PAD + HTOK:PAD + SEQ]]

        def f32(ap):
            return ap.bitcast(F32)

        g = sems("g", ["consts", "cast", "init", "lists_ready", "gain_ready", "small",
                       "sq", "var", "std", "rstd", "waited", "hn", "t_full", "t_hi", "t_lo", "out_stored"],
                 {"x_loaded": HT, "comb": COMBS})
        RINGS = ["hi", "lo", "used"]
        s = sems("sgu", RINGS + ["full", "ev_act", "ev_dve", "v_sq", "v_gelu", "v_chain", "v_var", "v_std",
                                 "v_scaled", "gated", "y_hi", "y_lo"],
                 {"raw": RING})
        q = sems("pool", RINGS + ["full", "ev_act", "ev_dve", "zeroed", "chain", "d_ready", "d_hi",
                                  "d_lo", "g_out", "y_hi", "y_lo"],
                 {"raw": RING})
        MOE = ["hi", "lo", "used", "rw_hi", "rw_lo", "logits", "biased", "logits_read", "chain",
               "exps", "g_shifted", "e_shifted", "chosen", "ranked", "placed", "listed", "table",
               "meta_g", "gathered", "x_full", "x_hi", "x_lo", "silu", "hid",
               "h_full", "h_hi", "h_lo", "y_out", "meta_s", "scattered",
               "added", "small", "summed"]
        m = [sems(f"moe{n}", MOE, {"raw": ROUND, "stored": HALVES}) for n in range(LAYERS)]

        SU = 3 * 2 * KC
        PV, PG, PO = KC, 2, KC

        BF = BANKS - 1
        S_FULL = 2 * BF + 2 * BF + SGU // P + BF
        S_EVD = 2 * BANKS + SGU // P + BANKS
        S_EVA = 2 * BANKS

        block = ctx.enter_context(nc.Block())

        @block.sync
        def _(sp):
            sp.dma_start(cf[:, :], A["c_float"]).then_inc(g.consts, 16)
            xv = A["x"].rearrange("o (t p) d -> p (o t) d", p=P)
            for h in range(HALVES):
                for t in range(HT):
                    if h:
                        sp.wait_ge(g.x_loaded[t], 16)
                    sp.dma_start(x_res[:, h * HT + t, :], xv[:, h * HT + t, :]).then_inc(g.x_loaded[t], 16)
                if h == 0:
                    for kc in range(RING):
                        sp.dma_start(raw[:, kc, :], A["a_w_in"][0, kc * P:(kc + 1) * P, SGU:SGU + UNIT]) \
                            .then_inc(s.raw[kc], 16)
            sp.sem_inc(s.lo, RING)

            def sgu_in(hf, c, col, first):
                for kc in range(first, KC):
                    sp.wait_ge(s.lo, hf * SU + c * KC + kc + 1)
                    sp.dma_start(raw[:, kc % RING, :], A["a_w_in"][0, kc * P:(kc + 1) * P, bass.ds(col, UNIT)]) \
                        .then_inc(s.raw[kc % RING], 16)

            def sgu_half(hf, first):
                sgu_in(hf, 0, SGU, RING if first else 0)
                sgu_in(hf, 1, SGU + UNIT, 0)
                with sp.Fori(0, 2) as c:
                    sgu_in(hf, c + 2, c * UNIT, 0)
                with sp.Fori(0, 2) as o:
                    for kc in range(KC):
                        sp.wait_ge(s.lo, hf * SU + 4 * KC + o * KC + kc + 1)
                        sp.dma_start(raw[:, kc % RING, :], A["a_w_out"][0, bass.ds((o * KC + kc) * P, P), :]) \
                            .then_inc(s.raw[kc % RING], 16)
            sgu_half(0, True)
            sgu_half(1, False)

            def moe(L, before_lo, before_y, next_weights):
                M = m[L]
                gate = A["w_gate"][L].rearrange("e (p k) f -> p e k f", k=KC)
                up = A["w_up"][L].rearrange("e (p k) f -> p e k f", k=KC)
                down = A["w_down"][L].rearrange("e (p k) d -> p e k d", k=DN)

                def load_gu(e, j, slots=moe_raw):
                    w = gate if j < DN else up
                    k = 2 * (j % DN)
                    sp.dma_start(slots[j].rearrange("p (e k f) -> p e k f", e=1, k=2),
                                 w[:, bass.ds(e, 1), k:k + 2, :]).then_inc(M.raw[j], 16)

                def load_dn(e, j, slot=None):
                    sp.dma_start((slot if slot is not None else moe_raw[GU + j]).rearrange("p (e k d) -> p e k d", e=1, k=1),
                                 down[:, bass.ds(e, 1), j:j + 1, :]).then_inc(M.raw[GU + j], 16)

                before_lo(sp)
                for j in range(RING):
                    load_gu(0, j)
                before_y(sp)
                for j in range(RING, GU):
                    load_gu(0, j)
                for j in range(DN):
                    load_dn(0, j)
                for h in range(HALVES):
                    sp.wait_ge(g.hn, HT * (4 * L + 2 + h + 1))
                    sp.dma_start(normed[L].rearrange("(t p) d -> p t d", p=P)[:, h * HT:(h + 1) * HT, :],
                                 hn[h]).then_inc(M.stored[h], 16)
                place_free = {0: lambda: (sp.wait_ge(M.stored[0], 16), sp.wait_ge(M.logits, 1)),
                              4: lambda: (sp.wait_ge(M.stored[1], 16), sp.wait_ge(M.logits, 3)),
                              5: lambda: sp.wait_ge(M.rw_lo, 1),
                              6: lambda: sp.wait_ge(M.table, 1)}

                def item_1(units):
                    for j in units:
                        if j in place_free:
                            place_free[j]()
                        sp.wait_ge(M.raw[j], 16)
                        load_gu(1, j, early_raw)

                def item_2(units):
                    for j in units:
                        sp.wait_ge(M.lo, j + 1)
                        sp.wait_ge(M.raw[j], 32)
                        load_gu(2, j)

                item_1(range(6))
                item_2(range(RING))
                item_1(range(6, GU))
                item_2(range(RING, GU))
                for j in range(DN):
                    sp.wait_ge(M.lo, ROUND + j + 1)
                    sp.wait_ge(M.raw[GU + j], 16)
                    load_dn(1, j, early_raw[j])
                for j in range(DN):
                    sp.wait_ge(M.lo, ROUND + GU + j + 1)
                    sp.wait_ge(M.raw[GU + j], 32)
                    load_dn(2, j)
                for j in range(GU):
                    sp.wait_ge(M.lo, 2 * ROUND + j + 1)
                    load_gu(3, j)
                n = sp.value_load(table[0:1, 0, TABLE - 1:TABLE], min_val=E - 2, max_val=ITEMS_MAX - 2) + 2
                with sp.Fori(4, n) as i:
                    e_up = sp.value_load(table[0:1, 0, bass.ds(i, 1)], min_val=0, max_val=E - 1)
                    e_dn = sp.value_load(table[0:1, 0, bass.ds(i - 1, 1)], min_val=0, max_val=E - 1)
                    for j in range(GU):
                        sp.wait_ge(M.lo, ROUND * (i - 1) + j + 1)
                        load_gu(e_up, j)
                    for j in range(DN):
                        sp.wait_ge(M.lo, ROUND * (i - 1) + GU + j + 1)
                        load_dn(e_dn, j)
                e_dn = sp.value_load(table[0:1, 0, bass.ds(n - 1, 1)], min_val=0, max_val=E - 1)
                for j in range(DN):
                    sp.wait_ge(M.lo, ROUND * (n - 1) + GU + j + 1)
                    load_dn(e_dn, j)
                next_weights()
                sp.wait_ge(M.scattered, 16 * n)
                sp.wait_ge(M.gathered, 16 * (n + 1))
                yv = y_rows[L].rearrange("(t p k) d -> p t k d", p=P, k=2)
                for t in range(TT):
                    if t >= COMBS:
                        sp.wait_ge(M.added, t - COMBS + 1)
                    sp.dma_start(comb[t % COMBS], yv[:, t, :, :]).then_inc(g.comb[t % COMBS], 16)
                return n

            def pool_in(u):
                kc = u % PV
                sp.wait_ge(q.lo, u + 1)
                sp.dma_start(raw[:, u % RING, :], A["b_w_in"][0, kc * P:(kc + 1) * P, :]).then_inc(q.raw[u % RING], 16)

            def pool_first():
                for u in range(RING):
                    pool_in(u)

            sp.sem_inc(q.lo, RING)
            moe(0, lambda e: e.wait_ge(s.lo, RING + 2 * SU), lambda e: e.wait_ge(s.y_lo, 2 * 2 * KC), pool_first)

            for u in range(RING, HALVES * PV):
                pool_in(u)
            wg = A["b_w_group"][0].rearrange("g (k p) f -> p g k f", k=2)

            def pool_out(hf, base):
                for r in range(PG + PO):
                    sp.wait_ge(q.lo, base + r + 1)
                    slot = (base + r) % RING
                    if r < PG:
                        sp.dma_start(raw[:, slot, :].rearrange("p (g k f) -> p g k f", g=2, k=2),
                                     wg[:, 2 * r:2 * r + 2, :, :]).then_inc(q.raw[slot], 16)
                    else:
                        kc = r - PG
                        sp.dma_start(raw[:, slot, :], A["b_w_out"][0, kc * P:(kc + 1) * P, :]) \
                            .then_inc(q.raw[slot], 16)
            for hf in range(HALVES):
                pool_out(hf, HALVES * PV + hf * (PG + PO))
            total = HALVES * (PV + PG + PO)
            moe(1, lambda e: e.wait_ge(q.lo, RING + total), lambda e: e.wait_ge(q.y_lo, HALVES * KC),
                lambda: None)

            ov = out.rearrange("o (t p) d -> p (o t) d", p=P)
            for h in range(HALVES):
                for t in range(HT):
                    sp.wait_ge(g.hn, 4 * (8 + h) + t + 1)
                    sp.dma_start(ov[:, h * HT + t, :], hn[h][:, t, :]).then_inc(g.out_stored, 16)
            sp.wait_ge(g.out_stored, 16 * TT)

        @block.gpsimd
        def _(pool):
            def waited():
                pool.sem_inc(g.waited, 1)

            def load_gain(k, src):
                if k:
                    pool.wait_ge(g.hn, 8 * k)
                pool.dma_start(gain[:, :], src.partition_broadcast(P)).then_inc(g.gain_ready, 16)

            load_gain(0, A["norm_mix_g"][0])
            pool.dma_start(payload[:, :, :, :].rearrange("p t k w -> p (t k w)"), A["c_payload"]).then_inc(g.small, 16)
            pool.dma_start(table[:, :, :], A["c_table"]).then_inc(g.small, 16)
            pool.dma_start(cols[:, 0:16], A["u_bias"]).then_inc(g.small, 16)
            pool.dma_start(cols[:, 16:32], A["v_gain"]).then_inc(g.small, 16)
            pool.dma_start(cols[:, 32:40], A["pool_scale"]).then_inc(g.small, 16)
            pool.dma_start(spatial[:, :], A["w_s"]).then_inc(g.small, 16)
            pool.dma_start(sbias[:, :], A["a_b_spatial"][0].rearrange("h t -> (h t)").partition_broadcast(P)) \
                .then_inc(g.small, 16)
            pool.dma_start(vbias[:, :], A["a_b_in"][0, SGU:2 * SGU].partition_broadcast(P)).then_inc(g.small, 16)
            pool.memset(ones[:, :], 1.0).then_inc(g.init, 1)
            pool.memset(bu[:, 0:1024], 1.0).then_inc(g.init, 1)
            pool.wait_ge(g.init, 2)
            for L in range(LAYERS):
                pool.dma_start(lists[L].rearrange("(p r) w -> p (r w)", p=P), bu[:, 0:1024].bitcast(I32)) \
                    .then_inc(g.lists_ready, 16)
            load_gain(1, A["norm_ffn_g"][0])

            def moe(L):
                M = m[L]
                lst = lists[L].rearrange("(b p) w -> p b w", p=BLK)
                if L == 0:
                    pool.wait_ge(s.ev_dve, BANKS + S_EVD + 2 * BANKS + SGU // P)
                pool.dma_start(spatial[:, :], A["router_w"][L]).then_inc(M.small, 16)
                pool.dma_start(rb, A["router_b"][L]).then_inc(M.small, 16)
                load_gain(2 * L + 2, A["norm_mix_g"][1] if L == 0 else A["final_norm_g"])
                pool.wait_ge(g.lists_ready, 16 * LAYERS)
                for t in range(TT):
                    if t % HT == 0:
                        pool.wait_ge(M.placed, t // HT + 1)
                    for k in range(2):
                        pool.indirect_dma_start(
                            out=lists[L][:, :],
                            out_offset=bass.IndirectOffsetOnAxis(ap=place[:, t, k:k + 1], axis=0),
                            in_=payload[:, t, k, :], in_offset=None).then_inc(M.listed, 16)
                pool.wait_ge(M.listed, 16 * 2 * TT)
                for h in range(HALVES):
                    pool.wait_ge(M.stored[h], 16)
                def block_of(i):
                    if isinstance(i, int):
                        return i * BPE
                    return pool.value_load(table[0:1, 1, bass.ds(i, 1)], min_val=0, max_val=E * BPE - 1)

                def gather(i):
                    b = block_of(i)
                    if not isinstance(i, int) or i > 0:
                        pool.wait_ge(M.x_full, i)
                        waited()
                    pool.dma_start(meta_g, lst[:, bass.ds(b, 1), :].rearrange("p b w -> p (b w)")).then_inc(M.meta_g, 16)
                    pool.wait_ge(M.meta_g, 16 * (i + 1))
                    waited()
                    pool.indirect_dma_start(
                        out=xg, out_offset=None, in_=normed[L][:, :],
                        in_offset=bass.IndirectOffsetOnAxis(ap=meta_g[:, 0:1], axis=0),
                        bounds_check=SEQ - 1, oob_is_err=False).then_inc(M.gathered, 16)

                def load_meta(i):
                    b = block_of(i)
                    pool.dma_start(meta_s, lst[:, bass.ds(b, 1), :].rearrange("p b w -> p (b w)")).then_inc(M.meta_s, 16)

                def scatter(i):
                    pool.wait_ge(M.y_out, 2 * (i + 1))
                    waited()
                    pool.indirect_dma_start(
                        out=y_rows[L][:, :],
                        out_offset=bass.IndirectOffsetOnAxis(ap=meta_s[:, 1:2], axis=0),
                        in_=y_sb.rearrange("p n f -> p (n f)"), in_offset=None,
                        bounds_check=2 * SEQ - 1, oob_is_err=False).then_inc(M.scattered, 16)
                    pool.wait_ge(M.scattered, 16 * (i + 1))
                    waited()

                gather(0)
                load_meta(0)
                gather(1)
                gather(2)
                pool.wait_ge(M.table, 1)
                n = pool.value_load(table[0:1, 0, TABLE - 1:TABLE], min_val=E - 2, max_val=ITEMS_MAX - 2) + 2
                with pool.Fori(2, n) as i:
                    gather(i + 1)
                    scatter(i - 2)
                    load_meta(i - 1)
                scatter(n - 2)
                load_meta(n - 1)
                scatter(n - 1)
                pool.wait_ge(M.gathered, 16 * (n + 1))
                waited()
                for t in range(TT):
                    pool.wait_ge(g.comb[t % COMBS], 16 * ((L * TT + t) // COMBS + 1))
                    two = comb[t % COMBS]
                    pool.tensor_tensor(two[:, 0, :], two[:, 0, :], two[:, 1, :], ALU.add).then_inc(M.summed, 1)

            moe(0)
            load_gain(3, A["norm_ffn_g"][1])
            moe(1)

        @block.tensor
        def _(pe):
            def three(dst, left_hi, left_lo, right_hi, right_lo, first, last):
                pe.matmul(dst, left_hi, right_hi, start=first, stop=False)
                pe.matmul(dst, left_hi, right_lo, start=False, stop=False)
                return pe.matmul(dst, left_lo, right_hi, start=False, stop=last)

            def transposes(n, h, wait_bank, by_chunk):
                for a in range(KC if by_chunk else HT):
                    for b in range(HT if by_chunk else KC):
                        t, k = (b, a) if by_chunk else (a, b)
                        if k == 0:
                            pe.wait_ge(g.hn, HT * n + t + 1)
                        if t == 0:
                            wait_bank(k)
                        last = pe.transpose(bank[k][:, t * P:(t + 1) * P], hn[h][:, t, k * P:(k + 1) * P], ident)
                        if t == HT - 1:
                            last.then_inc(g.t_full, 1)

            def channels_by_tokens(slot, kc, used, full, wait_bank):
                for c in range(BANKS):
                    if kc == 0:
                        wait_bank(c)
                    w = slice(c * P, (c + 1) * P)
                    last = three(bank[c][:, :], w_hi[:, slot, w], w_lo[:, slot, w],
                                 a_hi[:, kc, :], a_lo[:, kc, :], kc == 0, kc == KC - 1)
                    if kc == KC - 1 and c < BF:
                        last.then_inc(full, 1)
                last.then_inc(used, 1)

            def tokens_by_channels(slot, left_hi, left_lo, first, final, used, full, wait_bank):
                for t in range(HT):
                    for c in range(2):
                        if first:
                            wait_bank(2 * t + c)
                        col, row = slice(c * 512, (c + 1) * 512), slice(t * P, (t + 1) * P)
                        last = three(bank[2 * t + c][:, :], left_hi[:, row], left_lo[:, row],
                                     w_hi[:, slot, col], w_lo[:, slot, col], first, final)
                        if final and 2 * t + c < BF:
                            last.then_inc(full, 1)
                last.then_inc(used, 1)

            pe.wait_ge(g.consts, 16)

            pe.sem_inc(s.used, RING)
            with pe.Fori(0, HALVES) as hf:
                transposes(hf, 0, lambda k: pe.wait_ge(s.ev_dve, hf * S_EVD + k + 1), True)
                with pe.Fori(0, 2) as c4:
                    for kc in range(KC):
                        pe.wait_ge(s.lo, RING + hf * SU + c4 * KC + kc + 1)

                        def wait_bank(b):
                            pe.wait_ge(g.t_lo, hf * KC + b + 1)
                            pe.wait_ge(s.ev_dve, hf * S_EVD + c4 * BANKS + b + 1)
                        tokens_by_channels(kc % RING, a_hi[:, kc, :], a_lo[:, kc, :], kc == 0, kc == KC - 1,
                                           s.used, s.full, wait_bank)
                with pe.Fori(0, 2) as c4:
                    for kc in range(KC):
                        pe.wait_ge(s.lo, RING + hf * SU + (2 + c4) * KC + kc + 1)

                        def wait_bank(c):
                            pe.wait_ge(s.ev_dve, BANKS + hf * S_EVD + BANKS + c + 1)
                            pe.wait_ge(s.ev_act, hf * S_EVA + c4 * BANKS + c + 1)
                        channels_by_tokens(kc % RING, kc, s.used, s.full, wait_bank)
                pe.wait_ge(g.small, 16 * 8)
                pe.wait_ge(s.v_scaled, HT * (hf + 1))
                for c in range(SGU // P):
                    if c < BANKS:
                        pe.wait_ge(s.ev_act, BANKS + hf * S_EVA + BANKS + c + 1)
                    else:
                        pe.wait_ge(s.ev_dve, BANKS + hf * S_EVD + 2 * BANKS + c - BANKS + 1)
                    for t in range(HT):
                        last = pe.matmul(bank[c % BANKS][:, t * P:(t + 1) * P], v_all[:, t, c * P:(c + 1) * P],
                                         w_s[:, c * P * HEADS // SGU, :], start=True, stop=True)
                    last.then_inc(s.full, 1)
                for kc in range(SGU // P):
                    pe.wait_ge(s.lo, RING + hf * SU + 4 * KC + kc + 1)
                    pe.wait_ge(s.y_lo, hf * (SGU // P) + kc + 1)

                    def wait_bank(b):
                        pe.wait_ge(s.ev_dve, BANKS + hf * S_EVD + BANKS + SGU // P + b + 1)
                    tokens_by_channels(kc % RING, y_hi[:, kc % 2, :], y_lo[:, kc % 2, :], kc == 0,
                                       kc == SGU // P - 1, s.used, s.full, wait_bank)

            def moe(L, wait_mixer):
                M, n0 = m[L], 4 * L + 2
                pe.wait_ge(g.cast, 1)
                pe.wait_ge(g.init, 1)

                def ranks(h):
                    pe.wait_ge(M.chosen, h + 1)
                    for t in range(h * HT, (h + 1) * HT):
                        dst = bank[2 + h][:, t % HT * E:(t % HT + 1) * E]
                        last = pe.matmul(dst, tri[:, :], chosen[:, t, :], start=True, stop=t == 0)
                        for b in range(t):
                            last = pe.matmul(dst, ones[:, :], chosen[:, b, :], start=False, stop=b == t - 1)
                    last.then_inc(M.ranked, 1)

                for h in range(HALVES):
                    if h:
                        transposes(n0 + h, h, lambda k: pe.wait_ge(M.logits_read, 1) if k == 1 else None, False)
                    else:
                        transposes(n0, 0, wait_mixer, True)
                    pe.wait_ge(M.rw_lo, 1)
                    for k in range(KC):
                        pe.wait_ge(g.t_lo, KC * (n0 + h) + k + 1)
                        last = three(bank[0][:, :], rw_hi[:, k, :], rw_lo[:, k, :], a_hi[:, k, :], a_lo[:, k, :],
                                     k == 0, k == KC - 1)
                    last.then_inc(M.logits, 1)
                    if h:
                        ranks(0)
                    pe.wait_ge(M.biased, h + 1)
                    for t in range(HT):
                        last = pe.transpose(bank[1][:, t * P:(t + 1) * P], lt[:, t * P:(t + 1) * P], ident)
                    last.then_inc(M.logits, 1)
                ranks(1)
                for t in range(TT):
                    last = pe.matmul(bank[7][:, 0:E], ones[:, :], chosen[:, t, :], start=t == 0, stop=t == TT - 1)
                last.then_inc(M.ranked, 1)

                def x_transposes(i):
                    pe.wait_ge(M.gathered, 16 * (i + 1))
                    rows = xg.rearrange("t (p k) -> t k p", k=KC)
                    for k in range(KC):
                        last = pe.transpose(bank[4 + k // 4][:, k % 4 * P:(k % 4 + 1) * P], rows[:, k, :], ident)
                    last.then_inc(M.x_full, 1)

                def gate_up(i, lo_wait, gap):
                    pe.wait_ge(M.x_lo, 2 * (i + 1))
                    for j in range(GU):
                        lo_wait(j)
                        for k in range(2):
                            c = 2 * (j % DN) + k
                            col = slice(k * F, (k + 1) * F)
                            last = three(bank[j // DN][:, :], x_hi[:, c, :], x_lo[:, c, :],
                                         w_hi[:, j % RING, col], w_lo[:, j % RING, col], c == 0, c == KC - 1)
                        last.then_inc(M.used, 1 + (gap if j == GU - 1 else 0))

                def down(i, lo_wait):
                    pe.wait_ge(M.h_lo, i + 1)
                    for j in range(DN):
                        lo_wait(j)
                        for c in range(2):
                            col = slice(c * 512, (c + 1) * 512)
                            last = three(bank[2 + c][:, :], h_hi[:, j, :], h_lo[:, j, :],
                                         w_hi[:, j, col], w_lo[:, j, col], j == 0, j == DN - 1)
                        last.then_inc(M.used, 1)

                def h_transposes(i):
                    pe.wait_ge(M.hid, i + 1)
                    cols_of = hid.rearrange("t (p k) -> t k p", k=DN)
                    for k in range(DN):
                        last = pe.transpose(bank[6][:, k * P:(k + 1) * P], cols_of[:, k, :], ident)
                    last.then_inc(M.h_full, 1)

                def round_(i, before_down):
                    pe.wait_ge(M.hid, i)
                    gate_up(i, lambda j: pe.wait_ge(M.lo, ROUND * i + j + 1), 0)
                    x_transposes(i + 1)
                    before_down(i)
                    down(i - 1, lambda j: pe.wait_ge(M.lo, ROUND * i + GU + j + 1))
                    h_transposes(i)

                x_transposes(0)
                pe.wait_ge(M.table, 1)
                n = pe.value_load(table[0:1, 0, TABLE - 1:TABLE], min_val=E - 2, max_val=ITEMS_MAX - 2) + 2
                gate_up(0, lambda j: pe.wait_ge(M.lo, j + 1), DN)
                x_transposes(1)
                h_transposes(0)
                round_(1, lambda i: None)
                with pe.Fori(2, n) as i:
                    round_(i, lambda i: pe.wait_ge(M.y_out, 2 * (i - 1)))
                pe.wait_ge(M.y_out, 2 * (n - 1))
                down(n - 1, lambda j: pe.wait_ge(M.lo, ROUND * n + j + 1))

            moe(0, lambda k: pe.wait_ge(s.ev_dve, HALVES * S_EVD + k + 1))

            pe.sem_inc(q.used, RING)
            for hf in range(HALVES):
                transposes(4 + hf, 1, lambda k: pe.wait_ge(q.ev_act, hf * BANKS + k + 1), bool(hf))
                for kc in range(KC):
                    pe.wait_ge(q.lo, RING + hf * PV + kc + 1)
                    channels_by_tokens(kc % RING, kc, q.used, q.full,
                                       lambda c: pe.wait_ge(g.t_lo, (4 + hf) * KC + c + 1))
            for hf in range(HALVES):
                base = HALVES * PV + hf * (PG + PO)
                for r in range(PG):
                    pe.wait_ge(q.lo, RING + base + r + 1)
                    for c in range(4):
                        b, grp, o = 4 * r + c, c // 2, c % 2
                        pe.wait_ge(q.d_lo, hf * KC + 4 * r + 2 * grp + 2)
                        if hf == 0:
                            pe.wait_ge(q.ev_act, BANKS + HALVES * BANKS)
                        else:
                            pe.wait_ge(q.ev_dve, (hf - 1) * BANKS + b + 1)
                        for k in range(2):
                            w = slice((2 * grp + k) * 256 + o * P, (2 * grp + k) * 256 + (o + 1) * P)
                            a = 4 * r + 2 * grp + k
                            last = three(bank[b][:, :], w_hi[:, (base + r) % RING, w], w_lo[:, (base + r) % RING, w],
                                         a_hi[:, a, :], a_lo[:, a, :], k == 0, k == 1)
                        if c < 3:
                            last.then_inc(q.full, 1)
                    last.then_inc(q.used, 1)
                for kc in range(KC):
                    u = base + PG + kc
                    pe.wait_ge(q.lo, RING + u + 1)
                    pe.wait_ge(q.y_lo, hf * KC + kc + 1)
                    tokens_by_channels(u % RING, y_hi[:, kc % 2, :], y_lo[:, kc % 2, :], kc == 0, kc == KC - 1,
                                       q.used, q.full, lambda b: pe.wait_ge(q.g_out, hf * BANKS + b + 1))
            moe(1, lambda k: pe.wait_ge(q.ev_dve, BANKS + k + 1))

        Q_V = HALVES * BF
        Q_HALF = 6 + BF

        @block.scalar
        def _(act):
            def copy(dst, src):
                return nc.scalar.activation(dst, src, ACT.Copy)

            def split(M, slot_raw, slot, src, loads, used):
                act.wait_ge(M.raw[slot_raw], 16 * loads)
                act.wait_ge(M.used, used)
                copy(w_hi[:, slot, :], src).then_inc(M.hi, 1)

            def square(h, base, t):
                nc.scalar.activation(hn[h][:, t, :], x_res[:, bass.ds(base + t, 1), :].rearrange("p o d -> p (o d)"),
                                     ACT.Square, accum_out=ss[:, t:t + 1]).then_inc(g.sq, 1)

            def root(n, t):
                act.wait_ge(g.var, n * HT + t + 1)
                nc.scalar.activation(std[:, t:t + 1], var[:, t:t + 1], ACT.Sqrt).then_inc(g.std, 1)

            def norm(n, h, base, wait_x):
                for t in range(HT + 1):
                    if t < HT:
                        wait_x(t)
                        square(h, base, t)
                    if t:
                        root(n, t - 1)

            def norm_added(L, n, h, base, t):
                act.wait_ge(m[L].added, base + t + 1)
                square(h, base, t)
                root(n, t)

            def transposed(n):
                for k in range(KC):
                    act.wait_ge(g.t_full, n * KC + k + 1)
                    copy(a_hi[:, k, :], bank[k][:, :]).then_inc(g.t_hi, 1)

            act.sem_inc(s.ev_act, BANKS)
            norm(0, 0, 0, lambda t: act.wait_ge(g.x_loaded[t], 16))
            with act.Fori(0, HALVES) as hf:
                def unit(u):
                    split(s, u % RING, u % RING, raw[:, u % RING, :],
                          hf * (SU // RING) + u // RING + 1, hf * SU + u + 1)
                unit(0)
                transposed(hf)
                unit(1)
                unit(2)

                def wait_full(first_full, b, last_unit):
                    if b < BF:
                        act.wait_ge(s.full, hf * S_FULL + first_full + b + 1)
                    else:
                        act.wait_ge(s.used, RING + hf * SU + last_unit)

                def v_tiles(c4):
                    for b in range(BANKS):
                        act.wait_ge(s.ev_dve, BANKS + hf * S_EVD + c4 * BANKS + b + 1)
                        col = slice(c4 * 1024 + b % 2 * 512, c4 * 1024 + b % 2 * 512 + 512)
                        nc.scalar.activation(v_all[:, b // 2, col], v_all[:, b // 2, col], ACT.Gelu).then_inc(s.v_gelu, 1)
                        act.wait_ge(s.v_gelu, hf * 2 * BANKS + c4 * BANKS + b + 1)
                        nc.scalar.activation(y_hi[:, 0, :], v_all[:, b // 2, col], ACT.Square,
                                             accum_out=v_ss[:, b // 2, 2 * c4 + b % 2:2 * c4 + b % 2 + 1]) \
                            .then_inc(s.v_sq, 1)
                def u_banks(c4):
                    for b in range(BANKS):
                        wait_full((2 + c4) * BF, b, (3 + c4) * KC)
                        c = c4 * BANKS + b
                        nc.scalar.activation(u_all[:, c, :], bank[b][:, :], ACT.Gelu,
                                             bias=cols[:, c:c + 1]).then_inc(s.ev_act, 1)
                for c4 in range(5):
                    for kc in range(3 if c4 else 0):
                        unit(c4 * KC + kc)
                    if c4 in (1, 2):
                        v_tiles(c4 - 1)
                    if c4 in (3, 4):
                        act.wait_ge(g.small, 16 * 8)
                        act.wait_ge(g.lists_ready, 16 * LAYERS)
                        u_banks(c4 - 3)
                    if c4 < 4:
                        for kc in range(3, KC):
                            unit(c4 * KC + kc)
                    if c4 == 2:
                        act.wait_ge(s.v_var, hf + 1)
                        nc.scalar.activation(std, var, ACT.Sqrt).then_inc(s.v_std, 1)
                for kc in range(SGU // P):
                    act.wait_ge(s.ev_dve, BANKS + hf * S_EVD + 2 * BANKS + kc + 1)
                    if kc >= 2:
                        act.wait_ge(s.used, RING + hf * SU + 4 * KC + kc - 1)
                    copy(y_hi[:, kc % 2, :], u_all[:, kc, :]).then_inc(s.y_hi, 1)
                    if kc + 3 < SGU // P:
                        unit(4 * KC + kc + 3)
                act.wait_ge(s.ev_dve, BANKS + hf * S_EVD)
                norm(hf + 1, 0, HT - hf * HT, lambda t: act.wait_ge(g.x_loaded[t], 32))

            def moe(L, wait_y, wait_x):
                M, n0 = m[L], 4 * L + 2
                act.wait_ge(M.small, 32)
                wait_y()
                copy(y_hi[:, :, :].rearrange("p a c -> p (a c)"), spatial[:, :]).then_inc(M.rw_hi, 1)

                def exps(h):
                    half = slice(h * HT, (h + 1) * HT)
                    act.wait_ge(M.g_shifted, h + 1)
                    nc.scalar.activation(r_gexp[:, half, :], r_gexp[:, half, :], ACT.Exp).then_inc(M.exps, 1)
                    act.wait_ge(M.e_shifted, h + 1)
                    nc.scalar.activation(r_eexp[:, half, :], r_ediff[:, half, :], ACT.Exp).then_inc(M.exps, 1)

                for h in range(HALVES):
                    transposed(n0 + h)
                    if h == 0:
                        wait_x()
                        norm(n0 + 1, 1, HT, lambda t: None)
                    else:
                        exps(0)
                    act.wait_ge(M.logits, 2 * h + 1)
                    nc.scalar.activation(lt, bank[0][:, :], ACT.Identity, bias=rb).then_inc(M.biased, 1)
                exps(1)

                def unit(c, loads, used, gap=0, slots=moe_raw):
                    act.wait_ge(M.raw[c], 16 * loads)
                    if used is not None:
                        act.wait_ge(M.used, used)
                    copy(w_hi[:, c % RING, :], slots[c]).then_inc(M.hi, 1 + gap)

                def x_split(i):
                    act.wait_ge(M.x_full, i + 1)
                    for b in range(2):
                        copy(x_hi[:, 4 * b:4 * b + 4, :].rearrange("p k t -> p (k t)"), bank[4 + b][:, :]) \
                            .then_inc(M.x_hi, 1)

                def silu(i):
                    act.wait_ge(M.used, ROUND * i + DN)
                    nc.scalar.activation(silu_g, bank[0][:, :], ACT.Silu).then_inc(M.silu, 1)

                def h_split(i):
                    act.wait_ge(M.h_full, i + 1)
                    copy(h_hi.rearrange("p k t -> p (k t)"), bank[6][:, :]).then_inc(M.h_hi, 1)

                def y_out(i, used):
                    act.wait_ge(M.used, used)
                    act.wait_ge(M.meta_s, 16 * (i + 1))
                    for c in range(2):
                        nc.scalar.activation(y_sb[:, c, :], bank[2 + c][:, :], ACT.Copy,
                                             scale=meta_s[:, 2:3].bitcast(F32)).then_inc(M.y_out, 1)

                def round_(i, with_y, slots, down_slots=moe_raw):
                    for c in range(4):
                        unit(c, i + 1, ROUND * i + c - 3, slots=slots)
                    if with_y:
                        y_out(i - 2, ROUND * i)
                    h_split(i - 1)
                    for c in range(4, GU):
                        unit(c, i + 1, ROUND * i + c - 3, slots=slots)
                    silu(i)
                    for c in range(GU, ROUND):
                        unit(c, i, ROUND * i + c - 3, slots=down_slots)
                    x_split(i + 1)

                for c in range(GU):
                    if c == RING:
                        x_split(0)
                    unit(c, 1, c - 3 if c >= RING else None, DN if c == GU - 1 else 0)
                silu(0)
                x_split(1)
                act.wait_ge(M.table, 1)
                n = act.value_load(table[0:1, 0, TABLE - 1:TABLE], min_val=E - 2, max_val=ITEMS_MAX - 2) + 2
                round_(1, False, early_raw)
                round_(2, True, moe_raw, early_down)
                with act.Fori(3, n) as i:
                    round_(i, True, moe_raw)
                for c in range(DN):
                    unit(GU + c, n, ROUND * (n - 1) + GU + c + 1)
                y_out(n - 2, ROUND * n)
                h_split(n - 1)
                y_out(n - 1, ROUND * n + DN)

            moe(0, lambda: act.wait_ge(s.used, RING + HALVES * SU), lambda: act.wait_ge(s.ev_dve, BANKS + HALVES * S_EVD))

            act.sem_inc(q.ev_act, BANKS)
            def unit(u):
                split(q, u % RING, u % RING, raw[:, u % RING, :], u // RING + 1, u + 1)

            def v_banks(hf):
                for c in range(BANKS):
                    if c < BF:
                        act.wait_ge(q.full, hf * BF + c + 1)
                    else:
                        act.wait_ge(q.used, RING + hf * PV + PV)
                    copy(padded[:, c, PAD + hf * HTOK:PAD + (hf + 1) * HTOK], bank[c][:, :]).then_inc(q.ev_act, 1)

            for u in range(PV):
                if u == 3:
                    for t in range(HT):
                        norm_added(0, 4, 1, 0, t)
                    transposed(4)
                unit(u)
                if u >= PV - HT:
                    norm_added(0, 5, 1, HT, u - (PV - HT))
            for u in range(PV, PV + 3):
                unit(u)
            v_banks(0)
            transposed(5)
            for u in range(PV + 3, 2 * PV + 3):
                unit(u)
            v_banks(1)

            def d_split(hf, c):
                act.wait_ge(q.d_ready, hf * len(WINDOWS) + c // 2 + 1)
                copy(a_hi[:, c, :], d_of[hf][:, c, :]).then_inc(q.d_hi, 1)

            for c in range(KC):
                d_split(0, c)
            for hf in range(HALVES):
                base = HALVES * PV + hf * (PG + PO)
                for r in range(3 if hf else 0):
                    unit(base + r)
                for b in range(BANKS):
                    if b % 4 < 3:
                        act.wait_ge(q.full, Q_V + hf * Q_HALF + b // 4 * 3 + b % 4 + 1)
                    else:
                        act.wait_ge(q.used, RING + base + b // 4 + 1)
                    if hf:
                        act.wait_ge(q.y_lo, hf * KC)
                    nc.scalar.activation(y_f32[:, b, :], bank[b][:, :], ACT.Copy, scale=cols[:, 32 + b:33 + b]) \
                        .then_inc(q.g_out, 1)
                for kc in range(KC):
                    act.wait_ge(q.g_out, hf * BANKS + kc + 1)
                    if kc >= 2:
                        act.wait_ge(q.used, RING + base + PG + kc - 1)
                    elif hf:
                        act.wait_ge(q.used, RING + base)
                    copy(y_hi[:, kc % 2, :], y_f32[:, kc, :]).then_inc(q.y_hi, 1)
                    if PG + kc + 1 < PG + PO:
                        unit(base + PG + kc + 1)
                    if hf == 0 and kc >= KC // 2:
                        act.wait_ge(q.used, RING + base + PG)
                        d_split(1, 2 * kc - KC)
                        d_split(1, 2 * kc - KC + 1)
            act.wait_ge(q.ev_dve, BANKS)
            norm(6, 0, 0, lambda t: None)

            moe(1, lambda: act.wait_ge(q.used, RING + HALVES * (PV + PG + PO)), lambda: act.wait_ge(q.ev_dve, HALVES * BANKS))

            for t in range(TT):
                norm_added(1, 8 + t // HT, t // HT, t // HT * HT, t % HT)

        @block.vector
        def _(dve):
            def lo_of(dst, src, hi):
                return nc.vector.tensor_tensor(dst, src, f32(hi), ALU.subtract)

            def mean_square(n, t):
                dve.wait_ge(g.sq, HT * n + t + 1)
                nc.vector.tensor_scalar(var[:, t:t + 1], ss[:, t:t + 1], 1.0 / D, EPS, ALU.mult, ALU.add).then_inc(g.var, 1)

            def normed_tile(n, h, base, t):
                x = x_res[:, bass.ds(base + t, 1), :].rearrange("p o d -> p (o d)")
                dve.wait_ge(g.std, HT * n + t + 1)
                nc.vector.reciprocal(rstd[:, t:t + 1], std[:, t:t + 1]).then_inc(g.rstd, 1)
                dve.wait_ge(g.rstd, HT * n + t + 1)
                nc.vector.scalar_tensor_tensor(hn[h][:, t, :], x, rstd[:, t:t + 1], gain[:, :], ALU.mult, ALU.mult) \
                    .then_inc(g.hn, 1)

            def norm(n, h, base):
                mean_square(n, 0)
                for t in range(HT):
                    if t + 1 < HT:
                        mean_square(n, t + 1)
                    normed_tile(n, h, base, t)

            def add(L, t):
                M = m[L]
                dve.wait_ge(M.summed, t + 1)
                nc.vector.tensor_tensor(x_res[:, t, :], x_res[:, t, :], comb[t % COMBS][:, 0, :], ALU.add).then_inc(M.added, 1)

            def add_and_norm(L, n, slots, tiles):
                add(L, 0)
                for t in range(tiles):
                    if t + 1 < tiles:
                        add(L, t + 1)
                    mean_square(n + t // HT, t % HT)
                    normed_tile(n + t // HT, slots[t // HT], t // HT * HT, t % HT)

            def transposed(n):
                for k in range(KC):
                    dve.wait_ge(g.t_hi, n * KC + k + 1)
                    lo_of(a_lo[:, k, :], bank[k][:, :], a_hi[:, k, :]).then_inc(g.t_lo, 1)

            dve.wait_ge(g.consts, 16)
            nc.vector.tensor_copy(tri[:, :], cf[:, C_TRI:C_TRI + P]).then_inc(g.cast, 1)
            dve.sem_inc(s.ev_dve, BANKS)
            dve.wait_ge(g.gain_ready, 16)
            norm(0, 0, 0)
            with dve.Fori(0, HALVES) as hf:
                def unit(u):
                    dve.wait_ge(s.hi, hf * SU + u + 1)
                    lo_of(w_lo[:, u % RING, :], raw[:, u % RING, :], w_hi[:, u % RING, :]).then_inc(s.lo, 1)
                unit(0)
                transposed(hf)
                unit(1)
                unit(2)

                def wait_full(first_full, b, last_unit):
                    if b < BF:
                        dve.wait_ge(s.full, hf * S_FULL + first_full + b + 1)
                    else:
                        dve.wait_ge(s.used, RING + hf * SU + last_unit)

                def v_banks(c4):
                    for b in range(BANKS):
                        wait_full(c4 * BF, b, (1 + c4) * KC)
                        col = slice(c4 * 1024 + b % 2 * 512, c4 * 1024 + b % 2 * 512 + 512)
                        nc.vector.tensor_tensor(v_all[:, b // 2, col], bank[b][:, :], vbias[:, col], ALU.add) \
                            .then_inc(s.ev_dve, 1)

                for c4 in range(5):
                    for kc in range(3 if c4 else 0):
                        unit(c4 * KC + kc)
                    if c4 == 1:
                        dve.wait_ge(g.small, 16 * 8)
                    if c4 in (1, 2):
                        v_banks(c4 - 1)
                    if c4 < 4:
                        for kc in range(3, KC):
                            unit(c4 * KC + kc)
                    if c4 == 2:
                        dve.wait_ge(s.v_sq, (hf + 1) * 2 * BANKS)
                        nc.vector.tensor_reduce(ss, v_ss, AX.X, ALU.add).then_inc(s.v_chain, 1)
                        dve.wait_ge(s.v_chain, 2 * hf + 1)
                        nc.vector.tensor_scalar(var, ss, 1.0 / SGU, EPS, ALU.mult, ALU.add).then_inc(s.v_var, 1)
                        dve.wait_ge(s.v_std, hf + 1)
                        nc.vector.reciprocal(rstd, std).then_inc(s.v_chain, 1)
                        dve.wait_ge(s.v_chain, 2 * hf + 2)
                        for t in range(HT):
                            nc.vector.tensor_scalar(v_all[:, t, :], v_all[:, t, :], rstd[:, t:t + 1], None, ALU.mult) \
                                .then_inc(s.v_scaled, 1)

                def y_split(kc):
                    dve.wait_ge(s.y_hi, hf * (SGU // P) + kc + 1)
                    lo_of(y_lo[:, kc % 2, :], u_all[:, kc, :], y_hi[:, kc % 2, :]).then_inc(s.y_lo, 1)

                for c in range(SGU // P):
                    dve.wait_ge(s.full, hf * S_FULL + 4 * BF + c + 1)
                    sv = bank[c % BANKS][:, :].rearrange("p (t s) -> p t s", s=P)
                    head = c * P * HEADS // SGU
                    nc.vector.scalar_tensor_tensor(sv, sv, cols[:, 16 + c:17 + c],
                                                   b_s[:, head:head + 1, :].to_broadcast([P, HT, P]),
                                                   ALU.mult, ALU.add).then_inc(s.gated, 1)
                    dve.wait_ge(s.gated, hf * (SGU // P) + c + 1)
                    nc.vector.tensor_tensor(u_all[:, c, :], bank[c % BANKS][:, :], u_all[:, c, :], ALU.mult) \
                        .then_inc(s.ev_dve, 1)
                    if c == BANKS:
                        y_split(0)
                        unit(4 * KC + 3)
                    if c == BANKS + 2:
                        y_split(1)
                unit(4 * KC + 4)
                for kc in range(2, SGU // P):
                    y_split(kc)
                    if kc + 3 < SGU // P:
                        unit(4 * KC + kc + 3)
                dve.wait_ge(g.gain_ready, 16 * (hf + 1))
                norm(hf + 1, 0, HT - hf * HT)
                for b in range(BANKS):
                    wait_full(4 * BF + SGU // P, b, SU)
                    x = x_res[:, bass.ds(hf * HT + b // 2, 1), b % 2 * 512:b % 2 * 512 + 512].rearrange("p o d -> p (o d)")
                    nc.vector.tensor_tensor(x, bank[b][:, :], x, ALU.add).then_inc(s.ev_dve, 1)
                dve.wait_ge(s.ev_dve, BANKS + (hf + 1) * S_EVD)

            def moe(L):
                M, n0 = m[L], 4 * L + 2

                steps = [0]

                def step(ins):
                    steps[0] += 1
                    ins.then_inc(M.chain, 1)
                    dve.wait_ge(M.chain, steps[0])

                def tt(dst, a, b, op):
                    return nc.vector.tensor_tensor(dst, a, b, op)

                def logits(h):
                    dve.wait_ge(M.logits, 2 * h + 2)
                    nc.vector.tensor_copy(lg[:, h * HT:(h + 1) * HT, :],
                                          bank[1][:, :].rearrange("p (t c) -> p t c", c=P)[:, :, 0:36]) \
                        .then_inc(M.logits_read, 1)

                def choose(h):
                    ts, c3 = slice(h * HT, (h + 1) * HT), [P, HT, E]
                    tiles = range(h * HT, (h + 1) * HT)
                    dve.wait_ge(M.logits_read, h + 1)
                    step(nc.vector.tensor_copy(r_gpad[:, ts, 0:GROUPS], lg[:, ts, 0:GROUPS]))
                    for t in tiles:
                        last = nc.vector.max(r_gmax[:, t, :], r_gpad[:, t, :])
                    step(last)
                    tt(r_gexp[:, ts, :], lg[:, ts, 0:GROUPS], r_gmax[:, ts, 0:1].to_broadcast([P, HT, GROUPS]), ALU.subtract) \
                        .then_inc(M.g_shifted, 1)
                    for t in tiles:
                        last = nc.vector.max_index(r_gidx[:, t, :], r_gmax[:, t, :], r_gpad[:, t, :])
                    step(last)
                    step(nc.vector.tensor_copy(r_grp[:, ts, :], r_gidx[:, ts, 0:1]))
                    step(tt(r_mask[:, ts, :], const3(C_GRP, E, HT), r_grp[:, ts, :].to_broadcast(c3), ALU.is_equal))
                    tt(r_el[:, ts, :], r_mask[:, ts, :], lg[:, ts, GROUPS:36], ALU.mult)
                    step(nc.vector.tensor_scalar(r_mask[:, ts, :], r_mask[:, ts, :], BIG, -BIG, ALU.mult, ALU.add))
                    step(tt(r_el[:, ts, :], r_el[:, ts, :], r_mask[:, ts, :], ALU.add))
                    for t in tiles:
                        last = nc.vector.max(r_emax[:, t, :], r_el[:, t, :])
                    step(last)
                    tt(r_ediff[:, ts, :], r_emax[:, ts, 1:2], r_emax[:, ts, 0:1], ALU.subtract).then_inc(M.e_shifted, 1)
                    for t in tiles:
                        last = nc.vector.max_index(r_eidx[:, t, :], r_emax[:, t, :], r_el[:, t, :])
                    step(last)
                    step(nc.vector.tensor_copy(r_e[:, ts, :], r_eidx[:, ts, 0:2]))
                    for k in range(2):
                        last = tt(r_oh[k][:, ts, :], const3(C_E, E, HT), r_e[:, ts, k:k + 1].to_broadcast(c3), ALU.is_equal)
                    step(last)
                    tt(chosen[:, ts, :], r_oh[0][:, ts, :], r_oh[1][:, ts, :], ALU.add).then_inc(M.chosen, 1)
                    dve.wait_ge(M.exps, 2 * h + 1)
                    nc.vector.tensor_reduce(r_gsum[:, ts, :], r_gexp[:, ts, :], AX.X, ALU.add)
                    dve.wait_ge(M.exps, 2 * h + 2)
                    step(nc.vector.tensor_scalar(r_den[:, ts, :], r_eexp[:, ts, :], 1.0, None, ALU.add))
                    nc.vector.reciprocal(r_gw[:, ts, :], r_gsum[:, ts, :])
                    step(nc.vector.reciprocal(r_rden[:, ts, :], r_den[:, ts, :]))
                    step(tt(r_w[:, ts, 0:1], r_gw[:, ts, :], r_rden[:, ts, :], ALU.mult))
                    step(tt(r_w[:, ts, 1:2], r_w[:, ts, 0:1], r_eexp[:, ts, :], ALU.mult))
                    step(nc.vector.tensor_copy(payload[:, ts, :, 2:3].bitcast(F32).rearrange("p t k w -> p t (k w)"),
                                               r_w[:, ts, :]))

                def places(h):
                    ts = slice(h * HT, (h + 1) * HT)
                    dve.wait_ge(M.ranked, h + 1)
                    step(tt(r_pos[:, ts, :], bank[2 + h][:, 0:HT * E].rearrange("p (t e) -> p t e", e=E),
                            const3(C_BASE, E, HT), ALU.add))
                    for k in range(2):
                        last = tt(r_oh[k][:, ts, :], r_oh[k][:, ts, :], r_pos[:, ts, :], ALU.mult)
                    step(last)
                    for k in range(2):
                        last = nc.vector.tensor_reduce(r_place[:, ts, k:k + 1], r_oh[k][:, ts, :], AX.X, ALU.add)
                    step(last)
                    nc.vector.tensor_copy(place[:, ts, :], r_place[:, ts, :]).then_inc(M.placed, 1)

                def unit(c, hi, slots=moe_raw):
                    dve.wait_ge(M.hi, hi)
                    return lo_of(w_lo[:, c % RING, :], slots[c], w_hi[:, c % RING, :])

                dve.wait_ge(M.rw_hi, 1)
                lo_of(y_lo[:, :, :].rearrange("p a c -> p (a c)"), spatial[:, :],
                      y_hi[:, :, :].rearrange("p a c -> p (a c)")).then_inc(M.rw_lo, 1)
                transposed(n0)
                step(nc.vector.memset(r_gpad, -BIG))
                norm(n0 + 1, 1, HT)
                logits(0)
                transposed(n0 + 1)
                choose(0)
                places(0)
                logits(1)
                choose(1)
                places(1)
                for c in range(RING):
                    unit(c, c + 1).then_inc(M.lo, 1)
                dve.wait_ge(M.ranked, 3)

                step(nc.vector.memset(sbias[0:1, 0:12 * E], 0.0))
                over = [sbias[0:1, 2 * E * k:2 * E * (k + 1)] for k in range(6)]
                cmp = sbias[0:1, 512:512 + E * (BPE - 1)].rearrange("p (e b) -> p e b", b=BPE - 1)
                thr = cf[0:1, C_THR:C_THR + BPE - 1].rearrange("p (o b) -> p o b", o=1)
                step(tt(cmp, bank[7][0:1, 0:E].rearrange("p (e o) -> p e o", o=1).to_broadcast([1, E, BPE - 1]),
                        thr.to_broadcast([1, E, BPE - 1]), ALU.is_gt))
                step(nc.vector.tensor_reduce(over[0][:, E:2 * E], cmp, AX.X, ALU.add))
                for k in range(5):
                    step(tt(over[k + 1][:, E:2 * E], over[k][:, E:2 * E], over[k][:, E - 2 ** k:2 * E - 2 ** k], ALU.add))
                incl, excl, row = over[5][:, E:2 * E], sbias[0:1, 768:768 + E], sbias[0:1, 800:800 + E]
                step(tt(excl, incl, over[0][:, E:2 * E], ALU.subtract))
                step(tt(row, cf[0:1, C_E8:C_E8 + E], excl, ALU.subtract))
                ind, tmp = [vbias[0:1, 512 * k:512 * (k + 1)].rearrange("p (j e) -> p j e", e=E) for k in (0, 1)]

                def by_e(ap):
                    return ap.rearrange("p (o e) -> p o e", o=1).to_broadcast([1, EXTRA, E])
                by_j = cf[0:1, C_J:C_J + EXTRA].rearrange("p (j o) -> p j o", o=1).to_broadcast([1, EXTRA, E])
                step(tt(ind, by_e(excl), by_j, ALU.is_le))
                step(tt(tmp, by_e(incl), by_j, ALU.is_gt))
                step(tt(ind, ind, tmp, ALU.mult))
                step(tt(tmp, ind, by_e(cf[0:1, C_E:C_E + E]), ALU.mult))
                step(nc.vector.tensor_reduce(sbias[0:1, 832:832 + EXTRA], tmp, AX.X, ALU.add))
                step(tt(tmp, by_e(row), by_j, ALU.add))
                step(tt(tmp, tmp, ind, ALU.mult))
                step(nc.vector.tensor_reduce(sbias[0:1, 848:848 + EXTRA], tmp, AX.X, ALU.add))
                step(nc.vector.tensor_copy(table[0:1, 0, E:E + EXTRA], sbias[0:1, 832:832 + EXTRA]))
                step(nc.vector.tensor_copy(table[0:1, 1, E:E + EXTRA], sbias[0:1, 848:848 + EXTRA]))
                nc.vector.tensor_scalar(table[0:1, 0, TABLE - 1:TABLE], incl[:, E - 1:E], float(E - 2), None, ALU.add) \
                    .then_inc(M.table, 1)

                def x_split(i):
                    for b in range(2):
                        dve.wait_ge(M.x_hi, 2 * i + b + 1)
                        lo_of(x_lo[:, 4 * b:4 * b + 4, :].rearrange("p k t -> p (k t)"), bank[4 + b][:, :],
                              x_hi[:, 4 * b:4 * b + 4, :].rearrange("p k t -> p (k t)")).then_inc(M.x_lo, 1)

                def hidden(i):
                    dve.wait_ge(M.silu, i + 1)
                    dve.wait_ge(M.used, ROUND * i + GU)
                    if not isinstance(i, int) or i:
                        dve.wait_ge(M.h_full, i)
                    nc.vector.tensor_tensor(hid, bank[1][:, :], silu_g, ALU.mult).then_inc(M.hid, 1)

                def h_split(i):
                    dve.wait_ge(M.h_hi, i + 1)
                    lo_of(h_lo.rearrange("p k t -> p (k t)"), bank[6][:, :],
                          h_hi.rearrange("p k t -> p (k t)")).then_inc(M.h_lo, 1)

                def round_(i, slots, down_slots=moe_raw):
                    for c in range(4):
                        unit(c, ROUND * i + c + 1, slots).then_inc(M.lo, 1)
                    h_split(i - 1)
                    for c in range(4, ROUND):
                        unit(c, ROUND * i + c + 1, slots if c < GU else down_slots).then_inc(M.lo, 1)
                    hidden(i)
                    x_split(i + 1)

                x_split(0)
                for c in range(RING, GU):
                    unit(c, c + 1).then_inc(M.lo, 1 + (DN if c == GU - 1 else 0))
                hidden(0)
                x_split(1)
                dve.wait_ge(M.table, 1)
                n = dve.value_load(table[0:1, 0, TABLE - 1:TABLE], min_val=E - 2, max_val=ITEMS_MAX - 2) + 2
                round_(1, early_raw)
                round_(2, moe_raw, early_down)
                with dve.Fori(3, n) as i:
                    round_(i, moe_raw)
                for c in range(DN):
                    unit(GU + c, ROUND * n + c + 1).then_inc(M.lo, 1)
                h_split(n - 1)

            moe(0)

            dve.wait_ge(g.gain_ready, 16 * 3)
            steps = [0]

            def step(ins):
                steps[0] += 1
                ins.then_inc(q.chain, 1)
                dve.wait_ge(q.chain, steps[0])

            def unit(u):
                dve.wait_ge(q.hi, u + 1)
                lo_of(w_lo[:, u % RING, :], raw[:, u % RING, :], w_hi[:, u % RING, :]).then_inc(q.lo, 1)

            def pool_tokens(grp, start, end, dst):
                w = WINDOWS[grp]
                h = w // 2
                v = padded[:, 2 * grp:2 * grp + 2, :]
                cur, lo, width, other = v, -PAD, 1, 0
                while width < w:
                    back, ahead = (1, 0) if width == 1 else (width // 2, width // 2)
                    reach = h - width
                    nlo, nhi = start - reach, end + reach
                    nxt = sums[other]
                    step(nc.vector.tensor_tensor(nxt[:, :, 0:nhi - nlo], cur[:, :, nlo - back - lo:nhi - back - lo],
                                                 cur[:, :, nlo + ahead - lo:nhi + ahead - lo], ALU.add))
                    cur, lo, width, other = nxt, nlo, 2 * width, 1 - other
                first, last = start, end
                for at, size, cc in ((0, h, C_ASC + h), (SEQ - h + 1, h - 1, C_DESC + 16 - (w - 1))):
                    if size and start <= at < end:
                        count = cf[:, cc:cc + size].rearrange("p (o t) -> p o t", o=1).to_broadcast([P, 2, size])
                        step(nc.vector.tensor_tensor(edge[:, :, 0:size], cur[:, :, at - lo:at + size - lo], count, ALU.mult))
                        step(nc.vector.tensor_tensor(dst[:, 2 * grp:2 * grp + 2, at % HTOK:at % HTOK + size],
                                                     edge[:, :, 0:size], v[:, :, PAD + at:PAD + at + size], ALU.subtract))
                        first, last = (at + size, last) if at == 0 else (first, at)
                step(nc.vector.scalar_tensor_tensor(dst[:, 2 * grp:2 * grp + 2, first % HTOK:first % HTOK + last - first],
                                                    cur[:, :, first - lo:last - lo], 1.0 / w,
                                                    v[:, :, PAD + first:PAD + last], ALU.mult, ALU.subtract))

            def d_split(hf, c):
                dve.wait_ge(q.d_hi, hf * KC + c + 1)
                lo_of(a_lo[:, c, :], d_of[hf][:, c, :], a_hi[:, c, :]).then_inc(q.d_lo, 1)

            for u in range(PV):
                if u == 3:
                    add_and_norm(0, 4, (1,), HT)
                    transposed(4)
                t = u - (PV - HT)
                if t >= 0:
                    add(0, HT + t)
                unit(u)
                if t >= 0:
                    mean_square(5, t)
                    normed_tile(5, 1, HT, t)
            for u in range(PV, PV + 3):
                unit(u)
            for at in (0, PAD + SEQ):
                nc.vector.memset(padded[:, :, at:at + PAD], 0.0).then_inc(q.zeroed, 1)
            transposed(5)
            dve.wait_ge(q.zeroed, 2)
            for u in range(PV + 3, 2 * PV):
                unit(u)
                grp = u - (2 * PV - len(WINDOWS))
                if grp >= 0:
                    dve.wait_ge(q.ev_act, BANKS + 2 * grp + 2)
                    pool_tokens(grp, 0, HTOK - PAD, d_first)
            for r in range(3):
                unit(2 * PV + r)
            for grp in range(len(WINDOWS)):
                dve.wait_ge(q.ev_act, 2 * BANKS + 2 * grp + 2)
                pool_tokens(grp, HTOK - PAD, HTOK, d_first)
                dve.sem_inc(q.d_ready, 1)
                if grp:
                    d_split(0, 2 * grp - 2)
                    d_split(0, 2 * grp - 1)
            d_split(0, KC - 2)
            d_split(0, KC - 1)
            for hf in range(HALVES):
                base = HALVES * PV + hf * (PG + PO)
                for kc in range(KC):
                    dve.wait_ge(q.y_hi, hf * KC + kc + 1)
                    lo_of(y_lo[:, kc % 2, :], y_f32[:, kc, :], y_hi[:, kc % 2, :]).then_inc(q.y_lo, 1)
                    if PG + kc + 1 < PG + PO:
                        unit(base + PG + kc + 1)
                    if hf == 0 and kc < KC // 2:
                        pool_tokens(kc, HTOK, SEQ, d_of[1])
                        dve.sem_inc(q.d_ready, 1)
                    elif hf == 0:
                        d_split(1, 2 * kc - KC)
                        d_split(1, 2 * kc - KC + 1)
                if hf:
                    dve.wait_ge(g.gain_ready, 16 * 4)
                    norm(6, 0, 0)
                else:
                    for r in range(3):
                        unit(base + PG + PO + r)
                for b in range(BANKS):
                    if b < BF:
                        dve.wait_ge(q.full, Q_V + hf * Q_HALF + 6 + b + 1)
                    else:
                        dve.wait_ge(q.used, RING + base + PG + PO)
                    x = x_res[:, hf * HT + b // 2, b % 2 * 512:b % 2 * 512 + 512]
                    nc.vector.tensor_tensor(x, bank[b][:, :], x, ALU.add).then_inc(q.ev_dve, 1)
            dve.wait_ge(q.ev_dve, HALVES * BANKS)

            moe(1)

            dve.wait_ge(g.gain_ready, 16 * 5)
            add_and_norm(1, 8, (0, 1), TT)


_SHAPES = ((1, SEQ, D), "float32")


def kernel(**inputs):
    import numpy as np
    import concourse.bacc as bacc
    from concourse.bass_utils import run_bass_kernel_spmd as run

    def by_partition(a, width):
        return np.ascontiguousarray(a.reshape(width, P).T)

    a = {k: np.ascontiguousarray(inputs[k]) for k in (
        "x", "norm_mix_g", "norm_ffn_g", "final_norm_g", "a_w_in", "a_b_in", "a_w_out", "a_b_spatial",
        "b_w_in", "b_w_group", "b_w_out", "w_gate", "w_up", "w_down")}
    a["w_s"] = np.ascontiguousarray(np.asarray(inputs["a_w_spatial"])[0].transpose(2, 0, 1).reshape(P, HEADS * P))
    a["u_bias"] = by_partition(np.asarray(inputs["a_b_in"])[0, :SGU], SGU // P)
    a["v_gain"] = by_partition(np.asarray(inputs["a_norm_v"])[0], SGU // P)
    a["pool_scale"] = by_partition(np.asarray(inputs["b_scale"])[0], KC)
    rw = np.concatenate([np.asarray(inputs["router_group_w"]), np.asarray(inputs["router_expert_w"])], axis=2)
    rw = np.pad(rw, ((0, 0), (0, 0), (0, P - rw.shape[2])))
    a["router_w"] = np.ascontiguousarray(rw.reshape(LAYERS, KC, P, P).transpose(0, 2, 1, 3).reshape(LAYERS, P, KC * P))
    rb = np.concatenate([np.asarray(inputs["router_group_b"]), np.asarray(inputs["router_expert_b"])], axis=1)
    a["router_b"] = np.ascontiguousarray(np.pad(rb, ((0, 0), (0, P - rb.shape[1])))[:, :, None])

    c = np.zeros((P, C_ALL), np.float32)
    c[:, C_ID:C_ID + P] = np.eye(P)
    c[:, C_TRI:C_TRI + P] = np.triu(np.ones((P, P)), 1)
    c[:, C_E:C_E + E] = np.arange(E)
    c[:, C_GRP:C_GRP + E] = np.arange(E) // EPG
    c[:, C_BASE:C_BASE + E] = np.arange(E) * LISTED
    c[:, C_ASC + 1:C_ASC + 16] = 1.0 / np.arange(1, 16)
    c[:, C_DESC:C_DESC + 16] = 1.0 / (16 - np.arange(16))
    c[:, C_THR:C_THR + BPE - 1] = BLK * np.arange(1, BPE)
    c[:, C_J:C_J + EXTRA] = np.arange(EXTRA)
    c[:, C_E8:C_E8 + E] = BPE * np.arange(E) + 1
    a["c_float"] = c
    tok = np.arange(TT)[None, :] * P + np.arange(P)[:, None]
    pay = np.zeros((P, TT, 2, 4), np.int32)
    pay[..., 0] = tok[..., None]
    pay[..., 1] = 2 * tok[..., None] + np.arange(2)
    a["c_payload"] = pay.reshape(P, TT * 8)
    tab = np.zeros((1, 2, TABLE), np.int32)
    tab[0, 0, :E] = np.arange(E)
    tab[0, 1, :E] = np.arange(E) * BPE
    a["c_table"] = tab

    nc = bacc.Bacc("TRN2", target_bir_lowering=False, num_devices=1)
    arrays, aps = {}, {}
    for name, v in a.items():
        arrays[f"in_{name}"] = v
        aps[name] = nc.dram_tensor(f"in_{name}", v.shape, mybir.dt.from_np(v.dtype), kind="ExternalInput").ap()
    out = nc.dram_tensor("out_0", _SHAPES[0], F32, kind="ExternalOutput").ap()
    encoder_trunk(nc, aps, out)
    r = run(nc, [arrays], core_ids=[0])
    return r.results[0]["out_0"]
```
